# Optimizing a Trainium2 kernel written in Bass

```python
import jax, jax.numpy as jnp
from jax import lax
import numpy as np

D_MODEL = 2048
BATCH = 1
SEQ = 256
DEPTH = 1
DEC_BATCH = 8
DEC_SEQ = 1
PAST_LEN = 2048
PAGE_SIZE = 128

D_MIX = D_MODEL
D_CONF = D_MIX // 2
D_LRU = D_MIX - D_CONF
N_CONF_GROUPS = 8
N_LRU_HEADS = 8
LRU_HEAD_DIM = D_LRU // N_LRU_HEADS
CONF_KERNEL = 31
LRU_CONV = 4
LRU_C = 8.0
N_GROUPS = 4
EXPERTS_PER_GROUP = 8
N_EXPERTS = N_GROUPS * EXPERTS_PER_GROUP
TOP_K = 2
D_EXPERT = D_MODEL // 4
D_PLE = 256
EPS = 1e-6
D_IN = 2 * D_CONF + 2 * D_LRU

kernel_name = "hybrid_conformer_rglru_hmoe_step"

def rmsnorm(x, g):
    xf = x.astype(jnp.float32)
    y = xf * lax.rsqrt(jnp.mean(xf * xf, axis=-1, keepdims=True) + EPS) * g.astype(jnp.float32)
    return y.astype(x.dtype)

def layernorm(x, g, b):
    xf = x.astype(jnp.float32)
    mu = jnp.mean(xf, axis=-1, keepdims=True)
    var = jnp.mean(jnp.square(xf - mu), axis=-1, keepdims=True)
    y = (xf - mu) * lax.rsqrt(var + EPS) * g.astype(jnp.float32) + b.astype(jnp.float32)
    return y.astype(x.dtype)

def causal_dw_conv(u, buf, w, b):
    K, C = w.shape
    full = jnp.concatenate([buf.astype(u.dtype), u], axis=1)
    out = lax.conv_general_dilated(full, w.astype(u.dtype)[:, None, :], window_strides=(1,), padding='VALID',
                                   dimension_numbers=('NWC', 'WIO', 'NWC'), feature_group_count=C)
    return out + b.astype(u.dtype), full[:, full.shape[1] - (K - 1):]

def rg_lru(x, h0, w_a, b_a, w_x, b_x, lam):
    B, T, C = x.shape
    xh = x.reshape(B, T, N_LRU_HEADS, LRU_HEAD_DIM)
    r = jax.nn.sigmoid((jnp.einsum('bthi,hij->bthj', xh, w_a) + b_a).astype(jnp.float32)).reshape(B, T, C)
    i = jax.nn.sigmoid((jnp.einsum('bthi,hij->bthj', xh, w_x) + b_x).astype(jnp.float32)).reshape(B, T, C)
    log_a = -LRU_C * r * jax.nn.softplus(-lam.astype(jnp.float32))
    a = jnp.exp(log_a)
    u = jnp.sqrt(-jnp.expm1(2.0 * log_a)) * i * x.astype(jnp.float32)

    def step(h, inp):
        a_t, u_t = inp
        h = a_t * h + u_t
        return h, h

    h_last, hs = lax.scan(step, h0.astype(jnp.float32), (jnp.swapaxes(a, 0, 1), jnp.swapaxes(u, 0, 1)))
    return jnp.swapaxes(hs, 0, 1).astype(x.dtype), h_last.astype(h0.dtype)

def hier_moe(xn, w_grp, b_grp, w_rt, b_rt, w_gate, w_up, w_down):
    B, T, D = xn.shape
    xt = xn.reshape(-1, D)
    g_logits = (xt @ w_grp + b_grp).astype(jnp.float32)
    g_prob = jax.nn.softmax(g_logits, axis=-1)
    g_idx = jnp.argmax(g_logits, axis=-1)
    g_w = jnp.take_along_axis(g_prob, g_idx[:, None], axis=-1)
    e_logits = (xt @ w_rt + b_rt).astype(jnp.float32).reshape(-1, N_GROUPS, EXPERTS_PER_GROUP)
    e_in = jnp.take_along_axis(e_logits, g_idx[:, None, None], axis=1)[:, 0]
    top_v, top_i = lax.top_k(e_in, TOP_K)
    weights = g_w * jax.nn.softmax(top_v, axis=-1)
    expert_id = g_idx[:, None] * EXPERTS_PER_GROUP + top_i
    combine = jnp.einsum('nk,nke->ne', weights,
                         jax.nn.one_hot(expert_id, N_EXPERTS, dtype=jnp.float32)).astype(xt.dtype)
    out = jnp.zeros_like(xt)
    for grp in range(N_GROUPS):
        sl = slice(grp * EXPERTS_PER_GROUP, (grp + 1) * EXPERTS_PER_GROUP)
        hid = jax.nn.silu(jnp.einsum('nd,edf->nef', xt, w_gate[sl])) * jnp.einsum('nd,edf->nef', xt, w_up[sl])
        out = out + jnp.einsum('nef,efd->nd', hid * combine[:, sl, None], w_down[sl])
    return out.reshape(B, T, D)

def run_trunk(x, p, conf_bufs, lru_bufs, lru_hs,
              norm1_g, w_in, b_in, conf_dw_w, conf_dw_b, conf_ln_g, conf_ln_b,
              lru_conv_w, lru_conv_b, lru_wa, lru_ba, lru_wx, lru_bx, lru_lambda, w_out,
              norm2_g, w_grp, b_grp, w_rt, b_rt, w_gate, w_up, w_down,
              ple_norm_g, w_ple, w_pg, b_pg, final_g):
    h = x
    new_conf, new_lconv, new_h = [], [], []
    for l in range(DEPTH):
        xn = rmsnorm(h, norm1_g[l])
        proj = xn @ w_in[l] + b_in[l]
        c_val, c_gate, l_x, l_gate = jnp.split(proj, [D_CONF, 2 * D_CONF, 2 * D_CONF + D_LRU], axis=-1)
        u = c_val * jax.nn.sigmoid(c_gate)
        c, cb = causal_dw_conv(u, conf_bufs[l], conf_dw_w[l], conf_dw_b[l])
        c = jax.nn.silu(layernorm(c, conf_ln_g[l], conf_ln_b[l]))
        lx, lb = causal_dw_conv(l_x, lru_bufs[l], lru_conv_w[l], lru_conv_b[l])
        hs, hl = rg_lru(lx, lru_hs[l], lru_wa[l], lru_ba[l], lru_wx[l], lru_bx[l], lru_lambda[l])
        r_out = hs * jax.nn.gelu(l_gate)
        h = h + jnp.concatenate([c, r_out], axis=-1) @ w_out[l]
        h = h + hier_moe(rmsnorm(h, norm2_g[l]), w_grp[l], b_grp[l], w_rt[l], b_rt[l],
                         w_gate[l], w_up[l], w_down[l])
        gate = jax.nn.sigmoid(rmsnorm(h, ple_norm_g[l]) @ w_pg[l] + b_pg[l])
        h = h + gate * (p[l] @ w_ple[l])
        new_conf.append(cb); new_lconv.append(lb); new_h.append(hl)
    return rmsnorm(h, final_g), jnp.stack(new_conf), jnp.stack(new_lconv), jnp.stack(new_h)

def setup_inputs(seed: int = 0) -> dict:
    key = jax.random.key(seed)
    ks = iter(jax.random.split(key, 64))
    f32 = jnp.float32

    def nrm(shape, s):
        return jax.random.normal(next(ks), shape, f32) * s

    a0 = jax.random.uniform(next(ks), (DEPTH, D_LRU), f32, minval=0.9, maxval=0.999)
    return {
        "x_prompt": nrm((BATCH, SEQ, D_MODEL), 1.0),
        "x_sample": nrm((DEC_BATCH, DEC_SEQ, D_MODEL), 1.0),
        "state_conf_conv": nrm((DEPTH, DEC_BATCH, CONF_KERNEL - 1, D_CONF), 0.5),
        "state_lru_conv": nrm((DEPTH, DEC_BATCH, LRU_CONV - 1, D_LRU), 1.0),
        "state_lru_h": nrm((DEPTH, DEC_BATCH, D_LRU), 0.5),
        "p_prompt": nrm((DEPTH, BATCH, SEQ, D_PLE), 1.0),
        "p_sample": nrm((DEPTH, DEC_BATCH, DEC_SEQ, D_PLE), 1.0),
        "norm1_g": 1.0 + nrm((DEPTH, D_MODEL), 0.01),
        "w_in": nrm((DEPTH, D_MODEL, D_IN), D_MODEL ** -0.5),
        "b_in": nrm((DEPTH, D_IN), 0.01),
        "conf_dw_w": nrm((DEPTH, CONF_KERNEL, D_CONF), CONF_KERNEL ** -0.5),
        "conf_dw_b": nrm((DEPTH, D_CONF), 0.01),
        "conf_ln_g": 1.0 + nrm((DEPTH, D_CONF), 0.01),
        "conf_ln_b": nrm((DEPTH, D_CONF), 0.01),
        "lru_conv_w": nrm((DEPTH, LRU_CONV, D_LRU), LRU_CONV ** -0.5),
        "lru_conv_b": nrm((DEPTH, D_LRU), 0.01),
        "lru_wa": nrm((DEPTH, N_LRU_HEADS, LRU_HEAD_DIM, LRU_HEAD_DIM), LRU_HEAD_DIM ** -0.5),
        "lru_ba": nrm((DEPTH, N_LRU_HEADS, LRU_HEAD_DIM), 0.01),
        "lru_wx": nrm((DEPTH, N_LRU_HEADS, LRU_HEAD_DIM, LRU_HEAD_DIM), LRU_HEAD_DIM ** -0.5),
        "lru_bx": nrm((DEPTH, N_LRU_HEADS, LRU_HEAD_DIM), 0.01),
        "lru_lambda": jnp.log(a0) - jnp.log1p(-a0),
        "w_out": nrm((DEPTH, D_MIX, D_MODEL), D_MIX ** -0.5),
        "norm2_g": 1.0 + nrm((DEPTH, D_MODEL), 0.01),
        "w_grp": nrm((DEPTH, D_MODEL, N_GROUPS), D_MODEL ** -0.5),
        "b_grp": nrm((DEPTH, N_GROUPS), 0.01),
        "w_rt": nrm((DEPTH, D_MODEL, N_EXPERTS), D_MODEL ** -0.5),
        "b_rt": nrm((DEPTH, N_EXPERTS), 0.01),
        "w_gate": nrm((DEPTH, N_EXPERTS, D_MODEL, D_EXPERT), D_MODEL ** -0.5),
        "w_up": nrm((DEPTH, N_EXPERTS, D_MODEL, D_EXPERT), D_MODEL ** -0.5),
        "w_down": nrm((DEPTH, N_EXPERTS, D_EXPERT, D_MODEL), D_EXPERT ** -0.5),
        "ple_norm_g": 1.0 + nrm((DEPTH, D_MODEL), 0.01),
        "w_ple": nrm((DEPTH, D_PLE, D_MODEL), D_PLE ** -0.5),
        "w_pg": nrm((DEPTH, D_MODEL, D_MODEL), D_MODEL ** -0.5),
        "b_pg": nrm((DEPTH, D_MODEL), 0.01),
        "final_g": 1.0 + nrm((D_MODEL,), 0.01),
    }

def reference(x_prompt, x_sample, state_conf_conv, state_lru_conv, state_lru_h, p_prompt, p_sample,
              norm1_g, w_in, b_in, conf_dw_w, conf_dw_b, conf_ln_g, conf_ln_b,
              lru_conv_w, lru_conv_b, lru_wa, lru_ba, lru_wx, lru_bx, lru_lambda, w_out,
              norm2_g, w_grp, b_grp, w_rt, b_rt, w_gate, w_up, w_down,
              ple_norm_g, w_ple, w_pg, b_pg, final_g):
    weights = (norm1_g, w_in, b_in, conf_dw_w, conf_dw_b, conf_ln_g, conf_ln_b,
               lru_conv_w, lru_conv_b, lru_wa, lru_ba, lru_wx, lru_bx, lru_lambda, w_out,
               norm2_g, w_grp, b_grp, w_rt, b_rt, w_gate, w_up, w_down,
               ple_norm_g, w_ple, w_pg, b_pg, final_g)
    B = x_prompt.shape[0]
    zc = jnp.zeros((DEPTH, B, CONF_KERNEL - 1, D_CONF), x_prompt.dtype)
    zl = jnp.zeros((DEPTH, B, LRU_CONV - 1, D_LRU), x_prompt.dtype)
    zh = jnp.zeros((DEPTH, B, D_LRU), state_lru_h.dtype)
    y_prompt, conf_conv_prompt, lru_conv_prompt, lru_h_prompt = run_trunk(
        x_prompt, p_prompt, zc, zl, zh, *weights)
    y_sample, conf_conv_sample, lru_conv_sample, lru_h_sample = run_trunk(
        x_sample, p_sample, state_conf_conv, state_lru_conv, state_lru_h, *weights)
    return (y_prompt, y_sample, conf_conv_prompt, conf_conv_sample,
            lru_conv_prompt, lru_conv_sample, lru_h_prompt, lru_h_sample)


_drawn_inputs = setup_inputs


def setup_inputs(seed=0):
    import zlib

    import numpy as np

    out = dict(_drawn_inputs(seed))
    spreads = {}
    factors = {'norm1_g': 3.547,
     'conf_dw_b': 2.793,
     'conf_ln_g': 3.642,
     'conf_ln_b': 5.131,
     'lru_ba': 7.693,
     'lru_bx': 6.496,
     'norm2_g': 2.812,
     'b_grp': 4.014,
     'b_rt': 3.723,
     'ple_norm_g': 8.0,
     'b_pg': 8.0,
     'final_g': 5.739}
    for name, (base, spread) in spreads.items():
        noise = np.random.default_rng([zlib.crc32(name.encode()), seed]).standard_normal(out[name].shape)
        drawn = base * np.exp(spread * noise) if base else spread * noise
        out[name] = __import__('jax').numpy.asarray(drawn.astype(out[name].dtype))
    for name, factor in factors.items():
        out[name] = (out[name] * factor).astype(out[name].dtype)
    return out
```

```python
import numpy as np

import concourse.bass as bass
from concourse import mybir
from concourse.alu_op_type import AluOpType as ALU

ACT = mybir.ActivationFunctionType
F32 = mybir.dt.float32
I32 = mybir.dt.int32
U32 = mybir.dt.uint32
AX = mybir.AxisListType.X

D = 2048
SEQ = 256
NB = 8
TOK = SEQ + NB
DC = 1024
CK = 31
LK = 4
E = 32
NG = 4
EG = E // NG
F = D // 4
DP = 256
EPS = 1e-6
P = 128
KD = D // P
TC = DC // P
ROWS = [P, P, NB]

NS = 12
CH_IN = 32
CH_OUT = 16
CH_PLE = 2
CH_FRONT = CH_IN + CH_OUT + CH_PLE
CH_EXP = 12
CH_PG0 = CH_FRONT + E * CH_EXP

WIN = 64
NSLOT = 2 * TOK
XW = NSLOT + WIN
HALF = NSLOT // 2
FILL = -(-(XW + WIN) // (2 * P)) * 2 * P
MAX_OVER = NSLOT // WIN

V_CW = 0
V_N1, V_PN, V_BIN, V_BPG, V_DWB, V_LNG, V_LNB = 248, 264, 280, 312, 328, 336, 344
V_LW, V_LB, V_BA, V_BX, V_LAM, V_H0 = 352, 384, 392, 400, 408, 416
NV = 480

GROUP_COL = [0, 256, 512, 768, 2048, 2560, 3072, 3584]
UW = CK - 1 + TOK
LW = LK - 1 + TOK
CT_IN, CT_OUT, CT_PLE, CT_PG = 0, 32, 48, 64


def build(nc, a, o):
    top = [((nc.sbuf_base + 31) // 32) * 32]

    def region(size):
        at = top[0]
        top[0] += size
        assert top[0] <= nc.sbuf_usable_end, (top[0], nc.sbuf_usable_end)
        return at

    def place(name, shape, dt, at):
        return nc.alloc_sbuf_tensor_at(name, shape, dt, offset=at)

    def sem(name):
        return nc.alloc_semaphore(name)

    r_ring = region(NS * 8192)
    r_h = region(3 * 8192)
    r_big = region(KD * XW * 4)
    r_xs = region(3 * 8192)
    r_xt = region(KD * TOK * 4)
    r_const = region(10616 // 32 * 32)

    ring = place("ring", [P, NS, D], F32, r_ring)
    h = place("h", [P, 3, D], F32, r_h)

    U = place("U", [P, TC, UW], F32, r_big)
    at = r_big + TC * UW * 4
    mix = place("mix", [P, KD, TOK], F32, at)
    stage = place("stage", [P, 2, DC], F32, at)
    lstage = place("lstage", [P, DC], F32, at + 8192)
    vrow = place("vrow", [P, 4, P], F32, at + 12288)
    ptmp = place("ptmp", [P, 240], F32, at + 14336)
    at += KD * TOK * 4
    L = place("L", [P, TC, LW], F32, at)
    at += TC * LW * 4
    wr = place("wr", [P, KD, NG + E], F32, at)
    at += KD * (NG + E) * 4
    br = place("br", [P, NG + E], F32, at)
    at += 160
    htail = place("htail", [P, TC, NB + 1], F32, at)
    at += 288
    assert at <= r_big + KD * XW * 4
    xsort = place("xsort", [P, KD, XW], F32, r_big)
    g0 = place("g0", [P, 3, D], F32, r_big)
    fing = place("fing", [P, D], F32, r_big + 3 * 8192)

    xs = place("xs", [P, 3, D], F32, r_xs)
    xs2 = place("xs2", [P, 3, KD, P], F32, r_xs)
    lxc = place("lxc", [P, TC, TOK], F32, r_xs)
    wa = place("wa", [P, TC, P], F32, r_xs + 8448)
    wx = place("wx", [P, TC, P], F32, r_xs + 8448 + 4096)
    R = place("R", [P, 4, TOK], F32, r_xs + 16640)
    I = place("I", [P, 2, TOK], F32, r_xs + 20864)
    sc_out = place("sc_out", [P, DC], F32, r_xs)
    sl_out = place("sl_out", [P, DC], F32, r_xs + 4096)
    sh_out = place("sh_out", [P, DC], F32, r_xs + 8192)
    pleT = place("pleT", [P, KD, TOK], F32, r_xs)

    xT = place("xT", [P, KD, TOK], F32, r_xt)
    hT = place("hT", [P, 2, TOK], F32, r_xt)
    onehot = place("onehot", [P, 3, NSLOT], F32, r_xt)
    iota = place("iota", [P, NSLOT], F32, r_xt + 6336)
    prow = place("prow", [P, 3, DP], F32, r_xt + 8448)
    pT = place("pT", [P, 2, TOK], F32, r_xt + 11520)
    xwin = place("xwin", [P, KD, WIN], F32, r_xt)
    ysb = place("ysb", [P, 2, D // 2], F32, r_xt + 4096)
    hid = place("hid", [P, 4, WIN], F32, r_xt + 12288)
    sgl = place("sgl", [P, F], F32, r_xt + 13312)

    at = r_const
    ident = place("ident", [P, P], F32, at)
    ones = place("ones", [P, P], F32, at + 512)
    vT = place("vT", [P, NV], F32, at + 1024)
    T = place("T", [P, 4, TOK], F32, at + 2944)
    pconv = place("pconv", [P, TC, NB], F32, at + 2944)
    zeros = place("zeros", [P, 512], F32, at + 3200)
    sq = place("sq", [P, 2, TOK], F32, at + 7168)
    plru = place("plru", [P, TC, NB], F32, at + 7168)
    sg = place("sg", [P, TOK], F32, at + 9280)
    g2 = place("g2", [P, KD], F32, at + 10336)
    negc = place("negc", [P, TC], F32, at + 10400)
    ssum = place("ssum", [P, 4], F32, at + 10432)
    rstd = place("rstd", [P, 4], F32, at + 10464)
    spt = place("spt", [P, 3, TC], F32, at + 10496)
    sgb = place("sgb", [P, TOK], F32, r_xs + 22976)
    gate_buf = [sg, sgb]

    ra = at + 2944
    rsz = [0]

    def rt(name, shape, dt=F32):
        n = 4
        for s in shape[1:]:
            n *= s
        x = place(name, shape, dt, ra + rsz[0])
        rsz[0] += (n + 31) // 32 * 32
        assert rsz[0] <= 7392
        return x

    offs = rt("offs", [1, 64], I32)
    wts = rt("wts", [P, 2, 3])
    rowix = rt("rowix", [P, 2, 3], I32)
    logit = rt("logit", [P, 3, NG + E])
    gl = rt("gl", [P, 3, 8])
    gmx = rt("gmx", [P, 3, 8])
    gix = rt("gix", [P, 3, 8], U32)
    gf = rt("gf", [P, 3])
    gex = rt("gex", [P, 3, NG])
    gw = rt("gw", [P, 3])
    oh4 = rt("oh4", [P, 3, NG])
    el = rt("el", [P, 3, NG, EG])
    ein = rt("ein", [P, 3, EG])
    emx = rt("emx", [P, 3, 8])
    eix = rt("eix", [P, 3, 8], U32)
    ef = rt("ef", [P, 3, 2])
    ex = rt("ex", [P, 3])
    oh = rt("oh", [P, 2, 3, E])
    asg = rt("asg", [P, 3, E])
    rank = rt("rank", [P, 3, E])
    cnt = rt("cnt", [P, E])
    off = rt("off", [P, E])
    pos = rt("pos", [P, 2, 3])
    rnk = rt("rnk", [P, 2, 3])
    tri = rt("tri", [P, P])
    i32r = rt("i32r", [P, E])
    prod = rt("prod", [P, 3, E])
    over = rt("over", [P, E, 4])
    oidx = rt("oidx", [P, E, 4])
    osel = rt("osel", [P, E, 4])
    opr = rt("opr", [P, E, 4])
    win64 = rt("win64", [P, 4])
    pidx = rt("pidx", [P, 1])
    otab = rt("otab", [P, 2])
    otabi = rt("otabi", [P, 2], I32)

    ps = nc.alloc_psum_tensor("ps", [P, 8, 512], F32)

    y_dram = nc.dram_tensor("y_sorted", (2 * XW, D), F32, kind="Internal").ap()
    ov_dram = nc.dram_tensor("over_table", (MAX_OVER, 2), I32, kind="Internal").ap()

    slot_loaded = [sem(f"slot_loaded{i}") for i in range(NS)]
    chunk_used = sem("chunk_used")
    x_loaded = sem("x_loaded")
    rows_loaded = sem("rows_loaded")
    gates_loaded = sem("gates_loaded")
    router_loaded = sem("router_loaded")
    p_loaded = sem("p_loaded")
    fing_loaded = sem("fing_loaded")
    consts_ready = sem("consts_ready")
    iotas_ready = sem("iotas_ready")
    act_order = sem("act_order")
    dve_order = sem("dve_order")
    zeros_ready = sem("zeros_ready")
    ms_ready = sem("ms_ready")
    root_ready = sem("root_ready")
    xs_ready = sem("xs_ready")
    vec_turned = sem("vec_turned")
    vec_ready = sem("vec_ready")
    x_turned = sem("x_turned")
    xT_dve = sem("xT_dve")
    xT_act = sem("xT_act")
    state_turned = sem("state_turned")
    state_used = sem("state_used")
    acc_full = sem("acc_full")
    acc_free = sem("acc_free")
    sig_ready = sem("sig_ready")
    u_ready = sem("u_ready")
    conv_done = sem("conv_done")
    lconv_done = sem("lconv_done")
    gates_full = sem("gates_full")
    gates_taken = sem("gates_taken")
    i_ready = sem("i_ready")
    i_used = sem("i_used")
    tanh_ready = sem("tanh_ready")
    z_ready = sem("z_ready")
    beta_ready = sem("beta_ready")
    scan_done = sem("scan_done")
    gelu_ready = sem("gelu_ready")
    mixr_ready = sem("mixr_ready")
    mean_full = sem("mean_full")
    centred = sem("centred")
    sq_ready = sem("sq_ready")
    sq_used = sem("sq_used")
    var_full = sem("var_full")
    var_ready = sem("var_ready")
    sd_ready = sem("sd_ready")
    scaled = sem("scaled")
    mixc_ready = sem("mixc_ready")
    hT_ready = sem("hT_ready")
    h_turned = sem("h_turned")
    h_added = sem("h_added")
    tail_turned = sem("tail_turned")
    tail_taken = sem("tail_taken")
    state_out = sem("state_out")
    ssq_act = sem("ssq_act")
    logits_full = sem("logits_full")
    softmax_in = sem("softmax_in")
    softmax_out = sem("softmax_out")
    assigned = sem("assigned")
    ranks_full = sem("ranks_full")
    table_ready = sem("table_ready")
    table_out = sem("table_out")
    onehot_ready = sem("onehot_ready")
    sort_full = sem("sort_full")
    sort_dve = sem("sort_dve")
    sort_act = sem("sort_act")
    pad_ready = sem("pad_ready")
    p_turned = sem("p_turned")
    pT_ready = sem("pT_ready")
    y_out = sem("y_out")
    expert_steps = ("window", "products", "silu", "gated", "turned", "hid", "down", "evac")
    main = {n: sem(f"main_{n}") for n in expert_steps}
    extra = {n: sem(f"extra_{n}") for n in expert_steps}
    over_loaded = sem("over_loaded")
    over_out = sem("over_out")
    over_free = sem("over_free")
    rows_back = sem("rows_back")
    rows_back2 = sem("rows_back2")
    h2_first = sem("h2_first")
    pg_ready = sem("pg_ready")
    prod_ready = sem("prod_ready")
    y_ready = sem("y_ready")
    out_done = sem("out_done")

    block = nc.Block()
    block.__enter__()

    def chunk_view(n):
        if n < CH_IN:
            c0 = GROUP_COL[n // 4]
            if n < CH_IN // 2:
                v = a["w_in"].rearrange("l (k p) (h c) -> h p (l k) c", p=P, h=4)
                return v[:, :, 4 * (n % 4):4 * (n % 4) + 4, c0:c0 + 256], 256
            v = a["w_in"].rearrange("l (k p) c -> p (l k) c", p=P)
            return v[:, 4 * (n % 4):4 * (n % 4) + 4, c0:c0 + 512], 512
        if n < CH_IN + CH_OUT:
            m = n - CH_IN
            v = a["w_out"].rearrange("l (k p) c -> p (l k) c", p=P)
            return v[:, 4 * (m % 4):4 * (m % 4) + 4, 512 * (m // 4):512 * (m // 4) + 512], 512
        if n < CH_FRONT:
            v = a["w_ple"].rearrange("l (k p) c -> p (l k) c", p=P)
            return v[:, n - CH_FRONT + 2:n - CH_FRONT + 3, :], D
        m = n - CH_PG0
        v = a["w_pg"].rearrange("l (k p) c -> p (l k) c", p=P)
        return v[:, 4 * (m % 4):4 * (m % 4) + 4, 512 * (m // 4):512 * (m // 4) + 512], 512

    def freed(n):
        return n + 1 if n < CT_OUT else n + 1 - KD

    def used(n):
        if n < CH_IN + CH_OUT:
            if n % 4 == 3:
                return acc_full, n + 1
            return chunk_used, 3 * (n // 4) + n % 4 + 1
        if n < CH_FRONT:
            return acc_full, CT_PG
        m = n - CH_PG0
        if m % 4 == 3:
            return acc_full, CT_PG + m + 1
        return chunk_used, 3 * (CH_IN + CH_OUT) // 4 + 6 * E + 3 * (m // 4) + m % 4 + 1

    def used_expert(e, j):
        if j in (6, 7):
            return main["products"], e + 1
        if j == CH_EXP - 1:
            return main["down"], e + 1
        part = j // 2 if j < 8 else j - 5
        return chunk_used, e * 6 + (3 * (CH_IN + CH_OUT) // 4 + part + 1)

    def gate_tail(m):
        return sq[:, m % 2, :]

    def slot(n):
        return n % NS

    def slot_count(n):
        return 16 * sum(2 if m < CH_IN // 2 else 1 for m in range(slot(n), n + 1, NS))

    gate_v = a["w_gate"].rearrange("l e (p k) f -> p (l e) (k f)", k=KD)
    up_v = a["w_up"].rearrange("l e (p k) f -> p (l e) (k f)", k=KD)

    def down_view(e, t):
        return a["w_down"].rearrange("l e (t p) d -> t p (l e) d", p=P)[t, :, bass.ds(e, 1), :]

    def expert_view(e, j):
        if j < 8:
            return (gate_v, up_v)[j % 2][:, bass.ds(e, 1), j // 2 * D:(j // 2 + 1) * D]
        return down_view(e, j - 8)

    @block.sync
    def _(sp):
        def load(n):
            src, w = chunk_view(n)
            if n >= CH_PG0 and n - NS < CH_PG0:
                sp.wait_ge(*used_expert(E - 1, n - CH_PG0))
            elif n >= NS:
                sp.wait_ge(*used(n - NS))
            if w == 256:
                dst = ring[:, slot(n), :].rearrange("p (k h c) -> p k h c", c=w, h=2)
                for half in range(2):
                    sp.dma_start(dst[:, :, half, :], src[half]).then_inc(slot_loaded[slot(n)], 16)
            else:
                dst = ring[:, slot(n), :].rearrange("p (k c) -> p k c", c=w)
                sp.dma_start(dst, src).then_inc(slot_loaded[slot(n)], 16)

        sp.dma_start(h[:, 0:2, :], a["x_prompt"][0].rearrange("(c p) d -> p c d", p=P)).then_inc(x_loaded, 16)
        sp.dma_start(h[0:NB, 2, :], a["x_sample"][:, 0, :]).then_inc(x_loaded, 16)
        for n in range(CH_FRONT):
            load(n)
        for j in range(CH_EXP):
            s = slot(CH_FRONT + j)
            sp.wait_ge(*used(CH_FRONT + j - NS))
            sp.dma_start(ring[:, s:s + 1, :], expert_view(0, j)).then_inc(slot_loaded[s], 16)
        with sp.Fori(1, E) as e:
            for j in range(CH_EXP):
                sp.wait_ge(*used_expert(e - 1, j))
                s = slot(CH_FRONT + j)
                sp.dma_start(ring[:, s:s + 1, :], expert_view(e, j)).then_inc(slot_loaded[s], 16)
        sp.wait_ge(table_out, 16)
        n_over = sp.value_load(offs[0:1, 40:41], min_val=0, max_val=MAX_OVER)
        with sp.If(n_over > 0):
            sp.wait_ge(main["down"], E)
            with sp.Fori(0, n_over) as i:
                e = sp.value_load(ov_dram[bass.ds(i, 1), 0:1], min_val=0, max_val=E - 1)
                sp.wait_ge(over_free, i + 1)
                for j in range(CH_EXP):
                    sp.dma_start(ring[:, j:j + 1, :], expert_view(e, j)).then_inc(over_loaded, 16)
        for n in range(CH_PG0, CH_PG0 + CH_OUT):
            load(n)

    @block.gpsimd
    def _(pool):
        pool.memset(ident[:, :], 0.0).then_inc(consts_ready, 1)
        pool.memset(ones[:, :], 1.0).then_inc(consts_ready, 1)
        pool.memset(U[:, :, 0:CK - 1], 0.0).then_inc(consts_ready, 1)
        pool.memset(L[:, :, 0:LK - 1], 0.0).then_inc(consts_ready, 1)
        pool.memset(zeros[:, :], 0.0).then_inc(zeros_ready, 1)
        pool.wait_ge(consts_ready, 4)
        pool.affine_select(out=ident[:, :], in_=ident[:, :], compare_op=ALU.not_equal, fill=1.0,
                           base=0, pattern=[[-1, P]], channel_multiplier=1).then_inc(consts_ready, 1)
        pool.dma_start(o["conf_sample"][0, :, 0:CK - 2, :], a["state_conf_conv"][0, :, 1:CK - 1, :])\
            .then_inc(state_out, 16)
        pool.dma_start(o["lru_sample"][0, :, 0:LK - 2, :], a["state_lru_conv"][0, :, 1:LK - 1, :])\
            .then_inc(state_out, 16)
        pool.wait_ge(zeros_ready, 1)
        for x in range(2):
            pool.dma_start(y_dram[2 * XW - FILL + x * FILL // 2:2 * XW - FILL + (x + 1) * FILL // 2, :]
                          .rearrange("(p r) (a b) -> p (r a) b", p=P, b=512),
                          zeros[:, :].unsqueeze(1).broadcast_to([P, FILL // P * 2, 512])).then_inc(y_out, 16)

        pool.wait_ge(tail_taken, 1)
        pool.dma_start(o["conf_prompt"][0, 0, :, :], sc_out[0:CK - 1, :]).then_inc(state_out, 16)
        pool.dma_start(o["conf_sample"][0, :, CK - 2, :], sc_out[CK - 1:CK - 1 + NB, :]).then_inc(state_out, 16)
        pool.wait_ge(tail_taken, 2)
        pool.dma_start(o["lru_prompt"][0, 0, :, :], sl_out[0:LK - 1, :]).then_inc(state_out, 16)
        pool.dma_start(o["lru_sample"][0, :, LK - 2, :], sl_out[LK - 1:LK - 1 + NB, :]).then_inc(state_out, 16)
        pool.wait_ge(tail_taken, 3)
        pool.dma_start(o["h_prompt"][0, :, :], sh_out[0:1, :]).then_inc(state_out, 16)
        pool.dma_start(o["h_sample"][0, :, :], sh_out[1:1 + NB, :]).then_inc(state_out, 16)
        pool.memset(tri[:, :], 1.0).then_inc(iotas_ready, 1)
        pool.wait_ge(iotas_ready, 1)
        pool.affine_select(out=tri[:, :], in_=tri[:, :], compare_op=ALU.is_gt, fill=0.0, base=0,
                           pattern=[[1, P]], channel_multiplier=-1).then_inc(iotas_ready, 1)
        pool.iota(i32r[:, :], [[1, E]], base=0, channel_multiplier=0,
                  allow_small_or_imprecise_dtypes=True).then_inc(iotas_ready, 1)
        pool.iota(win64[:, :], [[WIN, 4]], base=WIN, channel_multiplier=0,
                  allow_small_or_imprecise_dtypes=True).then_inc(iotas_ready, 1)
        pool.iota(pidx[:, :], [[0, 1]], base=0, channel_multiplier=1,
                  allow_small_or_imprecise_dtypes=True).then_inc(iotas_ready, 1)
        pool.wait_ge(logits_full, 1)
        pool.iota(iota[:, :], [[1, NSLOT]], base=0, channel_multiplier=0,
                  allow_small_or_imprecise_dtypes=True).then_inc(iotas_ready, 1)
        pool.dma_start(prow[:, 0:2, :], a["p_prompt"][0, 0].rearrange("(c p) d -> p c d", p=P)).then_inc(p_loaded, 16)
        pool.dma_start(prow[0:NB, 2, :], a["p_sample"][0, :, 0, :]).then_inc(p_loaded, 16)
        pool.wait_ge(table_ready, 1)
        pool.dma_start(ov_dram[:, :], otabi[0:MAX_OVER, :]).then_inc(table_out, 16)

        def rows_of(row):
            return y_dram[bass.ds(row, WIN), :].rearrange("r (h c) -> h r c", h=2)

        with pool.Fori(0, E, 2) as e2:
            for par in range(2):
                start = pool.value_load(offs[0:1, bass.ds(e2 + par, 1)], min_val=0, max_val=NSLOT)
                pool.wait_ge(main["evac"], 2 * (e2 + par) + 2)
                pool.wait_ge(y_out, 16 * (e2 + par + 2))
                pool.dma_start(rows_of(start), ysb[:, par, :]).then_inc(y_out, 16)
        pool.wait_ge(table_out, 16)
        n_over = pool.value_load(offs[0:1, 40:41], min_val=0, max_val=MAX_OVER)
        pool.wait_ge(y_out, 16 * (E + 2))
        with pool.If(n_over > 0):
            pool.sem_inc(over_free, 1)
            with pool.Fori(0, n_over) as i:
                start = pool.value_load(ov_dram[bass.ds(i, 1), 1:2], min_val=0, max_val=NSLOT)
                pool.wait_ge(extra["evac"], 2 * i + 2)
                pool.dma_start(rows_of(start + XW), ysb[:, 0, :]).then_inc(over_out, 16)
                pool.wait_ge(over_out, 16 * (i + 1))
                pool.sem_inc(over_free, 1)
        pool.wait_ge(main["window"], E + 1)
        for c in range(3):
            r = ROWS[c]
            pool.indirect_dma_start(g0[0:r, c, :], None, y_dram[:, :],
                                    bass.IndirectOffsetOnAxis(ap=rowix[0:r, 0, c:c + 1], axis=0))\
                .then_inc(rows_back, 16)
        pool.wait_ge(h2_first, 3)
        for c in range(3):
            r = ROWS[c]
            pool.indirect_dma_start(g0[0:r, c, :], None, y_dram[:, :],
                                    bass.IndirectOffsetOnAxis(ap=rowix[0:r, 1, c:c + 1], axis=0))\
                .then_inc(rows_back2, 16)
        pool.wait_ge(state_out, 16 * 8)

    @block.tensor
    def _(pe):
        def turn(out, src, r):
            if r == P:
                return pe.transpose(out, src, ident[:, :])
            return pe.matmul(out, src, ident[:, :], start=True, stop=True)

        def dense(n, chunk0, rhs, kt, wait_k=None):
            if CT_OUT <= n - 3 < CT_PLE:
                pe.wait_ge(hT_ready, n - 3 - CT_OUT + 1)
            elif n >= 3:
                pe.wait_ge(acc_free, freed(n - 3))
            for k in range(kt):
                if kt == KD:
                    ch, kk = chunk0 + k // 4, k % 4
                    w = ring[:, slot(ch), kk * 512 + (n % 4) * P:kk * 512 + (n % 4) * P + P]
                    first, done = n % 4 == 0 and kk == 0, n % 4 == 3 and kk == 3
                else:
                    ch = chunk0 + k
                    w = ring[:, slot(ch), (n - CT_PLE) * P:(n - CT_PLE + 1) * P]
                    first, done = n == CT_PLE, False
                if first:
                    pe.wait_ge(slot_loaded[slot(ch)], slot_count(ch))
                if wait_k:
                    wait_k(k)
                mm = pe.matmul(ps[:, n % 3, 0:TOK], w, rhs[:, k, :], start=(k == 0), stop=(k == kt - 1))
                if done and k < kt - 1:
                    mm.then_inc(chunk_used, 1)
            mm.then_inc(acc_full, 1)

        pe.wait_ge(consts_ready, 5)
        pe.wait_ge(rows_loaded, 16 * N_ROWS)
        widths = [P, 120, 104, P]
        c0 = 0
        for b in range(4):
            w = widths[b]
            last = pe.transpose(ps[:, 7, c0:c0 + w], vrow[0:w, b, :], ident[0:w, 0:w])
            c0 += w
        last.then_inc(vec_turned, 1)
        for j in range(TC):
            if j >= 2:
                pe.wait_ge(state_used, j - 1)
            pe.transpose(ps[:, 5 + j % 2, 0:120], stage[0:120, 0, j * P:(j + 1) * P], ident[0:120, 0:120])
            pe.transpose(ps[:, 5 + j % 2, 120:240], stage[0:120, 1, j * P:(j + 1) * P], ident[0:120, 0:120])\
                .then_inc(state_turned, 1)
        pe.wait_ge(vec_ready, 1)
        for j in range(TC):
            last = pe.transpose(ps[:, 7, j * 24:(j + 1) * 24], lstage[0:24, j * P:(j + 1) * P], ident[0:24, 0:24])
        last.then_inc(state_turned, 1)

        def turn_x(base, src, ready):
            pe.wait_ge(xs_ready, ready)
            for k in range(KD):
                if k >= 2:
                    if k % 2 == 0:
                        pe.wait_ge(xT_dve, base + k // 2)
                    else:
                        pe.wait_ge(xT_act, base + k // 2)
                for c in range(3):
                    r = ROWS[c]
                    last = pe.transpose(ps[:, 3 + k % 2, c * P:c * P + r], src(c, k), ident[0:r, 0:r])
                last.then_inc(x_turned, 1)

        turn_x(0, lambda c, k: xs[0:ROWS[c], c, k * P:(k + 1) * P], 3)

        def lru_gates(j):
            if j == 0:
                pe.wait_ge(gates_loaded, 32)
            pe.wait_ge(lconv_done, j + 1)
            if j >= 1:
                pe.wait_ge(gates_taken, j)
            pe.matmul(ps[:, 3, 0:TOK], wa[:, j, :], lxc[:, j, :], start=True, stop=True)
            pe.matmul(ps[:, 4, 0:TOK], wx[:, j, :], lxc[:, j, :], start=True, stop=True).then_inc(gates_full, 1)

        def mean():
            pe.wait_ge(conv_done, TC)
            for j in range(TC):
                mm = pe.matmul(ps[:, 6, 0:TOK], ones[:, :], mix[:, j, :], start=(j == 0), stop=(j == TC - 1))
            mm.then_inc(mean_full, 1)

        def var(p):
            pe.wait_ge(sq_ready, 2 * p + 2)
            for j in range(2 * p, 2 * p + 2):
                mm = pe.matmul(ps[:, 7, 0:TOK], ones[:, :], sq[:, j % 2, :], start=(j == 0), stop=(j == TC - 1))
            mm.then_inc(sq_used, 1)

        def wait_xT(k):
            if k % 2 == 0:
                pe.wait_ge(xT_dve, k // 2 + 1)
            else:
                pe.wait_ge(xT_act, k // 2 + 1)

        for n in range(CT_OUT):
            dense(n, 4 * (n // 4), xT, KD, wait_xT if n == 0 else None)
            if 20 <= n < 28:
                lru_gates(n - 20)
            if n == 23:
                mean()
            if 26 <= n < 30:
                var(n - 26)

        def wait_mix(k):
            if k < TC:
                pe.wait_ge(mixc_ready, k + 1)
            else:
                pe.wait_ge(mixr_ready, k - TC + 1)

        def turn_back(m, base_free):
            pe.wait_ge(hT_ready, m + 1)
            if m >= 2:
                pe.wait_ge(h_added, m - 1)
            for c in range(3):
                r = ROWS[c]
                last = turn(ps[0:r, 3 + m % 2, c * P:(c + 1) * P], hT_tile(m)[:, c * P:c * P + r], r)
            last.then_inc(h_turned, 1)

        def hT_tile(m):
            return hT[:, m % 2, :]

        def turn_tails(which):
            if which:
                pe.wait_ge(tail_taken, which)
            for j in range(TC):
                src, r = [(U[:, j, SEQ:UW], CK - 1 + NB), (L[:, j, SEQ:LW], LK - 1 + NB), (htail[:, j, :], 1 + NB)][which]
                last = turn(ps[0:r, 5 + j // 4, (j % 4) * P:(j % 4 + 1) * P], src, r)
            last.then_inc(tail_turned, 1)

        for n in range(CT_OUT, CT_PLE):
            dense(n, CH_IN + 4 * ((n - CT_OUT) // 4), mix, KD, wait_mix if n == CT_OUT else None)
            if n > CT_OUT:
                turn_back(n - CT_OUT - 1, 0)
            if n - CT_OUT in (2, 4, 6):
                turn_tails((n - CT_OUT) // 2 - 1)
        turn_back(KD - 1, 0)

        turn_x(8, lambda c, k: xs2[0:ROWS[c], c, k, :], 6)
        pe.wait_ge(router_loaded, 16 * 4)
        for c in range(3):
            r = ROWS[c]
            for k in range(KD):
                if c == 0:
                    if k % 2 == 0:
                        pe.wait_ge(xT_dve, 8 + k // 2 + 1)
                    else:
                        pe.wait_ge(xT_act, 8 + k // 2 + 1)
                mm = pe.matmul(ps[0:r, 5, c * 64:c * 64 + NG + E], xT[:, k, c * P:c * P + r], wr[:, k, :],
                               start=(k == 0), stop=(k == KD - 1))
        mm.then_inc(logits_full, 1)
        pe.wait_ge(assigned, 1)
        pe.wait_ge(iotas_ready, 5)
        for c in range(3):
            r = ROWS[c]
            for cc in range(c + 1):
                rr = ROWS[cc]
                pe.matmul(ps[0:r, 6, c * 64:c * 64 + E], ones[0:rr, 0:r] if cc < c else tri[0:r, 0:r],
                          asg[0:rr, cc, :], start=(cc == 0), stop=(cc == c))
        for c in range(3):
            mm = pe.matmul(ps[:, 6, 192:192 + E], ones[0:ROWS[c], :], asg[0:ROWS[c], c, :],
                           start=(c == 0), stop=(c == 2))
        mm.then_inc(ranks_full, 1)
        pe.wait_ge(p_loaded, 32)
        for k in range(2):
            for c in range(3):
                r = ROWS[c]
                last = pe.transpose(ps[:, 7 - 4 * k, c * P:c * P + r], prow[0:r, c, k * P:(k + 1) * P], ident[0:r, 0:r])
        last.then_inc(p_turned, 1)
        pe.wait_ge(onehot_ready, 3)
        m = 0
        for half in range(2):
            for k in range(KD):
                if m >= 2:
                    pe.wait_ge(sort_dve if m % 2 == 0 else sort_act, m // 2)
                for c in range(3):
                    r = ROWS[c]
                    mm = pe.matmul(ps[:, 4 + m % 2, 0:HALF], xs2[0:r, c, k, :],
                                   onehot[0:r, c, half * HALF:(half + 1) * HALF], start=(c == 0), stop=(c == 2))
                mm.then_inc(sort_full, 1)
                m += 1
        pe.wait_ge(pT_ready, 2)
        for n in range(CT_PLE, CT_PG):
            dense(n, CH_IN + CH_OUT, pT, 2)
        pe.wait_ge(acc_free, freed(CT_PG - 1))

        def expert(i, sems, slots, loaded, release_chunks):
            pe.wait_ge(sems["window"], i + 1)
            for j in range(4):
                loaded(2 * j)
                loaded(2 * j + 1)
                for kk in range(4):
                    k = 4 * j + kk
                    for part in range(2):
                        mm = pe.matmul(ps[part * WIN:(part + 1) * WIN, 0, :], xwin[:, k, :],
                                       ring[:, slots[2 * j + part], kk * F:(kk + 1) * F],
                                       start=(k == 0), stop=(k == KD - 1))
                if j < 3 and release_chunks:
                    mm.then_inc(chunk_used, 1)
            mm.then_inc(sems["products"], 1)
            pe.wait_ge(sems["gated"], i + 1)
            for t in range(4):
                mm = pe.matmul(ps[:, 1, t * WIN:(t + 1) * WIN], sgl[WIN:2 * WIN, t * P:(t + 1) * P],
                               ident[WIN:2 * WIN, WIN:2 * WIN], start=True, stop=True)
            mm.then_inc(sems["turned"], 1)
            pe.wait_ge(sems["hid"], i + 1)
            for t in range(4):
                loaded(8 + t)
                for b in range(2):
                    for half in range(2):
                        q = 2 * half + b
                        mm = pe.matmul(ps[half * WIN:(half + 1) * WIN, 2 + b, :], hid[:, t, :],
                                       ring[:, slots[8 + t], q * 512:(q + 1) * 512], start=(t == 0), stop=(t == 3))
                if t < 3 and release_chunks:
                    mm.then_inc(chunk_used, 1)
            mm.then_inc(sems["down"], 1)

        main_slots = [slot(CH_FRONT + j) for j in range(CH_EXP)]
        with pe.Fori(0, E) as e:
            def main_loaded(j):
                pe.wait_ge(slot_loaded[main_slots[j]], e * 16 + slot_count(CH_FRONT + j))

            expert(e, main, main_slots, main_loaded, True)
        pe.wait_ge(table_out, 16)
        n_over = pe.value_load(offs[0:1, 40:41], min_val=0, max_val=MAX_OVER)
        with pe.If(n_over > 0):
            with pe.Fori(0, n_over) as i:
                def over_wait(j):
                    if j == 0:
                        pe.wait_ge(over_loaded, 16 * CH_EXP * (i + 1))

                expert(i, extra, list(range(CH_EXP)), over_wait, False)

        turn_x(16, lambda c, k: g0[0:ROWS[c], c, k * P:(k + 1) * P], 9)

        def wait_xT3(k):
            if k % 2 == 0:
                pe.wait_ge(xT_dve, 16 + k // 2 + 1)
            else:
                pe.wait_ge(xT_act, 16 + k // 2 + 1)

        def turn_prod(m):
            pe.wait_ge(prod_ready, m + 1)
            if m >= 2:
                pe.wait_ge(h_added, KD + m - 1)
            for c in range(3):
                r = ROWS[c]
                last = turn(ps[0:r, 3 + m % 2, c * P:(c + 1) * P], pleT[:, m, c * P:c * P + r], r)
            last.then_inc(h_turned, 1)

        for n in range(CT_PG, CT_PG + KD):
            dense(n, CH_PG0 + 4 * ((n - CT_PG) // 4), xT, KD, wait_xT3 if n == CT_PG else None)
            if n > CT_PG:
                turn_prod(n - CT_PG - 1)
        turn_prod(KD - 1)

    @block.scalar
    def _(act):
        order = [0]

        def step(ins):
            order[0] += 1
            ins.then_inc(act_order, 1)

        def link(ins):
            step(ins)
            act.wait_ge(act_order, order[0])

        for dst, src in row_loads(a, vrow, stage, lstage, g2):
            act.dma_start(dst, src).then_inc(rows_loaded, 16)

        act.wait_ge(ms_ready, 1)
        act.activation(ssum[:, 0:3], ssum[:, 0:3], ACT.Sqrt).then_inc(root_ready, 1)
        act.wait_ge(consts_ready, 5)
        act.wait_ge(vec_ready, 1)
        lam = vT[:, V_LAM:V_LAM + TC]
        link(act.activation(spt[:, 0, :], lam, ACT.Abs))
        link(act.activation(spt[:, 0, :], spt[:, 0, :], ACT.Exp, scale=-1.0))
        step(act.activation(spt[:, 1, :], spt[:, 0, :], ACT.Ln, bias=ones[:, 0:1]))

        def take_xT(base, gain):
            for k in range(1, KD, 2):
                act.wait_ge(x_turned, 2 * base + k + 1)
                act.activation(xT[:, k, :], ps[:, 4, 0:TOK], ACT.Copy, scale=gain(k)).then_inc(xT_act, 1)

        take_xT(0, lambda k: vT[:, V_N1 + k:V_N1 + k + 1])
        act.wait_ge(x_turned, KD)
        act.dma_start(wa[:, :, :], a["lru_wa"][0].rearrange("h i j -> i h j")).then_inc(gates_loaded, 16)
        act.dma_start(wx[:, :, :], a["lru_wx"][0].rearrange("h i j -> i h j")).then_inc(gates_loaded, 16)
        act.dma_start(wr[:, :, 0:NG], a["w_grp"][0].rearrange("(p k) n -> p k n", k=KD)).then_inc(router_loaded, 16)
        act.dma_start(wr[:, :, NG:], a["w_rt"][0].rearrange("(p k) n -> p k n", k=KD)).then_inc(router_loaded, 16)
        act.dma_start(br[:, 0:NG], a["b_grp"][0].partition_broadcast(P)).then_inc(router_loaded, 16)
        act.dma_start(br[:, NG:], a["b_rt"][0].partition_broadcast(P)).then_inc(router_loaded, 16)

        def gates(j):
            act.wait_ge(gates_full, j + 1)
            if j >= 4:
                act.wait_ge(scan_done, 1)
            act.activation(R[:, j % 4, :], ps[:, 3, 0:TOK], ACT.Sigmoid, bias=vT[:, V_BA + j:V_BA + j + 1])
            if j >= 2:
                act.wait_ge(i_used, j - 1)
            act.activation(I[:, j % 2, :], ps[:, 4, 0:TOK], ACT.Sigmoid, bias=vT[:, V_BX + j:V_BX + j + 1])\
                .then_inc(gates_taken, 1)

        def decays(b):
            act.wait_ge(gates_taken, 4 * b + 4)
            act.wait_ge(vec_ready, 2)
            if b:
                act.wait_ge(scan_done, 1)
            else:
                act.wait_ge(y_out, 32)
            for j in range(4):
                act.activation(T[:, j, :], R[:, j, :], ACT.Tanh, scale=negc[:, 4 * b + j:4 * b + j + 1])
            for j in range(4):
                last = act.activation(R[:, j, :], R[:, j, :], ACT.Exp, scale=negc[:, 4 * b + j:4 * b + j + 1])
            last.then_inc(tanh_ready, 1)
            act.wait_ge(z_ready, b + 1)
            act.activation(T[:, :, :], T[:, :, :], ACT.Sqrt, scale=-1.0).then_inc(beta_ready, 1)

        for n in range(CT_OUT):
            g, i = n // 4, n % 4
            col = V_BIN + GROUP_COL[g] // P + (i if g >= 4 else i % 2 + i // 2 * TC)
            bias = vT[:, col:col + 1]
            bank = ps[:, n % 3, 0:TOK]
            act.wait_ge(acc_full, n + 1)
            if g < 4 and i < 2:
                act.activation(U[:, 2 * g + i, CK - 1:], bank, ACT.Identity, bias=bias).then_inc(acc_free, 1)
            elif g < 4:
                t = 2 * g + i - 2
                if t >= 2:
                    act.wait_ge(u_ready, t - 1)
                act.activation(gate_buf[t % 2][:, :], bank, ACT.Sigmoid, bias=bias).then_inc(acc_free, 1)
            elif g in (4, 5):
                act.activation(L[:, n - 16, LK - 1:], bank, ACT.Identity, bias=bias).then_inc(acc_free, 1)
            else:
                t = n - 24
                if t >= 2:
                    act.wait_ge(mixr_ready, t - 1)
                act.activation(gate_buf[t % 2][:, :], bank, ACT.Gelu_apprx_tanh, bias=bias).then_inc(acc_free, 1)
            if 20 <= n < 28:
                gates(n - 20)
            if n == 23:
                decays(0)
            if n == 27:
                decays(1)
            if 25 <= n < 29:
                p = n - 25
                for j in range(2 * p, 2 * p + 2):
                    act.wait_ge(centred, j + 1)
                    if p:
                        act.wait_ge(sq_used, p)
                    act.activation(sq[:, j % 2, :], mix[:, j, :], ACT.Square).then_inc(sq_ready, 1)
            if n == 30:
                act.wait_ge(var_ready, 1)
                act.activation(I[:, 1, :], I[:, 0, :], ACT.Sqrt).then_inc(sd_ready, 1)
        for j in range(TC):
            act.wait_ge(scaled, j + 1)
            act.activation(mix[:, j, :], mix[:, j, :], ACT.Silu, scale=vT[:, V_LNG + j:V_LNG + j + 1],
                           bias=vT[:, V_LNB + j:V_LNB + j + 1]).then_inc(mixc_ready, 1)
        for m in range(KD):
            n = CT_OUT + m
            act.wait_ge(acc_full, n + 1)
            if m >= 2:
                act.wait_ge(h_turned, m - 1)
            act.activation(hT[:, m % 2, :], ps[:, n % 3, 0:TOK], ACT.Copy).then_inc(hT_ready, 1)
        act.wait_ge(ms_ready, 2)
        act.activation(ssum[:, 0:3], ssum[:, 0:3], ACT.Sqrt).then_inc(root_ready, 1)
        take_xT(8, lambda k: g2[:, k:k + 1])
        act.wait_ge(softmax_in, 1)
        act.activation(gex[:, :, :], gex[:, :, :], ACT.Exp)
        act.activation(ex[:, :], ex[:, :], ACT.Exp).then_inc(softmax_out, 1)
        act.wait_ge(p_turned, 1)
        act.activation(pT[:, 1, :], ps[:, 3, 0:TOK], ACT.Copy).then_inc(pT_ready, 1)
        act.wait_ge(pad_ready, 1)
        for m in range(1, 2 * KD, 2):
            half, k = m // KD, m % KD
            act.wait_ge(sort_full, m + 1)
            act.activation(xsort[:, k, half * HALF:(half + 1) * HALF], ps[:, 5, 0:HALF], ACT.Copy,
                           scale=g2[:, k:k + 1]).then_inc(sort_act, 1)
        for m in range(KD):
            n = CT_PLE + m
            act.wait_ge(acc_full, n + 1)
            act.activation(pleT[:, m, :], ps[:, n % 3, 0:TOK], ACT.Copy).then_inc(acc_free, 1)

        def expert(i, par, sems):
            act.wait_ge(sems["products"], i + 1)
            act.activation(sgl[WIN:2 * WIN, :], ps[0:WIN, 0, :], ACT.Silu).then_inc(sems["silu"], 1)
            act.wait_ge(sems["down"], i + 1)
            if sems is main:
                act.wait_ge(y_out, (i + 1) * 16)
            act.activation(ysb[:, par, 0:512], ps[:, 2, :], ACT.Copy).then_inc(sems["evac"], 1)

        act.wait_ge(table_ready, 1)
        with act.Fori(0, E, 2) as e2:
            for par in range(2):
                expert(e2 + par, par, main)
        act.wait_ge(table_out, 16)
        n_over = act.value_load(offs[0:1, 40:41], min_val=0, max_val=MAX_OVER)
        with act.If(n_over > 0):
            with act.Fori(0, n_over) as i:
                act.wait_ge(over_free, i + 1)
                expert(i, 0, extra)
        act.wait_ge(ms_ready, 3)
        act.activation(ssum[:, 0:3], ssum[:, 0:3], ACT.Sqrt).then_inc(root_ready, 1)
        act.dma_start(fing[:, :], a["final_g"].partition_broadcast(P)).then_inc(fing_loaded, 16)
        take_xT(16, lambda k: vT[:, V_PN + k:V_PN + k + 1])
        for m in range(KD):
            n = CT_PG + m
            act.wait_ge(acc_full, n + 1)
            if m >= 2:
                act.wait_ge(prod_ready, m - 1)
            act.activation(gate_tail(m), ps[:, n % 3, 0:TOK], ACT.Sigmoid,
                           bias=vT[:, V_BPG + m:V_BPG + m + 1]).then_inc(acc_free, 1)
        act.wait_ge(ms_ready, 4)
        act.activation(ssum[:, 0:3], ssum[:, 0:3], ACT.Sqrt).then_inc(root_ready, 1)
        for c in range(3):
            act.wait_ge(y_ready, c + 1)
            dst = o["y_prompt"][0, c * P:(c + 1) * P, :] if c < 2 else o["y_sample"][:, 0, :]
            act.dma_start(dst, h[0:ROWS[c], c, :]).then_inc(out_done, 16)
        act.wait_ge(out_done, 48)

    @block.vector
    def _(dve):
        order = [0]

        def step(ins):
            order[0] += 1
            ins.then_inc(dve_order, 1)
            return order[0]

        def link(ins):
            dve.wait_ge(dve_order, step(ins))

        def stt(out, in0, s, in1, op0, op1):
            return dve.scalar_tensor_tensor(out=out, in0=in0, scalar=s, in1=in1, op0=op0, op1=op1)

        def mean_square(dump, n):
            for c in range(3):
                r = ROWS[c]
                last = dve.tensor_tensor_reduce(dump[0:r, c, :], h[0:r, c, :], h[0:r, c, :], 1.0, 0.0, ALU.mult,
                                                ALU.add, ssum[0:r, c:c + 1])
            link(last)
            dve.tensor_scalar(ssum[:, 0:3], ssum[:, 0:3], 1.0 / D, EPS, ALU.mult, ALU.add).then_inc(ms_ready, 1)
            dve.wait_ge(root_ready, n)
            link(dve.reciprocal(rstd[:, 0:3], ssum[:, 0:3]))

        link(dve.memset(ssum[:, :], 1.0))
        dve.wait_ge(x_loaded, 32)
        mean_square(xs, 1)
        for c in range(3):
            r = ROWS[c]
            dve.tensor_scalar(xs[0:r, c, :], h[0:r, c, :], rstd[0:r, c:c + 1], None, ALU.mult).then_inc(xs_ready, 1)
        dve.wait_ge(vec_turned, 1)
        dve.tensor_copy(vT[:, :], ps[:, 7, 0:NV]).then_inc(vec_ready, 1)
        dve.wait_ge(vec_ready, 1)

        cw = vT[:, 0:TC * (CK - 1)].rearrange("p (t c) -> p c t", c=TC)
        for j in range(TC):
            dve.wait_ge(state_turned, j + 1)
            link(dve.tensor_tensor(ptmp[:, :].rearrange("p (b t) -> p b t", b=NB),
                                   ps[:, 5 + j % 2, 0:240].rearrange("p (b t) -> p b t", b=NB),
                                   cw[:, j:j + 1, :].broadcast_to([P, NB, CK - 1]), ALU.mult))
            dve.tensor_reduce(pconv[:, j, :], ptmp[:, :].rearrange("p (b t) -> p b t", b=NB), AX, ALU.add)\
                .then_inc(state_used, 1)
            dve.wait_ge(state_used, j + 1)
        link(dve.tensor_tensor(pconv[:, :, :], pconv[:, :, :],
                               vT[:, V_DWB:V_DWB + TC].unsqueeze(2).broadcast_to([P, TC, NB]), ALU.add))
        dve.wait_ge(state_turned, TC + 1)
        lw = vT[:, V_LW:V_LW + TC * (LK - 1)].rearrange("p (t c) -> p c t", c=TC)
        for j in range(TC):
            link(dve.tensor_tensor(ptmp[:, 0:24].rearrange("p (b t) -> p b t", b=NB),
                                   ps[:, 7, j * 24:(j + 1) * 24].rearrange("p (b t) -> p b t", b=NB),
                                   lw[:, j:j + 1, :].broadcast_to([P, NB, LK - 1]), ALU.mult))
            link(dve.tensor_reduce(plru[:, j, :], ptmp[:, 0:24].rearrange("p (b t) -> p b t", b=NB), AX, ALU.add))
        link(dve.tensor_tensor(plru[:, :, :], plru[:, :, :],
                               vT[:, V_LB:V_LB + TC].unsqueeze(2).broadcast_to([P, TC, NB]), ALU.add))

        def take_xT(base, gain):
            for k in range(0, KD, 2):
                dve.wait_ge(x_turned, 2 * base + k + 1)
                dve.tensor_scalar(xT[:, k, :], ps[:, 3, 0:TOK], gain(k), None, ALU.mult).then_inc(xT_dve, 1)

        take_xT(0, lambda k: vT[:, V_N1 + k:V_N1 + k + 1])

        dve.wait_ge(act_order, 3)
        z, ln1, t = spt[:, 0, :], spt[:, 1, :], spt[:, 2, :]
        link(dve.tensor_scalar(t, z, 1.0, -1.0, ALU.add, ALU.add))
        link(dve.tensor_scalar(negc[:, :], t, 0.0, None, ALU.is_equal))
        link(dve.tensor_tensor(t, t, negc[:, :], ALU.add))
        link(dve.tensor_tensor(ln1, ln1, negc[:, :], ALU.add))
        link(dve.reciprocal(t, t))
        link(dve.tensor_tensor(ln1, ln1, t, ALU.mult))
        link(dve.tensor_tensor(ln1, ln1, z, ALU.mult))
        link(dve.tensor_scalar(t, vT[:, V_LAM:V_LAM + TC], -1.0, 0.0, ALU.mult, ALU.max))
        link(dve.tensor_tensor(t, t, ln1, ALU.add))
        dve.tensor_scalar(negc[:, :], t, -8.0, None, ALU.mult).then_inc(vec_ready, 1)

        dve.wait_ge(consts_ready, 5)
        for p in range(0, TC, 2):
            for j in (p, p + 1):
                n = 4 * (j // 2) + 2 + j % 2
                dve.wait_ge(acc_free, n + 1)
                dve.tensor_tensor(U[:, j, CK - 1:], U[:, j, CK - 1:], gate_buf[j % 2][:, :], ALU.mult)\
                    .then_inc(u_ready, 1)
            dve.wait_ge(u_ready, p + 2)
            last = {}
            for t in range(CK):
                for j in (p, p + 1):
                    w = vT[:, t * TC + j:t * TC + j + 1]
                    if t == 0:
                        last[j] = step(dve.tensor_scalar(mix[:, j, 0:SEQ], U[:, j, 0:SEQ], w,
                                                         vT[:, V_DWB + j:V_DWB + j + 1], ALU.mult, ALU.add))
                    else:
                        dve.wait_ge(dve_order, last[j])
                        last[j] = step(stt(mix[:, j, 0:SEQ], U[:, j, t:t + SEQ], w, mix[:, j, 0:SEQ],
                                           ALU.mult, ALU.add))
            for j in (p, p + 1):
                w = vT[:, (CK - 1) * TC + j:(CK - 1) * TC + j + 1]
                stt(mix[:, j, SEQ:TOK], U[:, j, UW - NB:UW], w, pconv[:, j, :], ALU.mult, ALU.add)\
                    .then_inc(conv_done, 1)

        def lconv(j):
            dve.wait_ge(acc_free, 16 + j + 1)
            for t in range(LK):
                w = vT[:, V_LW + t * TC + j:V_LW + t * TC + j + 1]
                if t == 0:
                    link(dve.tensor_scalar(lxc[:, j, 0:SEQ], L[:, j, 0:SEQ], w, vT[:, V_LB + j:V_LB + j + 1],
                                           ALU.mult, ALU.add))
                else:
                    link(stt(lxc[:, j, 0:SEQ], L[:, j, t:t + SEQ], w, lxc[:, j, 0:SEQ], ALU.mult, ALU.add))
            stt(lxc[:, j, SEQ:TOK], L[:, j, LW - NB:LW], w, plru[:, j, :], ALU.mult, ALU.add).then_inc(lconv_done, 1)

        def gated(j):
            dve.wait_ge(gates_taken, j + 1)
            dve.tensor_tensor(lxc[:, j, :], lxc[:, j, :], I[:, j % 2, :], ALU.mult).then_inc(i_used, 1)

        def recur(b):
            dve.wait_ge(tanh_ready, b + 1)
            dve.wait_ge(i_used, 4 * b + 4)
            link(dve.tensor_scalar(T[:, :, :], T[:, :, :], -1e-30, None, ALU.min))
            for x in (0, 2):
                link(dve.tensor_tensor(I[:, :, :], R[:, x:x + 2, :], R[:, x:x + 2, :], ALU.mult))
                last = stt(T[:, x:x + 2, :], I[:, :, :], 1.0, T[:, x:x + 2, :], ALU.add, ALU.mult)
                if x == 0:
                    link(last)
            last.then_inc(z_ready, 1)
            dve.wait_ge(beta_ready, b + 1)
            link(dve.tensor_tensor(T[:, :, :], T[:, :, :], lxc[:, 4 * b:4 * b + 4, :], ALU.mult))
            for j in range(4):
                dve.tensor_tensor_scan(mix[:, TC + 4 * b + j, 0:SEQ], R[:, j, 0:SEQ], T[:, j, 0:SEQ], 0.0,
                                       ALU.mult, ALU.add)
            h0 = vT[:, V_H0:V_H0 + 64].rearrange("p (b c) -> p c b", c=TC)[:, 4 * b:4 * b + 4, :]
            link(dve.tensor_tensor(R[:, :, SEQ:TOK], R[:, :, SEQ:TOK], h0, ALU.mult))
            link(dve.tensor_tensor(mix[:, TC + 4 * b:TC + 4 * b + 4, SEQ:TOK], R[:, :, SEQ:TOK], T[:, :, SEQ:TOK],
                                   ALU.add))
            dve.tensor_copy(htail[:, 4 * b:4 * b + 4, :], mix[:, TC + 4 * b:TC + 4 * b + 4, SEQ - 1:TOK])\
                .then_inc(scan_done, 1)
            dve.wait_ge(scan_done, b + 1)

        def gelu_mul(j):
            dve.wait_ge(acc_free, 24 + j + 1)
            dve.tensor_tensor(mix[:, TC + j, :], mix[:, TC + j, :], gate_buf[j % 2][:, :], ALU.mult)\
                .then_inc(mixr_ready, 1)

        for j in range(4):
            lconv(j)
        for j in range(4):
            lconv(4 + j)
            gated(j)
        recur(0)
        gelu_mul(0)
        gated(4)
        dve.wait_ge(mean_full, 1)
        for j in range(TC):
            stt(mix[:, j, :], ps[:, 6, 0:TOK], -1.0 / DC, mix[:, j, :], ALU.mult, ALU.add).then_inc(centred, 1)
        for j in range(1, 4):
            gelu_mul(j)
            gated(4 + j)
        recur(1)
        for j in range(4, 6):
            gelu_mul(j)
        dve.wait_ge(sq_used, 4)
        dve.wait_ge(i_used, TC)
        dve.tensor_scalar(I[:, 0, :], ps[:, 7, 0:TOK], 1.0 / DC, EPS, ALU.mult, ALU.add).then_inc(var_ready, 1)
        gelu_mul(6)
        dve.wait_ge(sd_ready, 1)
        link(dve.reciprocal(I[:, 0, :], I[:, 1, :]))
        for j in range(TC):
            dve.tensor_tensor(mix[:, j, :], mix[:, j, :], I[:, 0, :], ALU.mult).then_inc(scaled, 1)
        gelu_mul(7)

        def add_back(m, base):
            dve.wait_ge(h_turned, base + m + 1)
            b = ps[:, 3 + m % 2, :]
            cols = slice(m * P, (m + 1) * P)
            dve.tensor_tensor(h[:, 0:2, cols], h[:, 0:2, cols], b[:, 0:2 * P].rearrange("p (c d) -> p c d", c=2), ALU.add)
            dve.tensor_tensor(h[0:NB, 2, cols], h[0:NB, 2, cols], b[0:NB, 2 * P:3 * P], ALU.add).then_inc(h_added, 1)

        for m in range(KD):
            add_back(m, 0)
            if m in (2, 4, 6):
                w = m // 2 - 1
                dst, r = [(sc_out, CK - 1 + NB), (sl_out, LK - 1 + NB), (sh_out, 1 + NB)][w]
                dve.wait_ge(tail_turned, w + 1)
                dve.tensor_copy(dst[0:r, :].rearrange("p (a b) -> p a b", a=2), ps[0:r, 5:7, :]).then_inc(tail_taken, 1)

        dve.wait_ge(h_added, KD)
        dve.wait_ge(state_out, 16 * 8)
        mean_square(xs, 2)
        for c in range(3):
            r = ROWS[c]
            dve.tensor_scalar(xs2[0:r, c, :, :], h[0:r, c, :].rearrange("t (p k) -> t k p", k=KD),
                              rstd[0:r, c:c + 1], None, ALU.mult).then_inc(xs_ready, 1)
        take_xT(8, lambda k: g2[:, k:k + 1])
        link(dve.memset(logit[:, :, :], 0.0))
        link(dve.memset(gl[:, :, :], -3.0e38))
        link(dve.memset(rank[:, :, :], 0.0))
        dve.wait_ge(logits_full, 1)
        lg = ps[:, 5, 0:192].rearrange("p (c n) -> p c n", c=3)
        dve.tensor_tensor(logit[:, 0:2, :], lg[:, 0:2, 0:NG + E], br[:, :].unsqueeze(1).broadcast_to([P, 2, NG + E]), ALU.add)
        link(dve.tensor_tensor(logit[0:NB, 2, :], lg[0:NB, 2, 0:NG + E], br[0:NB, :], ALU.add))
        link(dve.tensor_copy(gl[:, :, 0:NG], logit[:, :, 0:NG]))
        for c in range(3):
            last = dve.max(gmx[:, c, :], gl[:, c, :])
        link(last)
        for c in range(3):
            last = dve.max_index(gix[:, c, :], gmx[:, c, :], gl[:, c, :])
        link(last)
        link(dve.tensor_copy(gf[:, :], gix[:, :, 0]))
        link(dve.tensor_tensor(gex[:, :, :], logit[:, :, 0:NG], gmx[:, :, 0:1].broadcast_to([P, 3, NG]), ALU.subtract))
        dve.wait_ge(iotas_ready, 5)
        link(dve.tensor_tensor(oh4[:, :, :], i32r[:, 0:NG].unsqueeze(1).broadcast_to([P, 3, NG]),
                               gf[:, :].unsqueeze(2).broadcast_to([P, 3, NG]), ALU.is_equal))
        for c in range(3):
            last = dve.tensor_tensor(el[:, c, :, :], logit[:, c, NG:].rearrange("p (g j) -> p g j", g=NG),
                                     oh4[:, c, :].unsqueeze(2).broadcast_to([P, NG, EG]), ALU.mult)
        link(last)
        link(dve.tensor_reduce(ein[:, :, :], el[:, :, :, :].rearrange("p c g j -> p c j g"), AX, ALU.add))
        for c in range(3):
            last = dve.max(emx[:, c, :], ein[:, c, :])
        link(last)
        link(dve.tensor_tensor(ex[:, :], emx[:, :, 1], emx[:, :, 0], ALU.subtract))
        for c in range(3):
            last = dve.max_index(eix[:, c, :], emx[:, c, :], ein[:, c, :])
        last.then_inc(softmax_in, 1)
        dve.wait_ge(softmax_in, 1)
        link(dve.tensor_copy(ef[:, :, :], eix[:, :, 0:2]))
        for q in range(2):
            last = stt(ef[:, :, q], gf[:, :], float(EG), ef[:, :, q], ALU.mult, ALU.add)
        link(last)
        for q in range(2):
            last = dve.tensor_tensor(oh[:, q, :, :], i32r[:, :].unsqueeze(1).broadcast_to([P, 3, E]),
                                     ef[:, :, q].unsqueeze(2).broadcast_to([P, 3, E]), ALU.is_equal)
        link(last)
        dve.tensor_tensor(asg[:, :, :], oh[:, 0, :, :], oh[:, 1, :, :], ALU.add).then_inc(assigned, 1)
        dve.wait_ge(softmax_out, 1)
        link(dve.tensor_reduce(gw[:, :], gex[:, :, :], AX, ALU.add))
        link(dve.tensor_scalar(wts[:, 1, :], ex[:, :], 1.0, None, ALU.add))
        link(dve.tensor_tensor(gw[:, :], gw[:, :], wts[:, 1, :], ALU.mult))
        link(dve.reciprocal(wts[:, 0, :], gw[:, :]))
        link(dve.tensor_tensor(wts[:, 1, :], wts[:, 0, :], ex[:, :], ALU.mult))
        dve.wait_ge(ranks_full, 1)
        rk = ps[:, 6, 0:192].rearrange("p (c n) -> p c n", c=3)
        dve.tensor_copy(rank[:, 0:2, :], rk[:, 0:2, 0:E])
        dve.tensor_copy(rank[0:NB, 2, :], rk[0:NB, 2, 0:E])
        link(dve.tensor_copy(cnt[:, :], ps[:, 6, 192:192 + E]))
        link(dve.tensor_tensor_scan(off[:, :], ones[:, 0:E], cnt[:, :], 0.0, ALU.mult, ALU.add))
        link(dve.tensor_tensor(off[:, :], off[:, :], cnt[:, :], ALU.subtract))
        for q in range(2):
            link(dve.tensor_tensor(prod[:, :, :], oh[:, q, :, :], rank[:, :, :], ALU.mult))
            link(dve.tensor_reduce(rnk[:, q, :], prod[:, :, :], AX, ALU.add))
            link(dve.tensor_tensor(prod[:, :, :], oh[:, q, :, :], off[:, :].unsqueeze(1).broadcast_to([P, 3, E]), ALU.mult))
            link(dve.tensor_reduce(pos[:, q, :], prod[:, :, :], AX, ALU.add))
        link(dve.tensor_tensor(pos[:, :, :], pos[:, :, :], rnk[:, :, :], ALU.add))
        dve.wait_ge(iotas_ready, 6)
        for c in range(3):
            r = ROWS[c]
            link(dve.tensor_scalar(onehot[0:r, c, :], iota[0:r, :], pos[0:r, 0, c:c + 1], None, ALU.is_equal))
            stt(onehot[0:r, c, :], iota[0:r, :], pos[0:r, 1, c:c + 1], onehot[0:r, c, :], ALU.is_equal, ALU.add)\
                .then_inc(onehot_ready, 1)
        link(dve.tensor_scalar(rnk[:, :, :], rnk[:, :, :], float(WIN), float(XW), ALU.is_ge, ALU.mult))
        link(dve.tensor_tensor(rowix[:, :, :], pos[:, :, :], rnk[:, :, :], ALU.add))
        link(dve.tensor_copy(offs[0:1, 0:E], off[0:1, :]))
        link(dve.memset(offs[0:1, E:E + 1], NSLOT))
        cb = cnt[:, :].unsqueeze(2).broadcast_to([P, E, 4])
        wb = win64[:, :].unsqueeze(1).broadcast_to([P, E, 4])
        link(dve.tensor_tensor(over[:, :, :], cb, wb, ALU.is_gt))
        ov = over[:, :, :].rearrange("p e c -> p (e c)")
        oi = oidx[:, :, :].rearrange("p e c -> p (e c)")
        link(dve.tensor_tensor_scan(oi, ones[:, :], ov, 0.0, ALU.mult, ALU.add))
        link(dve.tensor_copy(offs[0:1, 40:41], oi[0:1, E * 4 - 1:E * 4]))
        link(dve.tensor_tensor(oi, oi, ov, ALU.subtract))
        link(dve.tensor_scalar(osel[:, :, :], oidx[:, :, :], pidx[:, 0:1], None, ALU.is_equal))
        link(dve.tensor_tensor(osel[:, :, :], osel[:, :, :], over[:, :, :], ALU.mult))
        link(dve.tensor_tensor(opr[:, :, :], osel[:, :, :], i32r[:, :].unsqueeze(2).broadcast_to([P, E, 4]), ALU.mult))
        link(dve.tensor_reduce(otab[:, 0:1], opr[:, :, :].rearrange("p e c -> p (e c)"), AX, ALU.add))
        link(dve.tensor_tensor(opr[:, :, :], off[:, :].unsqueeze(2).broadcast_to([P, E, 4]), wb, ALU.add))
        link(dve.tensor_tensor(opr[:, :, :], opr[:, :, :], osel[:, :, :], ALU.mult))
        link(dve.tensor_reduce(otab[:, 1:2], opr[:, :, :].rearrange("p e c -> p (e c)"), AX, ALU.add))
        dve.tensor_copy(otabi[:, :], otab[:, :]).then_inc(table_ready, 1)
        dve.wait_ge(p_turned, 1)
        dve.tensor_copy(pT[:, 0, :], ps[:, 7, 0:TOK]).then_inc(pT_ready, 1)
        dve.memset(xsort[:, :, NSLOT:XW], 0.0).then_inc(pad_ready, 1)
        for m in range(0, 2 * KD, 2):
            half, k = m // KD, m % KD
            dve.wait_ge(sort_full, m + 1)
            dve.tensor_scalar(xsort[:, k, half * HALF:(half + 1) * HALF], ps[:, 4, 0:HALF], g2[:, k:k + 1], None,
                              ALU.mult).then_inc(sort_dve, 1)
        dve.wait_ge(sort_dve, KD)
        dve.wait_ge(sort_act, KD)
        dve.wait_ge(table_ready, 1)
        dve.wait_ge(acc_full, CT_PG)

        def take_window(start, window):
            dve.tensor_copy(xwin[:, :, :], xsort[:, :, bass.ds(start, WIN)]).then_inc(window, 1)

        def expert(i, sems):
            dve.wait_ge(sems["silu"], i + 1)
            dve.tensor_tensor(sgl[WIN:2 * WIN, :], sgl[WIN:2 * WIN, :], ps[WIN:2 * WIN, 0, :], ALU.mult)\
                .then_inc(sems["gated"], 1)
            dve.wait_ge(sems["turned"], i + 1)
            dve.tensor_copy(hid[:, :, :].rearrange("p t w -> p (t w)"), ps[:, 1, 0:4 * WIN]).then_inc(sems["hid"], 1)

        def take_results(i, par, sems):
            dve.wait_ge(sems["down"], i + 1)
            if sems is main:
                dve.wait_ge(y_out, (i + 1) * 16)
            dve.tensor_copy(ysb[:, par, 512:1024], ps[:, 3, :]).then_inc(sems["evac"], 1)

        take_window(0, main["window"])
        with dve.Fori(0, E, 2) as e2:
            for par in range(2):
                expert(e2 + par, main)
                start = dve.value_load(offs[0:1, bass.ds(e2 + par + 1, 1)], min_val=0, max_val=NSLOT)
                take_window(start, main["window"])
                take_results(e2 + par, par, main)
        dve.wait_ge(table_out, 16)
        n_over = dve.value_load(offs[0:1, 40:41], min_val=0, max_val=MAX_OVER)
        with dve.If(n_over > 0):
            with dve.Fori(0, n_over) as i:
                start = dve.value_load(ov_dram[bass.ds(i, 1), 1:2], min_val=0, max_val=NSLOT)
                dve.wait_ge(main["down"], E)
                take_window(start, extra["window"])
                expert(i, extra)
                take_results(i, 0, extra)

        for q, s in ((0, rows_back), (1, rows_back2)):
            dve.wait_ge(s, 48)
            for c in range(3):
                r = ROWS[c]
                ins = stt(h[0:r, c, :], g0[0:r, c, :], wts[0:r, q, c:c + 1], h[0:r, c, :], ALU.mult, ALU.add)
                if q == 0:
                    ins.then_inc(h2_first, 1)
            if q == 0:
                dve.wait_ge(h2_first, 3)
        link(ins)
        mean_square(g0, 3)
        for c in range(3):
            r = ROWS[c]
            dve.tensor_scalar(g0[0:r, c, :], h[0:r, c, :], rstd[0:r, c:c + 1], None, ALU.mult).then_inc(xs_ready, 1)
        take_xT(16, lambda k: vT[:, V_PN + k:V_PN + k + 1])
        for m in range(KD):
            dve.wait_ge(acc_free, freed(CT_PG + m))
            dve.tensor_tensor(pleT[:, m, :], pleT[:, m, :], gate_tail(m), ALU.mult).then_inc(prod_ready, 1)
            if m:
                add_back(m - 1, KD)
        add_back(KD - 1, KD)
        dve.wait_ge(h_added, 2 * KD)
        mean_square(g0, 4)
        dve.wait_ge(fing_loaded, 16)
        for c in range(3):
            r = ROWS[c]
            stt(h[0:r, c, :], h[0:r, c, :], rstd[0:r, c:c + 1], fing[0:r, :], ALU.mult, ALU.mult).then_inc(y_ready, 1)

    block.__exit__(None, None, None)


N_ROWS = 18


def row_loads(a, vrow, stage, lstage, g2):
    def rows(x):
        return x.rearrange("l (r p) -> (l r) p", p=P)

    cw = a["conf_dw_w"].rearrange("l t (c p) -> (l t c) p", p=P)
    yield vrow[:, 0, :], cw[0:P, :]
    yield vrow[0:120, 1, :], cw[P:248, :]
    at = 0
    for name, n in (("norm1_g", 16), ("ple_norm_g", 16), ("b_in", 32), ("b_pg", 16), ("conf_dw_b", 8),
                    ("conf_ln_g", 8), ("conf_ln_b", 8)):
        yield vrow[at:at + n, 2, :], rows(a[name])
        at += n
    yield vrow[0:32, 3, :], a["lru_conv_w"].rearrange("l t (c p) -> (l t c) p", p=P)
    yield vrow[32:40, 3, :], rows(a["lru_conv_b"])
    yield vrow[40:48, 3, :], a["lru_ba"].rearrange("l h j -> (l h) j")
    yield vrow[48:56, 3, :], a["lru_bx"].rearrange("l h j -> (l h) j")
    yield vrow[56:64, 3, :], rows(a["lru_lambda"])
    yield vrow[64:128, 3, :], a["state_lru_h"].rearrange("l b (c p) -> (l b c) p", p=P)
    yield stage[0:120, :, :], a["state_conf_conv"].rearrange("l (q b) t c -> (b t) (l q) c", q=2)
    yield lstage[0:24, :], a["state_lru_conv"].rearrange("l b t c -> (l b t) c")
    yield g2[:, :], a["norm2_g"].rearrange("l (p k) -> p (l k)", k=KD)


INPUTS = ["x_prompt", "x_sample", "state_conf_conv", "state_lru_conv", "state_lru_h", "p_prompt", "p_sample",
          "norm1_g", "w_in", "b_in", "conf_dw_w", "conf_dw_b", "conf_ln_g", "conf_ln_b", "lru_conv_w", "lru_conv_b",
          "lru_wa", "lru_ba", "lru_wx", "lru_bx", "lru_lambda", "w_out", "norm2_g", "w_grp", "b_grp", "w_rt", "b_rt",
          "w_gate", "w_up", "w_down", "ple_norm_g", "w_ple", "w_pg", "b_pg", "final_g"]
OUTPUTS = [("y_prompt", (1, SEQ, D)), ("y_sample", (NB, 1, D)), ("conf_prompt", (1, 1, CK - 1, DC)),
           ("conf_sample", (1, NB, CK - 1, DC)), ("lru_prompt", (1, 1, LK - 1, DC)),
           ("lru_sample", (1, NB, LK - 1, DC)), ("h_prompt", (1, 1, DC)), ("h_sample", (1, NB, DC))]


def kernel(**inputs):
    import numpy as _np
    import concourse.bacc as _bacc
    from concourse import mybir as _mybir
    from concourse.bass_utils import run_bass_kernel_spmd as _run

    nc = _bacc.Bacc("TRN2", target_bir_lowering=False, num_devices=1)
    arrays, a, o = {}, {}, {}
    for name in INPUTS:
        x = _np.ascontiguousarray(inputs[name])
        arrays[f"in_{name}_dram"] = x
        a[name] = nc.dram_tensor(f"in_{name}_dram", x.shape, _mybir.dt.from_np(x.dtype), kind="ExternalInput").ap()
    for name, shape in OUTPUTS:
        o[name] = nc.dram_tensor(f"out_{name}_dram", shape, _mybir.dt.float32, kind="ExternalOutput").ap()
    build(nc, a, o)
    r = _run(nc, [arrays], core_ids=[0])
    return tuple(r.results[0][f"out_{name}_dram"] for name, _ in OUTPUTS)
```

```python
import numpy as np

import concourse.bass as bass
from concourse import mybir
from concourse.alu_op_type import AluOpType as ALU

ACT = mybir.ActivationFunctionType
F32 = mybir.dt.float32
I32 = mybir.dt.int32
U32 = mybir.dt.uint32
AX = mybir.AxisListType.X

D = 2048
SEQ = 256
NB = 8
TOK = SEQ + NB
DC = 1024
CK = 31
LK = 4
E = 32
NG = 4
EG = E // NG
F = D // 4
DP = 256
EPS = 1e-6
P = 128
KD = D // P
TC = DC // P
ROWS = [P, P, NB]

NS = 12
CH_IN = 32
CH_OUT = 16
CH_PLE = 2
CH_FRONT = CH_IN + CH_OUT + CH_PLE
CH_EXP = 12
CH_PG0 = CH_FRONT + E * CH_EXP

WIN = 64
NSLOT = 2 * TOK
XW = NSLOT + WIN
HALF = NSLOT // 2
FILL = -(-(XW + WIN) // (2 * P)) * 2 * P
MAX_OVER = NSLOT // WIN

V_CW = 0
V_N1, V_PN, V_BIN, V_BPG, V_DWB, V_LNG, V_LNB = 248, 264, 280, 312, 328, 336, 344
V_LW, V_LB, V_BA, V_BX, V_LAM, V_H0 = 352, 384, 392, 400, 408, 416
NV = 480

GROUP_COL = [0, 256, 512, 768, 2048, 2560, 3072, 3584]
UW = CK - 1 + TOK
LW = LK - 1 + TOK
CT_IN, CT_OUT, CT_PLE, CT_PG = 0, 32, 48, 64


def build(nc, a, o):
    top = [((nc.sbuf_base + 31) // 32) * 32]

    def region(size):
        at = top[0]
        top[0] += size
        assert top[0] <= nc.sbuf_usable_end, (top[0], nc.sbuf_usable_end)
        return at

    def place(name, shape, dt, at):
        return nc.alloc_sbuf_tensor_at(name, shape, dt, offset=at)

    def sem(name):
        return nc.alloc_semaphore(name)

    r_ring = region(NS * 8192)
    r_h = region(3 * 8192)
    r_big = region(KD * XW * 4)
    r_xs = region(3 * 8192)
    r_xt = region(KD * TOK * 4)
    r_const = region(10616)

    ring = place("ring", [P, NS, D], F32, r_ring)
    h = place("h", [P, 3, D], F32, r_h)

    U = place("U", [P, TC, UW], F32, r_big)
    at = r_big + TC * UW * 4
    mix = place("mix", [P, KD, TOK], F32, at)
    stage = place("stage", [P, 2, DC], F32, at)
    lstage = place("lstage", [P, DC], F32, at + 8192)
    vrow = place("vrow", [P, 5, P], F32, at + 12288)
    ptmp = place("ptmp", [P, 240], F32, at + 14848)
    at += KD * TOK * 4
    L = place("L", [P, TC, LW], F32, at)
    at += TC * LW * 4
    wr = place("wr", [P, KD, NG + E], F32, at)
    at += KD * (NG + E) * 4
    br = place("br", [P, NG + E], F32, at)
    at += 160
    htail = place("htail", [P, TC, NB + 1], F32, at)
    at += 288
    assert at <= r_big + KD * XW * 4
    sdump2 = place("sdump2", [P, 512], F32, r_big + 4 * 8192)
    xsort = place("xsort", [P, KD, XW], F32, r_big)
    g0 = place("g0", [P, 3, D], F32, r_big)
    hg = place("hg", [P, 3, D], F32, r_big)
    fing = place("fing", [P, D], F32, r_big + 3 * 8192)

    xdump = place("xdump", [P, 2, D], F32, r_xs)
    sdump = place("sdump", [P, 512], F32, r_xs + 12288)
    dg = place("dg", [P, 3, P], F32, r_xs + 16896)
    g1 = place("g1", [P, 3, D], F32, r_xs + 16896)
    lxc = place("lxc", [P, TC, TOK], F32, r_xs)
    wa = place("wa", [P, TC, P], F32, r_xs + 8448)
    wx = place("wx", [P, TC, P], F32, r_xs + 8448 + 4096)
    R = place("R", [P, 4, TOK], F32, r_xs + 16640)
    I = place("I", [P, 2, TOK], F32, r_xs + 20864)
    sc_out = place("sc_out", [P, DC], F32, r_xs)
    sl_out = place("sl_out", [P, DC], F32, r_xs + 4096)
    sh_out = place("sh_out", [P, DC], F32, r_xs + 8192)
    pleT = place("pleT", [P, KD, TOK], F32, r_xs)

    xT = place("xT", [P, KD, TOK], F32, r_xt)
    hT = place("hT", [P, 2, TOK], F32, r_xt)
    onehot = place("onehot", [P, 3, NSLOT], F32, r_xt)
    iota = place("iota", [P, NSLOT], F32, r_xt + 6336)
    rxT = place("rxT", [P, 3, TOK], F32, r_xt + 13632)
    prow = place("prow", [P, 3, DP], F32, r_xt + 8448)
    pT = place("pT", [P, 2, TOK], F32, r_xt + 11520)
    xwin = place("xwin", [P, KD, WIN], F32, r_xt)
    ysb = place("ysb", [P, 2, D // 2], F32, r_xt + 4096)
    hid = place("hid", [P, 4, WIN], F32, r_xt + 12288)
    sgl = place("sgl", [P, F], F32, r_xt + 13312)

    at = r_const
    ident = place("ident", [P, P], F32, at)
    ones = place("ones", [P, P], F32, at + 512)
    vT = place("vT", [P, NV], F32, at + 1024)
    T = place("T", [P, 4, TOK], F32, at + 2944)
    pconv = place("pconv", [P, TC, NB], F32, at + 2944)
    sqp = place("sqp", [P, 3, 4], F32, r_const + 10560)
    g2n = place("g2n", [P, KD], F32, r_const + 10496)
    zeros = place("zeros", [P, 512], F32, at + 3200)
    sq = place("sq", [P, 2, TOK], F32, at + 7168)
    plru = place("plru", [P, TC, NB], F32, at + 7168)
    sg = place("sg", [P, TOK], F32, at + 9280)
    g2 = place("g2", [P, KD], F32, at + 10336)
    negc = place("negc", [P, TC], F32, at + 10400)
    ssum = place("ssum", [P, 4], F32, at + 10432)
    rstd = place("rstd", [P, 4], F32, at + 10464)
    spt = place("spt", [P, 3, TC], F32, r_xs + 18432)
    sgb = place("sgb", [P, TOK], F32, r_xs + 22976)
    gate_buf = [sg, sgb]

    ra = at + 2944
    rsz = [0]

    def rt(name, shape, dt=F32):
        n = 4
        for s in shape[1:]:
            n *= s
        x = place(name, shape, dt, ra + rsz[0])
        rsz[0] += (n + 31) // 32 * 32
        assert rsz[0] <= 7392
        return x

    offs = rt("offs", [1, 64], I32)
    wts = rt("wts", [P, 2, 3])
    rowix = rt("rowix", [P, 2, 3], I32)
    logit = rt("logit", [P, 3, NG + E])
    gl = rt("gl", [P, 3, 8])
    gmx = rt("gmx", [P, 3, 8])
    gix = rt("gix", [P, 3, 8], U32)
    gf = rt("gf", [P, 3])
    gex = rt("gex", [P, 3, NG])
    gw = rt("gw", [P, 3])
    oh4 = rt("oh4", [P, 3, NG])
    el = rt("el", [P, 3, NG, EG])
    ein = rt("ein", [P, 3, EG])
    emx = rt("emx", [P, 3, 8])
    eix = rt("eix", [P, 3, 8], U32)
    ef = rt("ef", [P, 3, 2])
    ex = rt("ex", [P, 3])
    oh = rt("oh", [P, 2, 3, E])
    asg = rt("asg", [P, 3, E])
    rank = rt("rank", [P, 3, E])
    cnt = rt("cnt", [P, E])
    off = rt("off", [P, E])
    pos = rt("pos", [P, 2, 3])
    rnk = rt("rnk", [P, 2, 3])
    tri = rt("tri", [P, P])
    i32r = rt("i32r", [P, E])
    prod = rt("prod", [P, 3, E])
    over = rt("over", [P, E, 4])
    oidx = rt("oidx", [P, E, 4])
    osel = rt("osel", [P, E, 4])
    opr = rt("opr", [P, E, 4])
    win64 = rt("win64", [P, 4])
    pidx = rt("pidx", [P, 1])
    otab = rt("otab", [P, 2])
    otabi = rt("otabi", [P, 2], I32)

    ps = nc.alloc_psum_tensor("ps", [P, 8, 512], F32)

    y_dram = nc.dram_tensor("y_sorted", (2 * XW, D), F32, kind="Internal").ap()
    ov_dram = nc.dram_tensor("over_table", (MAX_OVER, 2), I32, kind="Internal").ap()

    slot_loaded = [sem(f"slot_loaded{i}") for i in range(NS)]
    chunk_used = sem("chunk_used")
    x_loaded = [sem(f"x_loaded{c}") for c in range(3)]
    late_rows = sem("late_rows")
    rows_loaded = sem("rows_loaded")
    gates_loaded = sem("gates_loaded")
    router_loaded = sem("router_loaded")
    p_loaded = sem("p_loaded")
    fing_loaded = sem("fing_loaded")
    consts_ready = sem("consts_ready")
    iotas_ready = sem("iotas_ready")
    act_order = sem("act_order")
    dve_order = sem("dve_order")
    zeros_ready = sem("zeros_ready")
    ms_ready = sem("ms_ready")
    root_ready = sem("root_ready")
    dg_ready = sem("dg_ready")
    vec_turned = sem("vec_turned")
    vec_ready = sem("vec_ready")
    x_turned = sem("x_turned")
    xT_dve = sem("xT_dve")
    xT_act = sem("xT_act")
    state_turned = sem("state_turned")
    state_used = sem("state_used")
    acc_full = sem("acc_full")
    acc_free = sem("acc_free")
    sig_ready = sem("sig_ready")
    u_ready = sem("u_ready")
    conv_done = sem("conv_done")
    lconv_done = sem("lconv_done")
    gates_full = sem("gates_full")
    gates_taken = sem("gates_taken")
    i_ready = sem("i_ready")
    i_used = sem("i_used")
    tanh_ready = sem("tanh_ready")
    z_ready = sem("z_ready")
    beta_ready = sem("beta_ready")
    scan_done = sem("scan_done")
    gelu_ready = sem("gelu_ready")
    mixr_ready = sem("mixr_ready")
    mean_full = sem("mean_full")
    centred = sem("centred")
    sq_ready = sem("sq_ready")
    sq_used = sem("sq_used")
    var_full = sem("var_full")
    var_ready = sem("var_ready")
    sd_ready = sem("sd_ready")
    scaled = sem("scaled")
    mixc_ready = sem("mixc_ready")
    hT_ready = sem("hT_ready")
    h_turned = sem("h_turned")
    h_added = sem("h_added")
    tail_turned = sem("tail_turned")
    tail_taken = sem("tail_taken")
    state_out = sem("state_out")
    ssq_act = sem("ssq_act")
    ssum_set = sem("ssum_set")
    r_turned = sem("r_turned")
    rx_ready = sem("rx_ready")
    logits_full = sem("logits_full")
    softmax_in = sem("softmax_in")
    softmax_out = sem("softmax_out")
    assigned = sem("assigned")
    ranks_full = sem("ranks_full")
    table_ready = sem("table_ready")
    table_out = sem("table_out")
    hot_ready = sem("hot_ready")
    onehot_ready = sem("onehot_ready")
    sort_full = sem("sort_full")
    sort_dve = sem("sort_dve")
    sort_act = sem("sort_act")
    pad_ready = sem("pad_ready")
    p_turned = sem("p_turned")
    pT_ready = sem("pT_ready")
    y_out = sem("y_out")
    expert_steps = ("window", "products", "silu", "gated", "turned", "hid", "down", "evac")
    main = {n: sem(f"main_{n}") for n in expert_steps}
    extra = {n: sem(f"extra_{n}") for n in expert_steps}
    over_loaded = sem("over_loaded")
    over_out = sem("over_out")
    over_free = sem("over_free")
    rows_back = [sem(f"rows_back{c}") for c in range(3)]
    h2_ready = sem("h2_ready")
    pg_ready = sem("pg_ready")
    prod_ready = sem("prod_ready")
    y_ready = sem("y_ready")
    y_act = sem("y_act")
    out_done = sem("out_done")

    block = nc.Block()
    block.__enter__()

    def chunk_view(n):
        if n < CH_IN:
            c0 = GROUP_COL[n // 4]
            if n < CH_IN // 2:
                v = a["w_in"].rearrange("l (k p) (h c) -> h p (l k) c", p=P, h=4)
                return v[:, :, 4 * (n % 4):4 * (n % 4) + 4, c0:c0 + 256], 256
            v = a["w_in"].rearrange("l (k p) c -> p (l k) c", p=P)
            return v[:, 4 * (n % 4):4 * (n % 4) + 4, c0:c0 + 512], 512
        if n < CH_IN + CH_OUT:
            m = n - CH_IN
            v = a["w_out"].rearrange("l (k p) c -> p (l k) c", p=P)
            return v[:, 4 * (m % 4):4 * (m % 4) + 4, 512 * (m // 4):512 * (m // 4) + 512], 512
        if n < CH_FRONT:
            v = a["w_ple"].rearrange("l (k p) c -> p (l k) c", p=P)
            return v[:, n - CH_FRONT + 2:n - CH_FRONT + 3, :], D
        m = n - CH_PG0
        v = a["w_pg"].rearrange("l (k p) c -> p (l k) c", p=P)
        return v[:, 4 * (m % 4):4 * (m % 4) + 4, 512 * (m // 4):512 * (m // 4) + 512], 512

    def freed(n):
        return n + 1 if n < CT_OUT else n + 1 - KD

    def used(n):
        if n < CH_IN + CH_OUT:
            if n % 4 == 3:
                return acc_full, n + 1
            return chunk_used, 3 * (n // 4) + n % 4 + 1
        if n < CH_FRONT:
            return acc_full, CT_PG
        m = n - CH_PG0
        if m % 4 == 3:
            return acc_full, CT_PG + m + 1
        return chunk_used, 3 * (CH_IN + CH_OUT) // 4 + 6 * E + 3 * (m // 4) + m % 4 + 1

    def used_expert(e, j):
        if j in (6, 7):
            return main["products"], e + 1
        if j == CH_EXP - 1:
            return main["down"], e + 1
        part = j // 2 if j < 8 else j - 5
        return chunk_used, e * 6 + (3 * (CH_IN + CH_OUT) // 4 + part + 1)

    def gate_tail(m):
        return sq[:, m % 2, :]

    def slot(n):
        return n % NS

    def slot_count(n):
        return 16 * sum(2 if m < CH_IN // 2 else 1 for m in range(slot(n), n + 1, NS))

    gate_v = a["w_gate"].rearrange("l e (p k) f -> p (l e) (k f)", k=KD)
    up_v = a["w_up"].rearrange("l e (p k) f -> p (l e) (k f)", k=KD)

    def down_view(e, t):
        return a["w_down"].rearrange("l e (t p) d -> t p (l e) d", p=P)[t, :, bass.ds(e, 1), :]

    def expert_view(e, j):
        if j < 8:
            return (gate_v, up_v)[j % 2][:, bass.ds(e, 1), j // 2 * D:(j // 2 + 1) * D]
        return down_view(e, j - 8)

    @block.sync
    def _(sp):
        def load(n):
            src, w = chunk_view(n)
            if n >= CH_PG0 and n - NS < CH_PG0:
                sp.wait_ge(*used_expert(E - 1, n - CH_PG0))
            elif n >= NS:
                sp.wait_ge(*used(n - NS))
            if w == 256:
                dst = ring[:, slot(n), :].rearrange("p (k h c) -> p k h c", c=w, h=2)
                for half in range(2):
                    sp.dma_start(dst[:, :, half, :], src[half]).then_inc(slot_loaded[slot(n)], 16)
            else:
                dst = ring[:, slot(n), :].rearrange("p (k c) -> p k c", c=w)
                sp.dma_start(dst, src).then_inc(slot_loaded[slot(n)], 16)

        sp.dma_start(h[:, 1, :], a["x_prompt"][0, P:2 * P, :]).then_inc(x_loaded[1], 16)
        sp.dma_start(h[0:NB, 2, :], a["x_sample"][:, 0, :]).then_inc(x_loaded[2], 16)
        sp.dma_start(h[:, 0, :], a["x_prompt"][0, 0:P, :]).then_inc(x_loaded[0], 16)
        for n, (dst, src) in enumerate(row_loads(a, vrow, stage, lstage, g2)):
            if n == N_ROWS:
                for m in range(4):
                    load(m)
            sp.dma_start(dst, src).then_inc(rows_loaded if n < N_ROWS else late_rows, 16)
        for n in range(4, CH_FRONT):
            load(n)
        for j in range(CH_EXP):
            s = slot(CH_FRONT + j)
            sp.wait_ge(*used(CH_FRONT + j - NS))
            sp.dma_start(ring[:, s:s + 1, :], expert_view(0, j)).then_inc(slot_loaded[s], 16)
        with sp.Fori(1, E) as e:
            for j in range(CH_EXP):
                sp.wait_ge(*used_expert(e - 1, j))
                s = slot(CH_FRONT + j)
                sp.dma_start(ring[:, s:s + 1, :], expert_view(e, j)).then_inc(slot_loaded[s], 16)
        sp.wait_ge(table_out, 16)
        n_over = sp.value_load(offs[0:1, 40:41], min_val=0, max_val=MAX_OVER)
        with sp.If(n_over > 0):
            sp.wait_ge(main["down"], E)
            with sp.Fori(0, n_over) as i:
                e = sp.value_load(ov_dram[bass.ds(i, 1), 0:1], min_val=0, max_val=E - 1)
                sp.wait_ge(over_free, i + 1)
                for j in range(CH_EXP):
                    sp.dma_start(ring[:, j:j + 1, :], expert_view(e, j)).then_inc(over_loaded, 16)
        for c in range(3):
            sp.wait_ge(rows_back[c], 32)
        for n in range(CH_PG0, CH_PG0 + CH_OUT):
            load(n)
        for c in (2, 0):
            sp.wait_ge(y_ready, 1 if c == 2 else 2)
            dst = o["y_prompt"][0, c * P:(c + 1) * P, :] if c < 2 else o["y_sample"][:, 0, :]
            sp.dma_start(dst, hg[0:ROWS[c], c, :]).then_inc(out_done, 16)
        sp.wait_ge(out_done, 48)

    @block.gpsimd
    def _(pool):
        pool.memset(ident[:, :], 0.0).then_inc(consts_ready, 1)
        pool.memset(ones[:, :], 1.0).then_inc(consts_ready, 1)
        pool.memset(U[:, :, 0:CK - 1], 0.0).then_inc(consts_ready, 1)
        pool.memset(L[:, :, 0:LK - 1], 0.0).then_inc(consts_ready, 1)
        pool.memset(zeros[:, :], 0.0).then_inc(zeros_ready, 1)
        pool.wait_ge(consts_ready, 4)
        pool.affine_select(out=ident[:, :], in_=ident[:, :], compare_op=ALU.not_equal, fill=1.0,
                           base=0, pattern=[[-1, P]], channel_multiplier=1).then_inc(consts_ready, 1)
        pool.dma_start(o["conf_sample"][0, :, 0:CK - 2, :], a["state_conf_conv"][0, :, 1:CK - 1, :])\
            .then_inc(state_out, 16)
        pool.dma_start(o["lru_sample"][0, :, 0:LK - 2, :], a["state_lru_conv"][0, :, 1:LK - 1, :])\
            .then_inc(state_out, 16)
        pool.wait_ge(acc_full, 8)
        pool.wait_ge(zeros_ready, 1)
        for x in range(2):
            pool.dma_start(y_dram[2 * XW - FILL + x * FILL // 2:2 * XW - FILL + (x + 1) * FILL // 2, :]
                          .rearrange("(p r) (a b) -> p (r a) b", p=P, b=512),
                          zeros[:, :].unsqueeze(1).broadcast_to([P, FILL // P * 2, 512])).then_inc(y_out, 16)

        pool.wait_ge(tail_taken, 1)
        pool.dma_start(o["conf_prompt"][0, 0, :, :], sc_out[0:CK - 1, :]).then_inc(state_out, 16)
        pool.dma_start(o["conf_sample"][0, :, CK - 2, :], sc_out[CK - 1:CK - 1 + NB, :]).then_inc(state_out, 16)
        pool.wait_ge(tail_taken, 2)
        pool.dma_start(o["lru_prompt"][0, 0, :, :], sl_out[0:LK - 1, :]).then_inc(state_out, 16)
        pool.dma_start(o["lru_sample"][0, :, LK - 2, :], sl_out[LK - 1:LK - 1 + NB, :]).then_inc(state_out, 16)
        pool.wait_ge(tail_taken, 3)
        pool.dma_start(o["h_prompt"][0, :, :], sh_out[0:1, :]).then_inc(state_out, 16)
        pool.dma_start(o["h_sample"][0, :, :], sh_out[1:1 + NB, :]).then_inc(state_out, 16)
        pool.memset(tri[:, :], 1.0).then_inc(iotas_ready, 1)
        pool.wait_ge(iotas_ready, 1)
        pool.affine_select(out=tri[:, :], in_=tri[:, :], compare_op=ALU.is_gt, fill=0.0, base=0,
                           pattern=[[1, P]], channel_multiplier=-1).then_inc(iotas_ready, 1)
        pool.iota(i32r[:, :], [[1, E]], base=0, channel_multiplier=0,
                  allow_small_or_imprecise_dtypes=True).then_inc(iotas_ready, 1)
        pool.iota(win64[:, :], [[WIN, 4]], base=WIN, channel_multiplier=0,
                  allow_small_or_imprecise_dtypes=True).then_inc(iotas_ready, 1)
        pool.iota(pidx[:, :], [[0, 1]], base=0, channel_multiplier=1,
                  allow_small_or_imprecise_dtypes=True).then_inc(iotas_ready, 1)
        pool.wait_ge(acc_full, CT_OUT)
        pool.iota(iota[:, :], [[1, NSLOT]], base=0, channel_multiplier=0,
                  allow_small_or_imprecise_dtypes=True).then_inc(iotas_ready, 1)
        pool.dma_start(prow[:, 0:2, :], a["p_prompt"][0, 0].rearrange("(c p) d -> p c d", p=P)).then_inc(p_loaded, 16)
        pool.dma_start(prow[0:NB, 2, :], a["p_sample"][0, :, 0, :]).then_inc(p_loaded, 16)
        pool.wait_ge(table_ready, 1)
        pool.dma_start(ov_dram[:, :], otabi[0:MAX_OVER, :]).then_inc(table_out, 16)

        def rows_of(row):
            return y_dram[bass.ds(row, WIN), :].rearrange("r (h c) -> h r c", h=2)

        with pool.Fori(0, E, 2) as e2:
            for par in range(2):
                start = pool.value_load(offs[0:1, bass.ds(e2 + par, 1)], min_val=0, max_val=NSLOT)
                pool.wait_ge(main["evac"], 2 * (e2 + par) + 2)
                pool.wait_ge(y_out, 16 * (e2 + par + 2))
                pool.dma_start(rows_of(start), ysb[:, par, :]).then_inc(y_out, 16)
        pool.wait_ge(table_out, 16)
        n_over = pool.value_load(offs[0:1, 40:41], min_val=0, max_val=MAX_OVER)
        pool.wait_ge(y_out, 16 * (E + 2))
        with pool.If(n_over > 0):
            pool.sem_inc(over_free, 1)
            with pool.Fori(0, n_over) as i:
                start = pool.value_load(ov_dram[bass.ds(i, 1), 1:2], min_val=0, max_val=NSLOT)
                pool.wait_ge(extra["evac"], 2 * i + 2)
                pool.dma_start(rows_of(start + XW), ysb[:, 0, :]).then_inc(over_out, 16)
                pool.wait_ge(over_out, 16 * (i + 1))
                pool.sem_inc(over_free, 1)
        pool.wait_ge(main["window"], E + 1)
        for c in (2, 0, 1):
            r = ROWS[c]
            for q, g in ((0, g0), (1, g1)):
                pool.indirect_dma_start(g[0:r, c, :], None, y_dram[:, :],
                                        bass.IndirectOffsetOnAxis(ap=rowix[0:r, q, c:c + 1], axis=0))\
                    .then_inc(rows_back[c], 16)
        pool.wait_ge(state_out, 16 * 8)

    @block.tensor
    def _(pe):
        def turn(out, src, r):
            if r == P:
                return pe.transpose(out, src, ident[:, :])
            return pe.matmul(out, src, ident[:, :], start=True, stop=True)

        def dense(n, chunk0, rhs, kt, wait_k=None):
            if CT_OUT <= n - 3 < CT_PLE:
                pe.wait_ge(hT_ready, n - 3 - CT_OUT + 1)
            elif n >= 3:
                pe.wait_ge(acc_free, freed(n - 3))
            for k in range(kt):
                if kt == KD:
                    ch, kk = chunk0 + k // 4, k % 4
                    w = ring[:, slot(ch), kk * 512 + (n % 4) * P:kk * 512 + (n % 4) * P + P]
                    first, done = n % 4 == 0 and kk == 0, n % 4 == 3 and kk == 3
                else:
                    ch = chunk0 + k
                    w = ring[:, slot(ch), (n - CT_PLE) * P:(n - CT_PLE + 1) * P]
                    first, done = n == CT_PLE, False
                if first:
                    pe.wait_ge(slot_loaded[slot(ch)], slot_count(ch))
                if wait_k:
                    wait_k(k)
                mm = pe.matmul(ps[:, n % 3, 0:TOK], w, rhs[:, k, :], start=(k == 0), stop=(k == kt - 1))
                if done and k < kt - 1:
                    mm.then_inc(chunk_used, 1)
            mm.then_inc(acc_full, 1)

        pe.wait_ge(consts_ready, 5)
        pe.wait_ge(rows_loaded, 16 * N_ROWS)
        widths = [P, 120, 104, P, 16]
        c0 = 0
        for b in range(5):
            w = widths[b]
            last = pe.transpose(ps[:, 7, c0:c0 + w], vrow[0:w, b, :], ident[0:w, 0:w])
            c0 += w
        last.then_inc(vec_turned, 1)

        def turn_states(first):
            if first == 0:
                pe.wait_ge(late_rows, 32)
            for j in range(first, first + 4):
                if j >= 4:
                    pe.wait_ge(state_used, j - 3)
                b = 3 + j % 4
                pe.transpose(ps[:, b, 0:120], stage[0:120, 0, j * P:(j + 1) * P], ident[0:120, 0:120])
                pe.transpose(ps[:, b, 120:240], stage[0:120, 1, j * P:(j + 1) * P], ident[0:120, 0:120])\
                    .then_inc(state_turned, 1)

        def turn_lru_states():
            pe.wait_ge(vec_ready, 1)
            for j in range(TC):
                last = pe.transpose(ps[:, 7, j * 24:(j + 1) * 24], lstage[0:24, j * P:(j + 1) * P], ident[0:24, 0:24])
            last.then_inc(state_turned, 1)

        def turn_x(base, src, ready):
            pe.wait_ge(dg_ready, ready)
            for k in range(KD):
                if k >= 4:
                    if k % 2 == 0:
                        pe.wait_ge(xT_dve, base + k // 2 - 1)
                    else:
                        pe.wait_ge(xT_act, base + k // 2 - 1)
                for c in range(3):
                    r = ROWS[c]
                    last = pe.matmul(ps[:, 3 + k % 4, c * P:c * P + r], src(c, k), dg[0:r, c, 0:r], start=True, stop=True)
                last.then_inc(x_turned, 1)

        turn_x(0, lambda c, k: h[0:ROWS[c], c, k * P:(k + 1) * P], 3)

        def lru_gates(j):
            if j == 0:
                pe.wait_ge(gates_loaded, 32)
            pe.wait_ge(lconv_done, j + 1)
            if j >= 1:
                pe.wait_ge(gates_taken, j)
            pe.matmul(ps[:, 3, 0:TOK], wa[:, j, :], lxc[:, j, :], start=True, stop=True)
            pe.matmul(ps[:, 4, 0:TOK], wx[:, j, :], lxc[:, j, :], start=True, stop=True).then_inc(gates_full, 1)

        def mean():
            pe.wait_ge(conv_done, TC)
            for j in range(TC):
                mm = pe.matmul(ps[:, 6, 0:TOK], ones[:, :], mix[:, j, :], start=(j == 0), stop=(j == TC - 1))
            mm.then_inc(mean_full, 1)

        def var(p):
            pe.wait_ge(sq_ready, 2 * p + 2)
            for j in range(2 * p, 2 * p + 2):
                mm = pe.matmul(ps[:, 7, 0:TOK], ones[:, :], sq[:, j % 2, :], start=(j == 0), stop=(j == TC - 1))
            mm.then_inc(sq_used, 1)

        def wait_xT(k):
            if k % 2 == 0:
                pe.wait_ge(xT_dve, k // 2 + 1)
            else:
                pe.wait_ge(xT_act, k // 2 + 1)

        for n in range(CT_OUT):
            dense(n, 4 * (n // 4), xT, KD, wait_xT if n == 0 else None)
            if n < 2:
                turn_states(4 * n)
            if n == 1:
                turn_lru_states()
            if 20 <= n < 28:
                lru_gates(n - 20)
            if n == 23:
                mean()
            if 26 <= n < 30:
                var(n - 26)

        def wait_mix(k):
            if k < TC:
                pe.wait_ge(mixc_ready, k + 1)
            else:
                pe.wait_ge(mixr_ready, k - TC + 1)

        def turn_back(m, base_free):
            pe.wait_ge(hT_ready, m + 1)
            if m >= 2:
                pe.wait_ge(h_added, m - 1)
            for c in range(3):
                r = ROWS[c]
                last = turn(ps[0:r, 3 + m % 2, c * P:(c + 1) * P], hT_tile(m)[:, c * P:c * P + r], r)
            last.then_inc(h_turned, 1)

        def hT_tile(m):
            return hT[:, m % 2, :]

        def turn_tails(which):
            if which:
                pe.wait_ge(tail_taken, which)
            pe.wait_ge(rx_ready, 2 * which + 1)
            for j in range(TC):
                src, r = [(U[:, j, SEQ:UW], CK - 1 + NB), (L[:, j, SEQ:LW], LK - 1 + NB), (htail[:, j, :], 1 + NB)][which]
                last = turn(ps[0:r, 5 + j // 4, (j % 4) * P:(j % 4 + 1) * P], src, r)
            last.then_inc(tail_turned, 1)

        def turn_router(m):
            pe.wait_ge(h_added, m + 1)
            if m:
                pe.wait_ge(rx_ready, m)
            if m in (1, 3, 5):
                pe.wait_ge(tail_taken, m // 2 + 1)
            for c in range(3):
                r = ROWS[c]
                last = pe.transpose(ps[:, 6, c * P:c * P + r], h[0:r, c, m * P:(m + 1) * P], ident[0:r, 0:r])
            last.then_inc(r_turned, 1)

        def logits(m):
            if m == 0:
                pe.wait_ge(router_loaded, 16 * 4)
            pe.wait_ge(rx_ready, m + 1)
            for c in range(3):
                r = ROWS[c]
                mm = pe.matmul(ps[0:r, 7, c * 64:c * 64 + NG + E], rxT[:, m % 3, c * P:c * P + r], wr[:, m, :],
                               start=(m == 0 and c == 0), stop=(m == KD - 1), skip_group_check=True)
            if m == KD - 1:
                mm.then_inc(logits_full, 1)

        for n in range(CT_OUT, CT_PLE):
            m = n - CT_OUT
            dense(n, CH_IN + 4 * (m // 4), mix, KD, wait_mix if m == 0 else None)
            if m >= 1:
                turn_back(m - 1, 0)
            if m >= 3:
                logits(m - 3)
            if m >= 2:
                turn_router(m - 2)
            if m in (2, 4, 6):
                turn_tails(m // 2 - 1)
            if m in (8, 9):
                k = m - 8
                if k == 0:
                    pe.wait_ge(p_loaded, 32)
                    pe.wait_ge(tail_taken, 3)
                else:
                    pe.wait_ge(pT_ready, 1)
                for c in range(3):
                    r = ROWS[c]
                    last = pe.transpose(ps[:, 5, c * P:c * P + r], prow[0:r, c, k * P:(k + 1) * P], ident[0:r, 0:r])
                last.then_inc(p_turned, 1)
        turn_back(KD - 1, 0)
        logits(KD - 3)
        turn_router(KD - 2)
        logits(KD - 2)
        turn_router(KD - 1)
        logits(KD - 1)
        pe.wait_ge(pT_ready, 2)
        for n in range(CT_PLE, CT_PLE + 12):
            dense(n, CH_IN + CH_OUT, pT, 2)
        pe.wait_ge(assigned, 1)
        pe.wait_ge(iotas_ready, 5)
        for c in range(3):
            r = ROWS[c]
            for cc in range(c + 1):
                rr = ROWS[cc]
                pe.matmul(ps[0:r, 6, c * 64:c * 64 + E], ones[0:rr, 0:r] if cc < c else tri[0:r, 0:r],
                          asg[0:rr, cc, :], start=(cc == 0), stop=(cc == c))
        for c in range(3):
            mm = pe.matmul(ps[:, 6, 192:192 + E], ones[0:ROWS[c], :], asg[0:ROWS[c], c, :],
                           start=(c == 0), stop=(c == 2))
        mm.then_inc(ranks_full, 1)
        for n in range(CT_PLE + 12, CT_PG):
            dense(n, CH_IN + CH_OUT, pT, 2)
        pe.wait_ge(onehot_ready, 3)
        m = 0
        for half in range(2):
            for k in range(KD):
                if m >= 2:
                    pe.wait_ge(sort_dve if m % 2 == 0 else sort_act, m // 2)
                for c in range(3):
                    r = ROWS[c]
                    mm = pe.matmul(ps[:, 4 + m % 2, 0:HALF], h[0:r, c, k:D:KD],
                                   onehot[0:r, c, half * HALF:(half + 1) * HALF], start=(c == 0), stop=(c == 2))
                mm.then_inc(sort_full, 1)
                m += 1
        pe.wait_ge(acc_free, freed(CT_PG - 1))

        def expert(i, sems, slots, loaded, release_chunks):
            pe.wait_ge(sems["window"], i + 1)
            for j in range(4):
                loaded(2 * j)
                loaded(2 * j + 1)
                for kk in range(4):
                    k = 4 * j + kk
                    for part in range(2):
                        mm = pe.matmul(ps[part * WIN:(part + 1) * WIN, 0, :], xwin[:, k, :],
                                       ring[:, slots[2 * j + part], kk * F:(kk + 1) * F],
                                       start=(k == 0), stop=(k == KD - 1))
                if j < 3 and release_chunks:
                    mm.then_inc(chunk_used, 1)
            mm.then_inc(sems["products"], 1)
            pe.wait_ge(sems["gated"], i + 1)
            for t in range(4):
                mm = pe.matmul(ps[:, 1, t * WIN:(t + 1) * WIN], sgl[WIN:2 * WIN, t * P:(t + 1) * P],
                               ident[WIN:2 * WIN, WIN:2 * WIN], start=True, stop=True)
            mm.then_inc(sems["turned"], 1)
            pe.wait_ge(sems["hid"], i + 1)
            for t in range(4):
                loaded(8 + t)
                for b in range(2):
                    for half in range(2):
                        q = 2 * half + b
                        mm = pe.matmul(ps[half * WIN:(half + 1) * WIN, 2 + b, :], hid[:, t, :],
                                       ring[:, slots[8 + t], q * 512:(q + 1) * 512], start=(t == 0), stop=(t == 3))
                if t < 3 and release_chunks:
                    mm.then_inc(chunk_used, 1)
            mm.then_inc(sems["down"], 1)

        main_slots = [slot(CH_FRONT + j) for j in range(CH_EXP)]
        with pe.Fori(0, E) as e:
            def main_loaded(j):
                pe.wait_ge(slot_loaded[main_slots[j]], e * 16 + slot_count(CH_FRONT + j))

            expert(e, main, main_slots, main_loaded, True)
        pe.wait_ge(table_out, 16)
        n_over = pe.value_load(offs[0:1, 40:41], min_val=0, max_val=MAX_OVER)
        with pe.If(n_over > 0):
            with pe.Fori(0, n_over) as i:
                def over_wait(j):
                    if j == 0:
                        pe.wait_ge(over_loaded, 16 * CH_EXP * (i + 1))

                expert(i, extra, list(range(CH_EXP)), over_wait, False)

        turn_x(8, lambda c, k: h[0:ROWS[c], c, k * P:(k + 1) * P], 6)

        def wait_xT3(k):
            if k % 2 == 0:
                pe.wait_ge(xT_dve, 8 + k // 2 + 1)
            else:
                pe.wait_ge(xT_act, 8 + k // 2 + 1)

        def turn_prod(m):
            pe.wait_ge(prod_ready, m + 1)
            if m >= 2:
                pe.wait_ge(h_added, KD + m - 1)
            for c in range(3):
                r = ROWS[c]
                last = turn(ps[0:r, 3 + m % 2, c * P:(c + 1) * P], pleT[:, m, c * P:c * P + r], r)
            last.then_inc(h_turned, 1)

        for n in range(CT_PG, CT_PG + KD):
            dense(n, CH_PG0 + 4 * ((n - CT_PG) // 4), xT, KD, wait_xT3 if n == CT_PG else None)
            if n > CT_PG:
                turn_prod(n - CT_PG - 1)
        turn_prod(KD - 1)

    @block.scalar
    def _(act):
        order = [0]

        def step(ins):
            order[0] += 1
            ins.then_inc(act_order, 1)

        def link(ins):
            step(ins)
            act.wait_ge(act_order, order[0])

        sums = [0]

        def squares(dst, src, out):
            if sums[0]:
                act.wait_ge(ssq_act, sums[0])
            sums[0] += 1
            act.activation(dst, src, ACT.Square, accum_out=out).then_inc(ssq_act, 1)

        act.wait_ge(ssum_set, 1)
        for c in (1, 2):
            r = ROWS[c]
            act.wait_ge(x_loaded[c], 16)
            squares(xdump[0:r, 1, :], h[0:r, c, :], ssum[0:r, c:c + 1])
        act.wait_ge(ms_ready, 1)
        act.activation(ssum[:, 0:3], ssum[:, 0:3], ACT.Sqrt).then_inc(root_ready, 1)
        act.wait_ge(consts_ready, 5)
        act.wait_ge(vec_ready, 1)
        lam = vT[:, V_LAM:V_LAM + TC]
        link(act.activation(spt[:, 0, :], lam, ACT.Abs))
        link(act.activation(spt[:, 0, :], spt[:, 0, :], ACT.Exp, scale=-1.0))
        step(act.activation(spt[:, 1, :], spt[:, 0, :], ACT.Ln, bias=ones[:, 0:1]))

        def take_xT(base, gain):
            for k in range(1, KD, 2):
                act.wait_ge(x_turned, 2 * base + k + 1)
                act.activation(xT[:, k, :], ps[:, 3 + k % 4, 0:TOK], ACT.Copy, scale=gain(k)).then_inc(xT_act, 1)

        take_xT(0, lambda k: vT[:, V_N1 + k:V_N1 + k + 1])
        act.wait_ge(x_turned, KD)
        act.dma_start(wa[:, :, :], a["lru_wa"][0].rearrange("h i j -> i h j")).then_inc(gates_loaded, 16)
        act.dma_start(wx[:, :, :], a["lru_wx"][0].rearrange("h i j -> i h j")).then_inc(gates_loaded, 16)
        act.dma_start(wr[:, :, 0:NG], a["w_grp"][0].rearrange("(k p) n -> p k n", k=KD)).then_inc(router_loaded, 16)
        act.dma_start(wr[:, :, NG:], a["w_rt"][0].rearrange("(k p) n -> p k n", k=KD)).then_inc(router_loaded, 16)
        act.dma_start(br[:, 0:NG], a["b_grp"][0].partition_broadcast(P)).then_inc(router_loaded, 16)
        act.dma_start(br[:, NG:], a["b_rt"][0].partition_broadcast(P)).then_inc(router_loaded, 16)

        def quarter_squares(q, base, dump):
            act.wait_ge(h_added, base + 4 * q + 4)
            for c in range(3):
                r = ROWS[c]
                squares(dump[0:r, :], h[0:r, c, 512 * q:512 * (q + 1)], sqp[0:r, c, q:q + 1])

        def gates(j):
            act.wait_ge(gates_full, j + 1)
            if j >= 4:
                act.wait_ge(scan_done, 1)
            act.activation(R[:, j % 4, :], ps[:, 3, 0:TOK], ACT.Sigmoid, bias=vT[:, V_BA + j:V_BA + j + 1])
            if j >= 2:
                act.wait_ge(i_used, j - 1)
            act.activation(I[:, j % 2, :], ps[:, 4, 0:TOK], ACT.Sigmoid, bias=vT[:, V_BX + j:V_BX + j + 1])\
                .then_inc(gates_taken, 1)

        def decays(b):
            act.wait_ge(gates_taken, 4 * b + 4)
            act.wait_ge(vec_ready, 2)
            if b:
                act.wait_ge(scan_done, 1)
            else:
                act.wait_ge(y_out, 32)
            for j in range(4):
                act.activation(T[:, j, :], R[:, j, :], ACT.Tanh, scale=negc[:, 4 * b + j:4 * b + j + 1])
            for j in range(4):
                last = act.activation(R[:, j, :], R[:, j, :], ACT.Exp, scale=negc[:, 4 * b + j:4 * b + j + 1])
            last.then_inc(tanh_ready, 1)
            act.wait_ge(z_ready, b + 1)
            act.activation(T[:, :, :], T[:, :, :], ACT.Sqrt, scale=-1.0).then_inc(beta_ready, 1)

        for n in range(CT_OUT):
            g, i = n // 4, n % 4
            col = V_BIN + GROUP_COL[g] // P + (i if g >= 4 else i % 2 + i // 2 * TC)
            bias = vT[:, col:col + 1]
            bank = ps[:, n % 3, 0:TOK]
            act.wait_ge(acc_full, n + 1)
            if g < 4 and i < 2:
                act.activation(U[:, 2 * g + i, CK - 1:], bank, ACT.Identity, bias=bias).then_inc(acc_free, 1)
            elif g < 4:
                t = 2 * g + i - 2
                if t >= 2:
                    act.wait_ge(u_ready, t - 1)
                act.activation(gate_buf[t % 2][:, :], bank, ACT.Sigmoid, bias=bias).then_inc(acc_free, 1)
            elif g in (4, 5):
                act.activation(L[:, n - 16, LK - 1:], bank, ACT.Identity, bias=bias).then_inc(acc_free, 1)
            else:
                t = n - 24
                if t >= 2:
                    act.wait_ge(mixr_ready, t - 1)
                act.activation(gate_buf[t % 2][:, :], bank, ACT.Gelu_apprx_tanh, bias=bias).then_inc(acc_free, 1)
            if 20 <= n < 28:
                gates(n - 20)
            if n == 23:
                decays(0)
            if n == 27:
                decays(1)
            if 25 <= n < 29:
                p = n - 25
                for j in range(2 * p, 2 * p + 2):
                    act.wait_ge(centred, j + 1)
                    if p:
                        act.wait_ge(sq_used, p)
                    act.activation(sq[:, j % 2, :], mix[:, j, :], ACT.Square).then_inc(sq_ready, 1)
            if n == 30:
                act.wait_ge(var_ready, 1)
                act.activation(I[:, 1, :], I[:, 0, :], ACT.Sqrt).then_inc(sd_ready, 1)
        for j in range(TC):
            act.wait_ge(scaled, j + 1)
            act.activation(mix[:, j, :], mix[:, j, :], ACT.Silu, scale=vT[:, V_LNG + j:V_LNG + j + 1],
                           bias=vT[:, V_LNB + j:V_LNB + j + 1]).then_inc(mixc_ready, 1)
        def take_router(m):
            act.wait_ge(r_turned, m + 1)
            act.activation(rxT[:, m % 3, :], ps[:, 6, 0:TOK], ACT.Copy, scale=g2n[:, m:m + 1]).then_inc(rx_ready, 1)

        for m in range(KD):
            n = CT_OUT + m
            act.wait_ge(acc_full, n + 1)
            if m >= 2:
                act.wait_ge(h_turned, m - 1)
            act.activation(hT[:, m % 2, :], ps[:, n % 3, 0:TOK], ACT.Copy).then_inc(hT_ready, 1)
            if m >= 2:
                take_router(m - 2)
            if m % 4 == 1 and m > 4:
                quarter_squares(m // 4 - 1, 0, sdump)
            if m in (9, 10):
                act.wait_ge(p_turned, m - 8)
                act.activation(pT[:, m - 9, :], ps[:, 5, 0:TOK], ACT.Copy).then_inc(pT_ready, 1)
        take_router(KD - 2)
        take_router(KD - 1)
        quarter_squares(3, 0, sdump)
        act.wait_ge(ms_ready, 2)
        act.activation(ssum[:, 0:3], ssum[:, 0:3], ACT.Sqrt).then_inc(root_ready, 1)
        act.wait_ge(state_out, 16 * 8)
        for m in range(KD):
            n = CT_PLE + m
            if m == 12:
                act.wait_ge(softmax_in, 1)
                act.activation(gex[:, :, :], gex[:, :, :], ACT.Exp)
                act.activation(ex[:, :], ex[:, :], ACT.Exp).then_inc(softmax_out, 1)
            act.wait_ge(acc_full, n + 1)
            act.activation(pleT[:, m, :], ps[:, n % 3, 0:TOK], ACT.Copy).then_inc(acc_free, 1)
        for c in range(3):
            r = ROWS[c]
            act.wait_ge(hot_ready, c + 1)
            act.activation(onehot[0:r, c, :], onehot[0:r, c, :], ACT.Copy, scale=rstd[0:r, c:c + 1]).then_inc(onehot_ready, 1)
        act.wait_ge(pad_ready, 1)
        for m in range(1, 2 * KD, 2):
            half, k = m // KD, m % KD
            act.wait_ge(sort_full, m + 1)
            act.activation(xsort[:, k, half * HALF:(half + 1) * HALF], ps[:, 5, 0:HALF], ACT.Copy,
                           scale=g2[:, k:k + 1]).then_inc(sort_act, 1)

        def expert(i, par, sems):
            act.wait_ge(sems["products"], i + 1)
            act.activation(sgl[WIN:2 * WIN, :], ps[0:WIN, 0, :], ACT.Silu).then_inc(sems["silu"], 1)
            act.wait_ge(sems["down"], i + 1)
            if sems is main:
                act.wait_ge(y_out, (i + 1) * 16)
            act.activation(ysb[:, par, 0:512], ps[:, 2, :], ACT.Copy).then_inc(sems["evac"], 1)

        act.wait_ge(table_ready, 1)
        with act.Fori(0, E, 2) as e2:
            for par in range(2):
                expert(e2 + par, par, main)
        act.wait_ge(table_out, 16)
        n_over = act.value_load(offs[0:1, 40:41], min_val=0, max_val=MAX_OVER)
        with act.If(n_over > 0):
            with act.Fori(0, n_over) as i:
                act.wait_ge(over_free, i + 1)
                expert(i, 0, extra)
        for n, c in enumerate((2, 0, 1)):
            r = ROWS[c]
            act.wait_ge(h2_ready, n + 1)
            squares(g0[0:r, c, :], h[0:r, c, :], ssum[0:r, c:c + 1])
        act.wait_ge(ms_ready, 3)
        act.activation(ssum[:, 0:3], ssum[:, 0:3], ACT.Sqrt).then_inc(root_ready, 1)
        act.dma_start(fing[:, :], a["final_g"].partition_broadcast(P)).then_inc(fing_loaded, 16)
        take_xT(8, lambda k: vT[:, V_PN + k:V_PN + k + 1])
        for m in range(KD):
            n = CT_PG + m
            act.wait_ge(acc_full, n + 1)
            if m >= 2:
                act.wait_ge(prod_ready, m - 1)
            act.activation(gate_tail(m), ps[:, n % 3, 0:TOK], ACT.Sigmoid,
                           bias=vT[:, V_BPG + m:V_BPG + m + 1]).then_inc(acc_free, 1)
            if m % 4 == 2 and m > 4:
                quarter_squares(m // 4 - 1, KD, sdump2)
        quarter_squares(3, KD, sdump2)
        act.wait_ge(ms_ready, 4)
        act.activation(ssum[:, 0:3], ssum[:, 0:3], ACT.Sqrt).then_inc(root_ready, 1)
        act.wait_ge(dg_ready, 7)
        act.activation(hg[:, 1, :], hg[:, 1, :], ACT.Copy, scale=rstd[:, 1:2]).then_inc(y_act, 1)
        act.wait_ge(y_act, 1)
        act.dma_start(o["y_prompt"][0, P:2 * P, :], hg[:, 1, :]).then_inc(out_done, 16)

    @block.vector
    def _(dve):
        order = [0]

        def step(ins):
            order[0] += 1
            ins.then_inc(dve_order, 1)
            return order[0]

        def link(ins):
            dve.wait_ge(dve_order, step(ins))

        def stt(out, in0, s, in1, op0, op1):
            return dve.scalar_tensor_tensor(out=out, in0=in0, scalar=s, in1=in1, op0=op0, op1=op1)

        def inverse_rms(n):
            dve.tensor_scalar(ssum[:, 0:3], ssum[:, 0:3], 1.0 / D, EPS, ALU.mult, ALU.add).then_inc(ms_ready, 1)
            dve.wait_ge(root_ready, n)
            return dve.reciprocal(rstd[:, 0:3], ssum[:, 0:3])

        def diagonals():
            for c in range(3):
                r = ROWS[c]
                dve.tensor_scalar(dg[0:r, c, 0:r], ident[0:r, 0:r], rstd[0:r, c:c + 1], None, ALU.mult)\
                    .then_inc(dg_ready, 1)

        dve.memset(ssum[:, :], 1.0).then_inc(ssum_set, 1)
        dve.wait_ge(ssum_set, 1)
        dve.wait_ge(x_loaded[0], 16)
        link(dve.tensor_tensor_reduce(xdump[:, 0, :], h[:, 0, :], h[:, 0, :], 1.0, 0.0, ALU.mult, ALU.add, ssum[:, 0:1]))
        dve.wait_ge(ssq_act, 2)
        link(inverse_rms(1))
        dve.wait_ge(consts_ready, 5)
        diagonals()
        dve.wait_ge(vec_turned, 1)
        dve.tensor_copy(g2n[:, :], ps[:, 7, NV:NV + KD])
        dve.tensor_copy(vT[:, :], ps[:, 7, 0:NV]).then_inc(vec_ready, 1)
        dve.wait_ge(vec_ready, 1)

        def take_xT(base, gain):
            for k in range(0, KD, 2):
                dve.wait_ge(x_turned, 2 * base + k + 1)
                dve.tensor_scalar(xT[:, k, :], ps[:, 3 + k % 4, 0:TOK], gain(k), None, ALU.mult).then_inc(xT_dve, 1)

        take_xT(0, lambda k: vT[:, V_N1 + k:V_N1 + k + 1])

        dve.wait_ge(act_order, 3)
        z, ln1, t = spt[:, 0, :], spt[:, 1, :], spt[:, 2, :]
        link(dve.tensor_scalar(t, z, 1.0, -1.0, ALU.add, ALU.add))
        link(dve.tensor_scalar(negc[:, :], t, 0.0, None, ALU.is_equal))
        link(dve.tensor_tensor(t, t, negc[:, :], ALU.add))
        link(dve.tensor_tensor(ln1, ln1, negc[:, :], ALU.add))
        link(dve.reciprocal(t, t))
        link(dve.tensor_tensor(ln1, ln1, t, ALU.mult))
        link(dve.tensor_tensor(ln1, ln1, z, ALU.mult))
        link(dve.tensor_scalar(t, vT[:, V_LAM:V_LAM + TC], -1.0, 0.0, ALU.mult, ALU.max))
        link(dve.tensor_tensor(t, t, ln1, ALU.add))
        dve.tensor_scalar(negc[:, :], t, -8.0, None, ALU.mult).then_inc(vec_ready, 1)
        link(dve.memset(sqp[:, :, :], 0.0))

        cw = vT[:, 0:TC * (CK - 1)].rearrange("p (t c) -> p c t", c=TC)
        for j in range(TC):
            dve.wait_ge(state_turned, j + 1)
            link(dve.tensor_tensor(ptmp[:, :].rearrange("p (b t) -> p b t", b=NB),
                                   ps[:, 3 + j % 4, 0:240].rearrange("p (b t) -> p b t", b=NB),
                                   cw[:, j:j + 1, :].broadcast_to([P, NB, CK - 1]), ALU.mult))
            dve.tensor_reduce(pconv[:, j, :], ptmp[:, :].rearrange("p (b t) -> p b t", b=NB), AX, ALU.add)\
                .then_inc(state_used, 1)
            dve.wait_ge(state_used, j + 1)
        link(dve.tensor_tensor(pconv[:, :, :], pconv[:, :, :],
                               vT[:, V_DWB:V_DWB + TC].unsqueeze(2).broadcast_to([P, TC, NB]), ALU.add))
        dve.wait_ge(state_turned, TC + 1)
        lw = vT[:, V_LW:V_LW + TC * (LK - 1)].rearrange("p (t c) -> p c t", c=TC)
        for j in range(TC):
            link(dve.tensor_tensor(ptmp[:, 0:24].rearrange("p (b t) -> p b t", b=NB),
                                   ps[:, 7, j * 24:(j + 1) * 24].rearrange("p (b t) -> p b t", b=NB),
                                   lw[:, j:j + 1, :].broadcast_to([P, NB, LK - 1]), ALU.mult))
            link(dve.tensor_reduce(plru[:, j, :], ptmp[:, 0:24].rearrange("p (b t) -> p b t", b=NB), AX, ALU.add))
        link(dve.tensor_tensor(plru[:, :, :], plru[:, :, :],
                               vT[:, V_LB:V_LB + TC].unsqueeze(2).broadcast_to([P, TC, NB]), ALU.add))

        dve.wait_ge(consts_ready, 5)
        for p in range(0, TC, 2):
            for j in (p, p + 1):
                n = 4 * (j // 2) + 2 + j % 2
                dve.wait_ge(acc_free, n + 1)
                dve.tensor_tensor(U[:, j, CK - 1:], U[:, j, CK - 1:], gate_buf[j % 2][:, :], ALU.mult)\
                    .then_inc(u_ready, 1)
            dve.wait_ge(u_ready, p + 2)
            last = {}
            for t in range(CK):
                for j in (p, p + 1):
                    w = vT[:, t * TC + j:t * TC + j + 1]
                    if t == 0:
                        last[j] = step(dve.tensor_scalar(mix[:, j, 0:SEQ], U[:, j, 0:SEQ], w,
                                                         vT[:, V_DWB + j:V_DWB + j + 1], ALU.mult, ALU.add))
                    else:
                        dve.wait_ge(dve_order, last[j])
                        last[j] = step(stt(mix[:, j, 0:SEQ], U[:, j, t:t + SEQ], w, mix[:, j, 0:SEQ],
                                           ALU.mult, ALU.add))
            for j in (p, p + 1):
                w = vT[:, (CK - 1) * TC + j:(CK - 1) * TC + j + 1]
                stt(mix[:, j, SEQ:TOK], U[:, j, UW - NB:UW], w, pconv[:, j, :], ALU.mult, ALU.add)\
                    .then_inc(conv_done, 1)

        def lconv(j):
            dve.wait_ge(acc_free, 16 + j + 1)
            for t in range(LK):
                w = vT[:, V_LW + t * TC + j:V_LW + t * TC + j + 1]
                if t == 0:
                    link(dve.tensor_scalar(lxc[:, j, 0:SEQ], L[:, j, 0:SEQ], w, vT[:, V_LB + j:V_LB + j + 1],
                                           ALU.mult, ALU.add))
                else:
                    link(stt(lxc[:, j, 0:SEQ], L[:, j, t:t + SEQ], w, lxc[:, j, 0:SEQ], ALU.mult, ALU.add))
            stt(lxc[:, j, SEQ:TOK], L[:, j, LW - NB:LW], w, plru[:, j, :], ALU.mult, ALU.add).then_inc(lconv_done, 1)

        def gated(j):
            dve.wait_ge(gates_taken, j + 1)
            dve.tensor_tensor(lxc[:, j, :], lxc[:, j, :], I[:, j % 2, :], ALU.mult).then_inc(i_used, 1)

        def recur(b):
            dve.wait_ge(tanh_ready, b + 1)
            dve.wait_ge(i_used, 4 * b + 4)
            link(dve.tensor_scalar(T[:, :, :], T[:, :, :], -1e-30, None, ALU.min))
            for x in (0, 2):
                link(dve.tensor_tensor(I[:, :, :], R[:, x:x + 2, :], R[:, x:x + 2, :], ALU.mult))
                last = stt(T[:, x:x + 2, :], I[:, :, :], 1.0, T[:, x:x + 2, :], ALU.add, ALU.mult)
                if x == 0:
                    link(last)
            last.then_inc(z_ready, 1)
            dve.wait_ge(beta_ready, b + 1)
            link(dve.tensor_tensor(T[:, :, :], T[:, :, :], lxc[:, 4 * b:4 * b + 4, :], ALU.mult))
            for j in range(4):
                dve.tensor_tensor_scan(mix[:, TC + 4 * b + j, 0:SEQ], R[:, j, 0:SEQ], T[:, j, 0:SEQ], 0.0,
                                       ALU.mult, ALU.add)
            h0 = vT[:, V_H0:V_H0 + 64].rearrange("p (b c) -> p c b", c=TC)[:, 4 * b:4 * b + 4, :]
            link(dve.tensor_tensor(R[:, :, SEQ:TOK], R[:, :, SEQ:TOK], h0, ALU.mult))
            link(dve.tensor_tensor(mix[:, TC + 4 * b:TC + 4 * b + 4, SEQ:TOK], R[:, :, SEQ:TOK], T[:, :, SEQ:TOK],
                                   ALU.add))
            dve.tensor_copy(htail[:, 4 * b:4 * b + 4, :], mix[:, TC + 4 * b:TC + 4 * b + 4, SEQ - 1:TOK])\
                .then_inc(scan_done, 1)
            dve.wait_ge(scan_done, b + 1)

        def gelu_mul(j):
            dve.wait_ge(acc_free, 24 + j + 1)
            dve.tensor_tensor(mix[:, TC + j, :], mix[:, TC + j, :], gate_buf[j % 2][:, :], ALU.mult)\
                .then_inc(mixr_ready, 1)

        for j in range(4):
            lconv(j)
        for j in range(4):
            lconv(4 + j)
            gated(j)
        recur(0)
        gelu_mul(0)
        gated(4)
        dve.wait_ge(mean_full, 1)
        for j in range(TC):
            stt(mix[:, j, :], ps[:, 6, 0:TOK], -1.0 / DC, mix[:, j, :], ALU.mult, ALU.add).then_inc(centred, 1)
        for j in range(1, 4):
            gelu_mul(j)
            gated(4 + j)
        recur(1)
        for j in range(4, 6):
            gelu_mul(j)
        dve.wait_ge(sq_used, 4)
        dve.wait_ge(i_used, TC)
        dve.tensor_scalar(I[:, 0, :], ps[:, 7, 0:TOK], 1.0 / DC, EPS, ALU.mult, ALU.add).then_inc(var_ready, 1)
        gelu_mul(6)
        dve.wait_ge(sd_ready, 1)
        link(dve.reciprocal(I[:, 0, :], I[:, 1, :]))
        for j in range(TC):
            dve.tensor_tensor(mix[:, j, :], mix[:, j, :], I[:, 0, :], ALU.mult).then_inc(scaled, 1)
        gelu_mul(7)

        def add_back(m, base):
            dve.wait_ge(h_turned, base + m + 1)
            b = ps[:, 3 + m % 2, :]
            cols = slice(m * P, (m + 1) * P)
            dve.tensor_tensor(h[:, 0:2, cols], h[:, 0:2, cols], b[:, 0:2 * P].rearrange("p (c d) -> p c d", c=2), ALU.add)
            dve.tensor_tensor(h[0:NB, 2, cols], h[0:NB, 2, cols], b[0:NB, 2 * P:3 * P], ALU.add).then_inc(h_added, 1)

        for m in range(KD):
            add_back(m, 0)
            if m in (2, 4, 6):
                w = m // 2 - 1
                dst, r = [(sc_out, CK - 1 + NB), (sl_out, LK - 1 + NB), (sh_out, 1 + NB)][w]
                dve.wait_ge(tail_turned, w + 1)
                dve.tensor_copy(dst[0:r, :].rearrange("p (a b) -> p a b", a=2), ps[0:r, 5:7, :]).then_inc(tail_taken, 1)

        dve.wait_ge(h_added, KD)
        dve.memset(logit[:, :, :], 0.0)
        dve.memset(gl[:, :, :], -3.0e38)
        link(dve.memset(rank[:, :, :], 0.0))
        dve.wait_ge(ssq_act, 2 + 12)
        link(dve.tensor_reduce(ssum[:, 0:3], sqp[:, :, :], AX, ALU.add))
        link(inverse_rms(2))
        dve.wait_ge(logits_full, 1)
        for c in range(3):
            r = ROWS[c]
            last = stt(logit[0:r, c, :], ps[0:r, 7, c * 64:c * 64 + NG + E], rstd[0:r, c:c + 1], br[0:r, :],
                       ALU.mult, ALU.add)
        link(last)
        link(dve.tensor_copy(gl[:, :, 0:NG], logit[:, :, 0:NG]))
        for c in range(3):
            last = dve.max(gmx[:, c, :], gl[:, c, :])
        link(last)
        for c in range(3):
            last = dve.max_index(gix[:, c, :], gmx[:, c, :], gl[:, c, :])
        link(last)
        link(dve.tensor_copy(gf[:, :], gix[:, :, 0]))
        link(dve.tensor_tensor(gex[:, :, :], logit[:, :, 0:NG], gmx[:, :, 0:1].broadcast_to([P, 3, NG]), ALU.subtract))
        dve.wait_ge(iotas_ready, 5)
        link(dve.tensor_tensor(oh4[:, :, :], i32r[:, 0:NG].unsqueeze(1).broadcast_to([P, 3, NG]),
                               gf[:, :].unsqueeze(2).broadcast_to([P, 3, NG]), ALU.is_equal))
        for c in range(3):
            last = dve.tensor_tensor(el[:, c, :, :], logit[:, c, NG:].rearrange("p (g j) -> p g j", g=NG),
                                     oh4[:, c, :].unsqueeze(2).broadcast_to([P, NG, EG]), ALU.mult)
        link(last)
        link(dve.tensor_reduce(ein[:, :, :], el[:, :, :, :].rearrange("p c g j -> p c j g"), AX, ALU.add))
        for c in range(3):
            last = dve.max(emx[:, c, :], ein[:, c, :])
        link(last)
        link(dve.tensor_tensor(ex[:, :], emx[:, :, 1], emx[:, :, 0], ALU.subtract))
        for c in range(3):
            last = dve.max_index(eix[:, c, :], emx[:, c, :], ein[:, c, :])
        last.then_inc(softmax_in, 1)
        dve.wait_ge(softmax_in, 1)
        link(dve.tensor_copy(ef[:, :, :], eix[:, :, 0:2]))
        for q in range(2):
            last = stt(ef[:, :, q], gf[:, :], float(EG), ef[:, :, q], ALU.mult, ALU.add)
        link(last)
        for q in range(2):
            last = dve.tensor_tensor(oh[:, q, :, :], i32r[:, :].unsqueeze(1).broadcast_to([P, 3, E]),
                                     ef[:, :, q].unsqueeze(2).broadcast_to([P, 3, E]), ALU.is_equal)
        link(last)
        dve.tensor_tensor(asg[:, :, :], oh[:, 0, :, :], oh[:, 1, :, :], ALU.add).then_inc(assigned, 1)
        dve.wait_ge(ranks_full, 1)
        rk = ps[:, 6, 0:192].rearrange("p (c n) -> p c n", c=3)
        dve.tensor_copy(rank[:, 0:2, :], rk[:, 0:2, 0:E])
        dve.tensor_copy(rank[0:NB, 2, :], rk[0:NB, 2, 0:E])
        link(dve.tensor_copy(cnt[:, :], ps[:, 6, 192:192 + E]))
        link(dve.tensor_tensor_scan(off[:, :], ones[:, 0:E], cnt[:, :], 0.0, ALU.mult, ALU.add))
        link(dve.tensor_tensor(off[:, :], off[:, :], cnt[:, :], ALU.subtract))
        for q in range(2):
            link(dve.tensor_tensor(prod[:, :, :], oh[:, q, :, :], rank[:, :, :], ALU.mult))
            link(dve.tensor_reduce(rnk[:, q, :], prod[:, :, :], AX, ALU.add))
            link(dve.tensor_tensor(prod[:, :, :], oh[:, q, :, :], off[:, :].unsqueeze(1).broadcast_to([P, 3, E]), ALU.mult))
            link(dve.tensor_reduce(pos[:, q, :], prod[:, :, :], AX, ALU.add))
        link(dve.tensor_tensor(pos[:, :, :], pos[:, :, :], rnk[:, :, :], ALU.add))
        dve.wait_ge(iotas_ready, 6)
        for c in range(3):
            r = ROWS[c]
            link(dve.tensor_scalar(onehot[0:r, c, :], iota[0:r, :], pos[0:r, 0, c:c + 1], None, ALU.is_equal))
            stt(onehot[0:r, c, :], iota[0:r, :], pos[0:r, 1, c:c + 1], onehot[0:r, c, :], ALU.is_equal, ALU.add)\
                .then_inc(hot_ready, 1)
        dve.wait_ge(softmax_out, 1)
        link(dve.tensor_reduce(gw[:, :], gex[:, :, :], AX, ALU.add))
        link(dve.tensor_scalar(wts[:, 1, :], ex[:, :], 1.0, None, ALU.add))
        link(dve.tensor_tensor(gw[:, :], gw[:, :], wts[:, 1, :], ALU.mult))
        link(dve.reciprocal(wts[:, 0, :], gw[:, :]))
        link(dve.tensor_tensor(wts[:, 1, :], wts[:, 0, :], ex[:, :], ALU.mult))
        link(dve.tensor_scalar(rnk[:, :, :], rnk[:, :, :], float(WIN), float(XW), ALU.is_ge, ALU.mult))
        link(dve.tensor_tensor(rowix[:, :, :], pos[:, :, :], rnk[:, :, :], ALU.add))
        link(dve.tensor_copy(offs[0:1, 0:E], off[0:1, :]))
        link(dve.memset(offs[0:1, E:E + 1], NSLOT))
        cb = cnt[:, :].unsqueeze(2).broadcast_to([P, E, 4])
        wb = win64[:, :].unsqueeze(1).broadcast_to([P, E, 4])
        link(dve.tensor_tensor(over[:, :, :], cb, wb, ALU.is_gt))
        ov = over[:, :, :].rearrange("p e c -> p (e c)")
        oi = oidx[:, :, :].rearrange("p e c -> p (e c)")
        link(dve.tensor_tensor_scan(oi, ones[:, :], ov, 0.0, ALU.mult, ALU.add))
        link(dve.tensor_copy(offs[0:1, 40:41], oi[0:1, E * 4 - 1:E * 4]))
        link(dve.tensor_tensor(oi, oi, ov, ALU.subtract))
        link(dve.tensor_scalar(osel[:, :, :], oidx[:, :, :], pidx[:, 0:1], None, ALU.is_equal))
        link(dve.tensor_tensor(osel[:, :, :], osel[:, :, :], over[:, :, :], ALU.mult))
        link(dve.tensor_tensor(opr[:, :, :], osel[:, :, :], i32r[:, :].unsqueeze(2).broadcast_to([P, E, 4]), ALU.mult))
        link(dve.tensor_reduce(otab[:, 0:1], opr[:, :, :].rearrange("p e c -> p (e c)"), AX, ALU.add))
        link(dve.tensor_tensor(opr[:, :, :], off[:, :].unsqueeze(2).broadcast_to([P, E, 4]), wb, ALU.add))
        link(dve.tensor_tensor(opr[:, :, :], opr[:, :, :], osel[:, :, :], ALU.mult))
        link(dve.tensor_reduce(otab[:, 1:2], opr[:, :, :].rearrange("p e c -> p (e c)"), AX, ALU.add))
        dve.tensor_copy(otabi[:, :], otab[:, :]).then_inc(table_ready, 1)
        dve.memset(xsort[:, :, NSLOT:XW], 0.0).then_inc(pad_ready, 1)
        for m in range(0, 2 * KD, 2):
            half, k = m // KD, m % KD
            dve.wait_ge(sort_full, m + 1)
            dve.tensor_scalar(xsort[:, k, half * HALF:(half + 1) * HALF], ps[:, 4, 0:HALF], g2[:, k:k + 1], None,
                              ALU.mult).then_inc(sort_dve, 1)
        dve.wait_ge(sort_dve, KD)
        dve.wait_ge(sort_act, KD)
        dve.wait_ge(table_ready, 1)
        dve.wait_ge(acc_full, CT_PG)

        def take_window(start, window):
            dve.tensor_copy(xwin[:, :, :], xsort[:, :, bass.ds(start, WIN)]).then_inc(window, 1)

        def expert(i, sems):
            dve.wait_ge(sems["silu"], i + 1)
            dve.tensor_tensor(sgl[WIN:2 * WIN, :], sgl[WIN:2 * WIN, :], ps[WIN:2 * WIN, 0, :], ALU.mult)\
                .then_inc(sems["gated"], 1)
            dve.wait_ge(sems["turned"], i + 1)
            dve.tensor_copy(hid[:, :, :].rearrange("p t w -> p (t w)"), ps[:, 1, 0:4 * WIN]).then_inc(sems["hid"], 1)

        def take_results(i, par, sems):
            dve.wait_ge(sems["down"], i + 1)
            if sems is main:
                dve.wait_ge(y_out, (i + 1) * 16)
            dve.tensor_copy(ysb[:, par, 512:1024], ps[:, 3, :]).then_inc(sems["evac"], 1)

        take_window(0, main["window"])
        with dve.Fori(0, E, 2) as e2:
            for par in range(2):
                expert(e2 + par, main)
                start = dve.value_load(offs[0:1, bass.ds(e2 + par + 1, 1)], min_val=0, max_val=NSLOT)
                take_window(start, main["window"])
                take_results(e2 + par, par, main)
        dve.wait_ge(table_out, 16)
        n_over = dve.value_load(offs[0:1, 40:41], min_val=0, max_val=MAX_OVER)
        with dve.If(n_over > 0):
            with dve.Fori(0, n_over) as i:
                start = dve.value_load(ov_dram[bass.ds(i, 1), 1:2], min_val=0, max_val=NSLOT)
                dve.wait_ge(main["down"], E)
                take_window(start, extra["window"])
                expert(i, extra)
                take_results(i, 0, extra)

        for c in (2, 0, 1):
            r = ROWS[c]
            dve.wait_ge(rows_back[c], 32)
            link(stt(h[0:r, c, :], g0[0:r, c, :], wts[0:r, 0, c:c + 1], h[0:r, c, :], ALU.mult, ALU.add))
            stt(h[0:r, c, :], g1[0:r, c, :], wts[0:r, 1, c:c + 1], h[0:r, c, :], ALU.mult, ALU.add).then_inc(h2_ready, 1)
        dve.wait_ge(ssq_act, 2 + 12 + 3)
        link(inverse_rms(3))
        diagonals()
        take_xT(8, lambda k: vT[:, V_PN + k:V_PN + k + 1])
        dve.wait_ge(fing_loaded, 16)

        def final_gain(q):
            cols = slice(512 * q, 512 * (q + 1))
            dve.wait_ge(h_added, KD + 4 * q + 4)
            dve.tensor_tensor(hg[:, 0:2, cols], h[:, 0:2, cols], fing[:, cols].unsqueeze(1).broadcast_to([P, 2, 512]),
                              ALU.mult)
            link(dve.tensor_tensor(hg[0:NB, 2, cols], h[0:NB, 2, cols], fing[0:NB, cols], ALU.mult))

        for m in range(KD):
            dve.wait_ge(acc_free, freed(CT_PG + m))
            dve.tensor_tensor(pleT[:, m, :], pleT[:, m, :], gate_tail(m), ALU.mult).then_inc(prod_ready, 1)
            if m:
                add_back(m - 1, KD)
            if m and m % 4 == 0:
                final_gain(m // 4 - 1)
        add_back(KD - 1, KD)
        final_gain(3)
        dve.wait_ge(ssq_act, 2 + 12 + 3 + 12)
        link(dve.tensor_reduce(ssum[:, 0:3], sqp[:, :, :], AX, ALU.add))
        inverse_rms(4).then_inc(dg_ready, 1)
        dve.wait_ge(dg_ready, 7)
        for c in (2, 0):
            r = ROWS[c]
            dve.tensor_scalar(hg[0:r, c, :], hg[0:r, c, :], rstd[0:r, c:c + 1], None, ALU.mult).then_inc(y_ready, 1)

    block.__exit__(None, None, None)


N_ROWS = 17


def row_loads(a, vrow, stage, lstage, g2):
    def rows(x):
        return x.rearrange("l (r p) -> (l r) p", p=P)

    cw = a["conf_dw_w"].rearrange("l t (c p) -> (l t c) p", p=P)
    yield vrow[:, 0, :], cw[0:P, :]
    yield vrow[0:120, 1, :], cw[P:248, :]
    at = 0
    for name, n in (("norm1_g", 16), ("ple_norm_g", 16), ("b_in", 32), ("b_pg", 16), ("conf_dw_b", 8),
                    ("conf_ln_g", 8), ("conf_ln_b", 8)):
        yield vrow[at:at + n, 2, :], rows(a[name])
        at += n
    yield vrow[0:32, 3, :], a["lru_conv_w"].rearrange("l t (c p) -> (l t c) p", p=P)
    yield vrow[32:40, 3, :], rows(a["lru_conv_b"])
    yield vrow[40:48, 3, :], a["lru_ba"].rearrange("l h j -> (l h) j")
    yield vrow[48:56, 3, :], a["lru_bx"].rearrange("l h j -> (l h) j")
    yield vrow[56:64, 3, :], rows(a["lru_lambda"])
    yield vrow[64:128, 3, :], a["state_lru_h"].rearrange("l b (c p) -> (l b c) p", p=P)
    yield vrow[0:16, 4, :], rows(a["norm2_g"])
    yield g2[:, :], a["norm2_g"].rearrange("l (p k) -> p (l k)", k=KD)
    yield stage[0:120, :, :], a["state_conf_conv"].rearrange("l (q b) t c -> (b t) (l q) c", q=2)
    yield lstage[0:24, :], a["state_lru_conv"].rearrange("l b t c -> (l b t) c")


INPUTS = ["x_prompt", "x_sample", "state_conf_conv", "state_lru_conv", "state_lru_h", "p_prompt", "p_sample",
          "norm1_g", "w_in", "b_in", "conf_dw_w", "conf_dw_b", "conf_ln_g", "conf_ln_b", "lru_conv_w", "lru_conv_b",
          "lru_wa", "lru_ba", "lru_wx", "lru_bx", "lru_lambda", "w_out", "norm2_g", "w_grp", "b_grp", "w_rt", "b_rt",
          "w_gate", "w_up", "w_down", "ple_norm_g", "w_ple", "w_pg", "b_pg", "final_g"]
OUTPUTS = [("y_prompt", (1, SEQ, D)), ("y_sample", (NB, 1, D)), ("conf_prompt", (1, 1, CK - 1, DC)),
           ("conf_sample", (1, NB, CK - 1, DC)), ("lru_prompt", (1, 1, LK - 1, DC)),
           ("lru_sample", (1, NB, LK - 1, DC)), ("h_prompt", (1, 1, DC)), ("h_sample", (1, NB, DC))]


def kernel(**inputs):
    import numpy as _np
    import concourse.bacc as _bacc
    from concourse import mybir as _mybir
    from concourse.bass_utils import run_bass_kernel_spmd as _run

    nc = _bacc.Bacc("TRN2", target_bir_lowering=False, num_devices=1)
    arrays, a, o = {}, {}, {}
    for name in INPUTS:
        x = _np.ascontiguousarray(inputs[name])
        arrays[f"in_{name}_dram"] = x
        a[name] = nc.dram_tensor(f"in_{name}_dram", x.shape, _mybir.dt.from_np(x.dtype), kind="ExternalInput").ap()
    for name, shape in OUTPUTS:
        o[name] = nc.dram_tensor(f"out_{name}_dram", shape, _mybir.dt.float32, kind="ExternalOutput").ap()
    build(nc, a, o)
    r = _run(nc, [arrays], core_ids=[0])
    return tuple(r.results[0][f"out_{name}_dram"] for name, _ in OUTPUTS)
```

```python
import numpy as np

import concourse.bass as bass
from concourse import mybir
from concourse.alu_op_type import AluOpType as ALU

ACT = mybir.ActivationFunctionType
F32 = mybir.dt.float32
F32R = mybir.dt.float32r
I32 = mybir.dt.int32
U32 = mybir.dt.uint32
AX = mybir.AxisListType.X

D = 2048
SEQ = 256
NB = 8
TOK = SEQ + NB
DC = 1024
CK = 31
LK = 4
E = 32
NG = 4
EG = E // NG
F = D // 4
DP = 256
EPS = 1e-6
P = 128
KD = D // P
TC = DC // P
ROWS = [P, P, NB]

NS = 12
CH_IN = 32
CH_PLE = DP // P
CH_EXP = 12
PG_SLOTS = 4
EXP_SLOT = [6, 7, 8, 0, 9, 1, 10, 2, 11, 3, 4, 5]
PLE_SLOT = 4
MIX_ORDER = list(range(TC, KD - 1)) + list(range(TC)) + [KD - 1]

WIN = 64
NSLOT = 2 * TOK
XW = NSLOT + WIN
ODD = 3
PLE_FIRST = 8
LOW = WIN // 2
R_BIG = 37888
YROWS = -(-2 * XW // (2 * P)) * 2 * P
MAX_OVER = NSLOT // WIN

V_CW = 0
V_N1, V_PN, V_BIN, V_BPG, V_DWB, V_LNG, V_LNB = 248, 264, 280, 312, 328, 336, 344
V_LW, V_LB, V_BA, V_BX, V_LAM, V_H0 = 352, 384, 392, 400, 408, 416
NV = 480

GROUP_COL = [0, 256, 512, 768, 2048, 2560, 3072, 3584]
UW = CK - 1 + TOK
LW = LK - 1 + TOK
CT_IN, CT_OUT, CT_PLE, CT_PG = 0, 32, 48, 64


def build(nc, a, o):
    top = [((nc.sbuf_base + 31) // 32) * 32]

    def region(size):
        at = top[0]
        top[0] += size
        assert top[0] <= nc.sbuf_usable_end, (top[0], nc.sbuf_usable_end)
        return at

    def place(name, shape, dt, at):
        return nc.alloc_sbuf_tensor_at(name, shape, dt, offset=at)

    def sem(name):
        return nc.alloc_semaphore(name)

    r_ring = region(NS * 8192)
    r_h = region(3 * 8192)
    r_big = region(R_BIG)
    r_xs = region(3 * 8192)
    r_xt = region(KD * TOK * 4)
    r_const = region(10616)

    ring = place("ring", [P, NS, D], F32, r_ring)
    ring_r = place("ring_r", [P, NS, KD, P], F32R, r_ring)
    x_lo = place("x_lo", [P, KD, TOK], F32R, r_ring + 2 * PG_SLOTS * 8192)
    h = place("h", [P, 3, D], F32, r_h)

    U = place("U", [P, TC, UW], F32, r_big)
    at = r_big + TC * UW * 4
    mix = place("mix", [P, KD, TOK], F32, at)
    mix_lo = place("mix_lo", [P, KD, TOK], F32R, at)
    stage = place("stage", [P, 2, DC], F32, at)
    lstage = place("lstage", [P, DC], F32, at + 8192)
    vrow = place("vrow", [P, 5, P], F32, at + 12288)
    ptmp = place("ptmp", [P, 240], F32, at + 14848)
    at += KD * TOK * 4
    L = place("L", [P, TC, LW], F32, at)
    at += TC * LW * 4
    wr = place("wr", [P, KD, NG + E], F32, at)
    at += KD * (NG + E) * 4
    br = place("br", [P, NG + E], F32, at)
    at += 160
    htail = place("htail", [P, TC, NB + 1], F32, at)
    at += 288
    assert at <= r_big + R_BIG
    sdump2 = place("sdump2", [P, 512], F32, r_big + 4 * 8192)
    ysb = place("ysb", [P, 2, D // 2], F32, r_big)
    xrow = place("xrow", [P, 2, 512], F32, r_big + 8192)
    odd_ring = place("odd_ring", [P, ODD, D], F32, r_big + 12288)
    g0 = place("g0", [P, 3, D], F32, r_big)
    hg = place("hg", [P, 3, D], F32, r_big)
    fing = place("fing", [P, D], F32, r_big + 3 * 8192)

    xdump = place("xdump", [P, 2, D], F32, r_xs)
    sdump = place("sdump", [P, 512], F32, r_xs + 12288)
    xs = place("xs", [P, 3, D], F32, r_xs)
    xs3 = place("xs3", [P, 3, D], F32, r_big)
    g1 = place("g1", [P, 3, D], F32, r_xs + 16896)
    lxc = place("lxc", [P, TC, TOK], F32, r_xs)
    wa = place("wa", [P, TC, P], F32, r_xs + 8448)
    wx = place("wx", [P, TC, P], F32, r_xs + 8448 + 4096)
    R = place("R", [P, 4, TOK], F32, r_xs + 16640)
    I = place("I", [P, 2, TOK], F32, r_xs + 20864)
    sc_out = place("sc_out", [P, DC], F32, r_xs)
    sl_out = place("sl_out", [P, DC], F32, r_xs + 4096)
    sh_out = place("sh_out", [P, DC], F32, r_xs + 8192)
    pleT = place("pleT", [P, KD, TOK], F32, r_xs)

    xT = place("xT", [P, KD, TOK], F32, r_xt)
    x_hi = place("x_hi", [P, KD, TOK], F32R, r_xt)
    onehot = place("onehot", [P, 3, XW], F32, r_xt)
    iota = place("iota", [P, XW], F32, r_xt + 7104)
    rxT = place("rxT", [P, 3, TOK], F32, r_xs + 14336)
    prow = place("prow", [P, 3, DP], F32, r_xs + 17504)
    pT = place("pT", [P, 2, TOK], F32, r_xs + 20576)
    xwin = place("xwin", [P, KD, WIN], F32, r_xt + 7104)
    hid = place("hid", [P, 4, WIN], F32, r_xt + 11200)
    wslot = place("wslot", [P, 3, WIN], F32, r_xt + 14272)
    sgl = place("sgl", [P, F], F32, r_xt + 12224)

    at = r_const
    ident = place("ident", [P, P], F32, at)
    ones = place("ones", [P, P], F32, at + 512)
    vT = place("vT", [P, NV], F32, at + 1024)
    T = place("T", [P, 4, TOK], F32, at + 2944)
    pconv = place("pconv", [P, TC, NB], F32, at + 2944)
    sqp = place("sqp", [P, 3, 4], F32, r_const + 10560)
    g2n = place("g2n", [P, KD], F32, r_const + 10496)
    zeros = place("zeros", [P, 512], F32, at + 3200)
    sq = place("sq", [P, 2, TOK], F32, at + 7168)
    plru = place("plru", [P, TC, NB], F32, at + 7168)
    sg = place("sg", [P, TOK], F32, at + 9280)
    g2 = place("g2", [P, KD], F32, at + 10336)
    negc = place("negc", [P, TC], F32, at + 10400)
    ssum = place("ssum", [P, 4], F32, at + 10432)
    rstd = place("rstd", [P, 4], F32, at + 10464)
    spt = place("spt", [P, 3, TC], F32, at + 5280)
    sgb = place("sgb", [P, TOK], F32, r_xs + 22976)
    gate_buf = [sg, sgb]

    ra = at + 2944
    rsz = [0]

    def rt(name, shape, dt=F32):
        n = 4
        for s in shape[1:]:
            n *= s
        x = place(name, shape, dt, ra + rsz[0])
        rsz[0] += (n + 31) // 32 * 32
        assert rsz[0] <= 7392
        return x

    offs = rt("offs", [1, 64], I32)
    wts = rt("wts", [P, 2, 3])
    high = place("high", [1, 2, 40], I32, r_big + 36864)
    highf = place("highf", [1, 2, E], F32, r_big + 37184)
    rowix = rt("rowix", [P, 2, 3], I32)
    logit = rt("logit", [P, 3, NG + E])
    gl = rt("gl", [P, 3, 8])
    gmx = rt("gmx", [P, 3, 8])
    gix = rt("gix", [P, 3, 8], U32)
    gf = rt("gf", [P, 3])
    gex = rt("gex", [P, 3, NG])
    gw = rt("gw", [P, 3])
    oh4 = rt("oh4", [P, 3, NG])
    el = rt("el", [P, 3, NG, EG])
    ein = rt("ein", [P, 3, EG])
    emx = rt("emx", [P, 3, 8])
    eix = rt("eix", [P, 3, 8], U32)
    ef = rt("ef", [P, 3, 2])
    ex = rt("ex", [P, 3])
    oh = rt("oh", [P, 2, 3, E])
    asg = rt("asg", [P, 3, E])
    rank = rt("rank", [P, 3, E])
    cnt = rt("cnt", [P, E])
    off = rt("off", [P, E])
    pos = rt("pos", [P, 2, 3])
    rnk = rt("rnk", [P, 2, 3])
    tri = rt("tri", [P, P])
    i32r = rt("i32r", [P, E])
    hT = place("hT", [P, 2, TOK], F32, ra + rsz[0])
    prod = rt("prod", [P, 3, E])
    over = rt("over", [P, E, 4])
    oidx = rt("oidx", [P, E, 4])
    osel = rt("osel", [P, E, 4])
    opr = rt("opr", [P, E, 4])
    win64 = rt("win64", [P, 4])
    pidx = rt("pidx", [P, 1])
    otab = rt("otab", [P, 2])
    otabi = rt("otabi", [P, 2], I32)

    ps = nc.alloc_psum_tensor("ps", [P, 8, 512], F32)

    y_dram = nc.dram_tensor("y_sorted", (YROWS, D), F32, kind="Internal").ap()
    ov_dram = nc.dram_tensor("over_table", (MAX_OVER, 2), I32, kind="Internal").ap()

    slot_loaded = [sem(f"slot_loaded{i}") for i in range(NS)]
    odd_loaded = [sem(f"odd_loaded{i}") for i in range(ODD)]
    chunk_used = sem("chunk_used")
    x_loaded = [sem(f"x_loaded{c}") for c in range(3)]
    late_rows = sem("late_rows")
    rows_loaded = sem("rows_loaded")
    gates_loaded = sem("gates_loaded")
    router_loaded = sem("router_loaded")
    p_loaded = sem("p_loaded")
    fing_loaded = sem("fing_loaded")
    consts_ready = sem("consts_ready")
    iotas_ready = sem("iotas_ready")
    act_order = sem("act_order")
    dve_order = sem("dve_order")
    zeros_ready = sem("zeros_ready")
    ms_ready = sem("ms_ready")
    root_ready = sem("root_ready")
    xs_ready = sem("xs_ready")
    rstd_ready = sem("rstd_ready")
    vec_turned = sem("vec_turned")
    vec_ready = sem("vec_ready")
    x_turned = sem("x_turned")
    xT_dve = sem("xT_dve")
    xT_act = sem("xT_act")
    state_turned = sem("state_turned")
    state_used = sem("state_used")
    acc_full = sem("acc_full")
    acc_free = sem("acc_free")
    sig_ready = sem("sig_ready")
    u_ready = sem("u_ready")
    conv_done = sem("conv_done")
    lconv_done = sem("lconv_done")
    gates_full = sem("gates_full")
    gates_taken = sem("gates_taken")
    i_ready = sem("i_ready")
    i_used = sem("i_used")
    tanh_ready = sem("tanh_ready")
    z_ready = sem("z_ready")
    beta_ready = sem("beta_ready")
    scan_done = sem("scan_done")
    gelu_ready = sem("gelu_ready")
    mixr_ready = sem("mixr_ready")
    mean_full = sem("mean_full")
    centred = sem("centred")
    sq_ready = sem("sq_ready")
    sq_used = sem("sq_used")
    var_full = sem("var_full")
    var_ready = sem("var_ready")
    sd_ready = sem("sd_ready")
    scaled = sem("scaled")
    mixc_ready = sem("mixc_ready")
    hT_ready = sem("hT_ready")
    h_turned = sem("h_turned")
    h_added = sem("h_added")
    tail_turned = sem("tail_turned")
    tail_taken = sem("tail_taken")
    state_out = sem("state_out")
    ssq_act = sem("ssq_act")
    ssum_set = sem("ssum_set")
    r_turned = sem("r_turned")
    rx_ready = sem("rx_ready")
    logits_full = sem("logits_full")
    softmax_in = sem("softmax_in")
    softmax_out = sem("softmax_out")
    assigned = sem("assigned")
    ranks_full = sem("ranks_full")
    table_ready = sem("table_ready")
    table_out = sem("table_out")
    hot_ready = sem("hot_ready")
    onehot_ready = sem("onehot_ready")
    p_turned = sem("p_turned")
    pT_ready = sem("pT_ready")
    y_out = sem("y_out")
    y_high = sem("y_high")
    expert_steps = ("slots", "gathered", "rows", "rows_turned", "window", "products", "silu", "gated", "turned", "hid", "down", "evac")
    main = {n: sem(f"main_{n}") for n in expert_steps}
    extra = {n: sem(f"extra_{n}") for n in expert_steps}
    over_loaded = sem("over_loaded")
    over_out = sem("over_out")
    over_free = sem("over_free")
    rows_back = [sem(f"rows_back{c}") for c in range(3)]
    h2_ready = sem("h2_ready")
    tile_loaded = [sem(f"tile_loaded{i}") for i in range(PG_SLOTS)]
    w_hi_ready = sem("w_hi_ready")
    w_lo_ready = sem("w_lo_ready")
    mix_hi_ready = sem("mix_hi_ready")
    mix_lo_ready = sem("mix_lo_ready")
    ple_loaded = sem("ple_loaded")
    prod_ready = sem("prod_ready")
    y_ready = sem("y_ready")
    y_act = sem("y_act")
    out_done = sem("out_done")

    block = nc.Block()
    block.__enter__()

    def chunk_view(n):
        c0 = GROUP_COL[n // 4]
        if n < CH_IN // 2:
            v = a["w_in"].rearrange("l (k p) (h c) -> h p (l k) c", p=P, h=4)
            return v[:, :, 4 * (n % 4):4 * (n % 4) + 4, c0:c0 + 256], 256
        v = a["w_in"].rearrange("l (k p) c -> p (l k) c", p=P)
        return v[:, 4 * (n % 4):4 * (n % 4) + 4, c0:c0 + 512], 512

    def freed(n):
        return n + 1 if n < CT_OUT else n + 1 - KD

    def used(n):
        if n % 4 == 3:
            return acc_full, n + 1
        return chunk_used, 3 * (n // 4) + n % 4 + 1

    def lo_slot(t):
        return (8 if t < KD else 0) + t % PG_SLOTS

    def hi_slot(t):
        return (0 if t < KD else 4) + t % PG_SLOTS

    def tile_view(t):
        v = a["w_out" if t < KD else "w_pg"].rearrange("l (k p) c -> p (l k) c", p=P)
        return v[:, :, t % KD * P:(t % KD + 1) * P]

    def tile_in(t):
        return tile_loaded[t % PG_SLOTS], 16 * (t // PG_SLOTS + 1)

    def used_expert(e, j):
        if j in (6, 7):
            return main["products"], e + 1
        if j == CH_EXP - 1:
            return main["down"], e + 1
        part = j // 2 if j < 8 else j - 5
        return chunk_used, e * 6 + (3 * CH_IN // 4 + part + 1)

    def gate_tail(m):
        return sq[:, m % 2, :]

    def slot(n):
        return n % NS

    def slot_count(n):
        return 16 * sum(2 if m < CH_IN // 2 else 1 for m in range(slot(n), n + 1, NS))

    def expert_count(j):
        return 16 + slot_count(max(n for n in range(CH_IN) if slot(n) == EXP_SLOT[j]))

    gate_v = a["w_gate"].rearrange("l e (p k) f -> p (l e) (k f)", k=KD)
    up_v = a["w_up"].rearrange("l e (p k) f -> p (l e) (k f)", k=KD)

    def down_view(e, t):
        return a["w_down"].rearrange("l e (t p) d -> t p (l e) d", p=P)[t, :, bass.ds(e, 1), :]

    def expert_view(e, j):
        if j < 8:
            return (gate_v, up_v)[j % 2][:, bass.ds(e, 1), j // 2 * D:(j // 2 + 1) * D]
        return down_view(e, j - 8)

    @block.sync
    def _(sp):
        def load(n):
            src, w = chunk_view(n)
            if n >= NS:
                sp.wait_ge(*used(n - NS))
            if w == 256:
                dst = ring[:, slot(n), :].rearrange("p (k h c) -> p k h c", c=w, h=2)
                for half in range(2):
                    sp.dma_start(dst[:, :, half, :], src[half]).then_inc(slot_loaded[slot(n)], 16)
            else:
                dst = ring[:, slot(n), :].rearrange("p (k c) -> p k c", c=w)
                sp.dma_start(dst, src).then_inc(slot_loaded[slot(n)], 16)

        sp.dma_start(h[:, 1, :], a["x_prompt"][0, P:2 * P, :]).then_inc(x_loaded[1], 16)
        sp.dma_start(h[0:NB, 2, :], a["x_sample"][:, 0, :]).then_inc(x_loaded[2], 16)
        sp.dma_start(h[:, 0, :], a["x_prompt"][0, 0:P, :]).then_inc(x_loaded[0], 16)
        for n, (dst, src) in enumerate(row_loads(a, vrow, stage, lstage, g2)):
            if n == N_ROWS:
                for m in range(4):
                    load(m)
            sp.dma_start(dst, src).then_inc(rows_loaded if n < N_ROWS else late_rows, 16)
        for n in range(4, CH_IN):
            load(n)

        def load_tile(t):
            sp.dma_start(ring[:, lo_slot(t), :].rearrange("p (k c) -> p k c", k=KD), tile_view(t))\
                .then_inc(tile_loaded[t % PG_SLOTS], 16)

        for t in range(KD):
            if t < PG_SLOTS:
                sp.wait_ge(*used(CH_IN - NS + t))
            else:
                sp.wait_ge(acc_full, CT_OUT + t - PG_SLOTS + 1)
            if t == 2 * PG_SLOTS:
                for k in range(CH_PLE):
                    sp.dma_start(ring[:, PLE_SLOT + k, :],
                                 a["w_ple"].rearrange("l (k p) c -> p (l k) c", p=P)[:, k, :]).then_inc(ple_loaded, 16)
            load_tile(t)
        for j in range(CH_EXP):
            s = EXP_SLOT[j]
            if s in (PLE_SLOT, PLE_SLOT + 1):
                sp.wait_ge(acc_full, CT_PG)
            elif s < 4 or s >= 8:
                sp.wait_ge(acc_full, CT_PLE - PG_SLOTS + s % PG_SLOTS + 1)
            sp.dma_start(ring[:, s:s + 1, :], expert_view(0, j)).then_inc(slot_loaded[s], 16)

        def load_expert(e, par, before):
            for j in range(CH_EXP):
                before(j)
                if par == 1 and j < ODD:
                    sp.dma_start(odd_ring[:, j:j + 1, :], expert_view(e, j)).then_inc(odd_loaded[j], 16)
                else:
                    s = EXP_SLOT[j]
                    sp.dma_start(ring[:, s:s + 1, :], expert_view(e, j)).then_inc(slot_loaded[s], 16)

        def before_second(j):
            if j < ODD:
                sp.wait_ge(assigned, 1)
            else:
                sp.wait_ge(*used_expert(0, j))

        load_expert(1, 1, before_second)
        with sp.Fori(1, E // 2) as pair:
            for par in range(2):
                e = pair * 2 + par

                def before(j):
                    sp.wait_ge(*used_expert(e - 2 if j < ODD else e - 1, j))

                load_expert(e, par, before)
        sp.wait_ge(table_out, 16)
        n_over = sp.value_load(offs[0:1, 40:41], min_val=0, max_val=MAX_OVER)
        with sp.If(n_over > 0):
            sp.wait_ge(main["down"], E)
            with sp.Fori(0, n_over) as i:
                e = sp.value_load(ov_dram[bass.ds(i, 1), 0:1], min_val=0, max_val=E - 1)
                sp.wait_ge(over_free, i + 1)
                for j in range(CH_EXP):
                    sp.dma_start(ring[:, j:j + 1, :], expert_view(e, j)).then_inc(over_loaded, 16)
        for c in range(3):
            sp.wait_ge(rows_back[c], 32)
        for m in range(KD):
            if m >= PG_SLOTS:
                sp.wait_ge(acc_full, CT_PG + m - PG_SLOTS + 1)
            load_tile(KD + m)
        for c in (2, 0):
            sp.wait_ge(y_ready, 1 if c == 2 else 2)
            dst = o["y_prompt"][0, c * P:(c + 1) * P, :] if c < 2 else o["y_sample"][:, 0, :]
            sp.dma_start(dst, hg[0:ROWS[c], c, :]).then_inc(out_done, 16)
        sp.wait_ge(out_done, 48)

    @block.gpsimd
    def _(pool):
        pool.memset(ident[:, :], 0.0).then_inc(consts_ready, 1)
        pool.memset(ones[:, :], 1.0).then_inc(consts_ready, 1)
        pool.memset(U[:, :, 0:CK - 1], 0.0).then_inc(consts_ready, 1)
        pool.memset(L[:, :, 0:LK - 1], 0.0).then_inc(consts_ready, 1)
        pool.memset(zeros[:, :], 0.0).then_inc(zeros_ready, 1)
        pool.wait_ge(consts_ready, 4)
        pool.affine_select(out=ident[:, :], in_=ident[:, :], compare_op=ALU.not_equal, fill=1.0,
                           base=0, pattern=[[-1, P]], channel_multiplier=1).then_inc(consts_ready, 1)
        pool.dma_start(o["conf_sample"][0, :, 0:CK - 2, :], a["state_conf_conv"][0, :, 1:CK - 1, :])\
            .then_inc(state_out, 16)
        pool.dma_start(o["lru_sample"][0, :, 0:LK - 2, :], a["state_lru_conv"][0, :, 1:LK - 1, :])\
            .then_inc(state_out, 16)
        pool.wait_ge(acc_full, 8)
        pool.wait_ge(zeros_ready, 1)
        for x in range(4):
            pool.dma_start(y_dram[x * YROWS // 4:(x + 1) * YROWS // 4, :].rearrange("(p r) (a b) -> p (r a) b", p=WIN, b=512),
                           zeros[0:WIN, :].unsqueeze(1).broadcast_to([WIN, YROWS // WIN, 512])).then_inc(y_out, 16)

        pool.wait_ge(tail_taken, 1)
        pool.dma_start(o["conf_prompt"][0, 0, :, :], sc_out[0:CK - 1, :]).then_inc(state_out, 16)
        pool.dma_start(o["conf_sample"][0, :, CK - 2, :], sc_out[CK - 1:CK - 1 + NB, :]).then_inc(state_out, 16)
        pool.wait_ge(tail_taken, 2)
        pool.dma_start(o["lru_prompt"][0, 0, :, :], sl_out[0:LK - 1, :]).then_inc(state_out, 16)
        pool.dma_start(o["lru_sample"][0, :, LK - 2, :], sl_out[LK - 1:LK - 1 + NB, :]).then_inc(state_out, 16)
        pool.wait_ge(tail_taken, 3)
        pool.dma_start(o["h_prompt"][0, :, :], sh_out[0:1, :]).then_inc(state_out, 16)
        pool.dma_start(o["h_sample"][0, :, :], sh_out[1:1 + NB, :]).then_inc(state_out, 16)
        pool.memset(tri[:, :], 1.0).then_inc(iotas_ready, 1)
        pool.wait_ge(iotas_ready, 1)
        pool.affine_select(out=tri[:, :], in_=tri[:, :], compare_op=ALU.is_gt, fill=0.0, base=0,
                           pattern=[[1, P]], channel_multiplier=-1).then_inc(iotas_ready, 1)
        pool.iota(i32r[:, :], [[1, E]], base=0, channel_multiplier=0,
                  allow_small_or_imprecise_dtypes=True).then_inc(iotas_ready, 1)
        pool.iota(win64[:, :], [[WIN, 4]], base=WIN, channel_multiplier=0,
                  allow_small_or_imprecise_dtypes=True).then_inc(iotas_ready, 1)
        pool.iota(pidx[:, :], [[0, 1]], base=0, channel_multiplier=1,
                  allow_small_or_imprecise_dtypes=True).then_inc(iotas_ready, 1)
        pool.wait_ge(mixr_ready, TC)
        pool.dma_start(prow[:, 0:2, :], a["p_prompt"][0, 0].rearrange("(c p) d -> p c d", p=P)).then_inc(p_loaded, 16)
        pool.dma_start(prow[0:NB, 2, :], a["p_sample"][0, :, 0, :]).then_inc(p_loaded, 16)
        pool.wait_ge(acc_full, CT_PLE)
        pool.iota(iota[:, :], [[1, XW]], base=0, channel_multiplier=0,
                  allow_small_or_imprecise_dtypes=True).then_inc(iotas_ready, 1)

        def take_slots(start, sems):
            pool.tensor_copy(wslot[:, 0:2, :], onehot[:, 0:2, bass.ds(start, WIN)])
            pool.tensor_copy(wslot[0:NB, 2, :], onehot[0:NB, 2, bass.ds(start, WIN)]).then_inc(sems["slots"], 1)

        pool.wait_ge(onehot_ready, 3)
        take_slots(0, main)
        pool.wait_ge(table_ready, 1)
        pool.dma_start(ov_dram[:, :], otabi[0:MAX_OVER, :]).then_inc(table_out, 16)

        def store(row, buf, first, n, out_sem):
            for half in range(2):
                pool.dma_start(y_dram[bass.ds(row, n), half * D // 2:(half + 1) * D // 2],
                               ysb[half * WIN + first:half * WIN + first + n, buf, :]).then_inc(out_sem, 16)

        def store_results(e, par):
            start = pool.value_load(offs[0:1, bass.ds(e, 1)], min_val=0, max_val=NSLOT)
            pool.wait_ge(main["evac"], 2 * e + 2)
            pool.wait_ge(y_out, 32 * (e + 2))
            tokens = pool.value_load(high[0:1, 0, bass.ds(e, 1)], min_val=0, max_val=NSLOT)
            with pool.If(tokens > LOW):
                stored = pool.value_load(high[0:1, 1, bass.ds(e, 1)], min_val=32, max_val=32 * E)
                store(start + LOW, par, LOW, WIN - LOW, y_high)
                pool.wait_ge(y_high, stored)
            store(start, par, 0, LOW, y_out)

        second = pool.value_load(offs[0:1, 1:2], min_val=0, max_val=NSLOT)
        pool.wait_ge(main["gathered"], 1)
        take_slots(second, main)
        with pool.Fori(0, E - 2, 2) as e2:
            for par in range(2):
                following = pool.value_load(offs[0:1, bass.ds(e2 + par + 2, 1)], min_val=0, max_val=NSLOT)
                pool.wait_ge(main["gathered"], e2 + par + 2)
                take_slots(following, main)
                store_results(e2 + par, par)
        store_results(E - 2, 0)
        store_results(E - 1, 1)
        pool.wait_ge(table_out, 16)
        n_over = pool.value_load(offs[0:1, 40:41], min_val=0, max_val=MAX_OVER)
        pool.wait_ge(y_out, 32 * (E + 2))
        with pool.If(n_over > 0):
            pool.sem_inc(over_free, 1)
            with pool.Fori(0, n_over) as i:
                start = pool.value_load(ov_dram[bass.ds(i, 1), 1:2], min_val=0, max_val=NSLOT)
                take_slots(start, extra)
                pool.wait_ge(extra["evac"], 2 * i + 2)
                store(start + XW, 0, 0, WIN, over_out)
                pool.wait_ge(over_out, 32 * (i + 1))
                pool.sem_inc(over_free, 1)
        for c in (2, 0, 1):
            r = ROWS[c]
            for q, g in ((0, g0), (1, g1)):
                pool.indirect_dma_start(g[0:r, c, :], None, y_dram[:, :],
                                        bass.IndirectOffsetOnAxis(ap=rowix[0:r, q, c:c + 1], axis=0))\
                    .then_inc(rows_back[c], 16)
        pool.wait_ge(state_out, 16 * 8)

    @block.tensor
    def _(pe):
        def turn(out, src, r):
            if r == P:
                return pe.transpose(out, src, ident[:, :])
            return pe.matmul(out, src, ident[:, :], start=True, stop=True)

        def dense(n, chunk0, rhs, kt, wait_k=None):
            if CT_OUT <= n - 3 < CT_PLE:
                pe.wait_ge(hT_ready, n - 3 - CT_OUT + 1)
            elif n >= 3:
                pe.wait_ge(acc_free, freed(n - 3))
            for k in range(kt):
                if kt == KD:
                    ch, kk = chunk0 + k // 4, k % 4
                    w = ring[:, slot(ch), kk * 512 + (n % 4) * P:kk * 512 + (n % 4) * P + P]
                    first, done = n % 4 == 0 and kk == 0, n % 4 == 3 and kk == 3
                else:
                    ch = chunk0 + k
                    w = ring[:, PLE_SLOT + k, (n - CT_PLE) * P:(n - CT_PLE + 1) * P]
                    first, done = False, False
                    if n == CT_PLE and k == 0:
                        pe.wait_ge(ple_loaded, 32)
                if first:
                    pe.wait_ge(slot_loaded[slot(ch)], slot_count(ch))
                if wait_k:
                    wait_k(k)
                mm = pe.matmul(ps[:, n % 3, 0:TOK], w, rhs[:, k, :], start=(k == 0), stop=(k == kt - 1))
                if done and k < kt - 1:
                    mm.then_inc(chunk_used, 1)
            mm.then_inc(acc_full, 1)

        pe.wait_ge(consts_ready, 5)
        pe.wait_ge(rows_loaded, 16 * N_ROWS)
        widths = [P, 120, 104, P, 16]
        c0 = 0
        for b in range(5):
            w = widths[b]
            last = pe.transpose(ps[:, 7, c0:c0 + w], vrow[0:w, b, :], ident[0:w, 0:w])
            c0 += w
        last.then_inc(vec_turned, 1)

        def turn_states(first):
            if first == 0:
                pe.wait_ge(late_rows, 32)
            for j in range(first, first + 4):
                if j >= 4:
                    pe.wait_ge(state_used, j - 3)
                b = 3 + j % 4
                pe.transpose(ps[:, b, 0:120], stage[0:120, 0, j * P:(j + 1) * P], ident[0:120, 0:120])
                pe.transpose(ps[:, b, 120:240], stage[0:120, 1, j * P:(j + 1) * P], ident[0:120, 0:120])\
                    .then_inc(state_turned, 1)

        def turn_lru_states():
            pe.wait_ge(vec_ready, 1)
            for j in range(TC):
                last = pe.transpose(ps[:, 7, j * 24:(j + 1) * 24], lstage[0:24, j * P:(j + 1) * P], ident[0:24, 0:24])
            last.then_inc(state_turned, 1)

        def turn_x(base, src, ready):
            pe.wait_ge(xs_ready, ready)
            for k in range(KD):
                if k >= 4:
                    if base:
                        pe.wait_ge(xT_dve, base + k - 3)
                    elif k % 2 == 0:
                        pe.wait_ge(xT_dve, base + k // 2 - 1)
                    else:
                        pe.wait_ge(xT_act, base + k // 2 - 1)
                for c in range(3):
                    r = ROWS[c]
                    last = pe.transpose(ps[:, 3 + k % 4, c * P:c * P + r], src(c, k), ident[0:r, 0:r])
                last.then_inc(x_turned, 1)

        turn_x(0, lambda c, k: xs[0:ROWS[c], c, k * P:(k + 1) * P], 3)

        def lru_gates(j):
            if j == 0:
                pe.wait_ge(gates_loaded, 32)
            pe.wait_ge(lconv_done, j + 1)
            if j >= 1:
                pe.wait_ge(gates_taken, j)
            pe.matmul(ps[:, 3, 0:TOK], wa[:, j, :], lxc[:, j, :], start=True, stop=True)
            pe.matmul(ps[:, 4, 0:TOK], wx[:, j, :], lxc[:, j, :], start=True, stop=True).then_inc(gates_full, 1)

        def mean():
            pe.wait_ge(conv_done, TC)
            for j in range(TC):
                mm = pe.matmul(ps[:, 6, 0:TOK], ones[:, :], mix[:, j, :], start=(j == 0), stop=(j == TC - 1))
            mm.then_inc(mean_full, 1)

        def var(p):
            pe.wait_ge(sq_ready, 2 * p + 2)
            for j in range(2 * p, 2 * p + 2):
                mm = pe.matmul(ps[:, 7, 0:TOK], ones[:, :], sq[:, j % 2, :], start=(j == 0), stop=(j == TC - 1))
            mm.then_inc(sq_used, 1)

        def wait_xT(k):
            if k % 2 == 0:
                pe.wait_ge(xT_dve, k // 2 + 1)
            else:
                pe.wait_ge(xT_act, k // 2 + 1)

        for n in range(CT_OUT):
            dense(n, 4 * (n // 4), xT, KD, wait_xT if n == 0 else None)
            if n < 2:
                turn_states(4 * n)
            if n == 1:
                turn_lru_states()
            if 20 <= n < 28:
                lru_gates(n - 20)
            if n == 23:
                mean()
            if 26 <= n < 30:
                var(n - 26)

        def split_product(t, n, ks, rest, ready):
            if t < KD and n >= CT_OUT + 3:
                pe.wait_ge(hT_ready, n - 3 - CT_OUT + 1)
            else:
                pe.wait_ge(acc_free, freed(n - 3))
            pe.wait_ge(w_lo_ready, t + 1)
            out = ps[:, n % 3, 0:TOK]
            for i, k in enumerate(ks):
                if t % KD == 0:
                    pe.wait_ge(ready[0], ready[1] + i + 1)
                w_hi, w_lo = ring_r[:, hi_slot(t), k, :], ring_r[:, lo_slot(t), k, :]
                pe.matmul(out, w_hi, x_hi[:, k, :], start=(i == 0), stop=False)
                pe.matmul(out, w_hi, rest[:, k, :], start=False, stop=False)
                mm = pe.matmul(out, w_lo, x_hi[:, k, :], start=False, stop=(i == KD - 1))
            mm.then_inc(acc_full, 1)

        def turn_back(m, base_free):
            pe.wait_ge(hT_ready, m + 1)
            if m >= 2:
                pe.wait_ge(h_added, m - 1)
            for c in range(3):
                r = ROWS[c]
                last = turn(ps[0:r, 3 + m % 2, c * P:(c + 1) * P], hT_tile(m)[:, c * P:c * P + r], r)
            last.then_inc(h_turned, 1)

        def hT_tile(m):
            return hT[:, m % 2, :]

        def turn_tails(which):
            if which:
                pe.wait_ge(tail_taken, which)
            pe.wait_ge(rx_ready, 2 * which + 1)
            for j in range(TC):
                src, r = [(U[:, j, SEQ:UW], CK - 1 + NB), (L[:, j, SEQ:LW], LK - 1 + NB), (htail[:, j, :], 1 + NB)][which]
                last = turn(ps[0:r, 5 + j // 4, (j % 4) * P:(j % 4 + 1) * P], src, r)
            last.then_inc(tail_turned, 1)

        def turn_router(m):
            pe.wait_ge(h_added, m + 1)
            if m:
                pe.wait_ge(rx_ready, m)
            if m in (1, 3, 5):
                pe.wait_ge(tail_taken, m // 2 + 1)
            for c in range(3):
                r = ROWS[c]
                last = pe.transpose(ps[:, 6, c * P:c * P + r], h[0:r, c, m * P:(m + 1) * P], ident[0:r, 0:r])
            last.then_inc(r_turned, 1)

        def logits(m):
            if m == 0:
                pe.wait_ge(router_loaded, 16 * 4)
            pe.wait_ge(rx_ready, m + 1)
            for c in range(3):
                r = ROWS[c]
                mm = pe.matmul(ps[0:r, 7, c * 64:c * 64 + NG + E], rxT[:, m % 3, c * P:c * P + r], wr[:, m, :],
                               start=(m == 0 and c == 0), stop=(m == KD - 1), skip_group_check=True)
            if m == KD - 1:
                mm.then_inc(logits_full, 1)

        for n in range(CT_OUT, CT_PLE):
            m = n - CT_OUT
            split_product(m, n, MIX_ORDER, mix_lo, (mix_lo_ready, 0))
            if m >= 1:
                turn_back(m - 1, 0)
            if m >= 3:
                logits(m - 3)
            if m >= 2:
                turn_router(m - 2)
            if m in (2, 4, 6):
                turn_tails(m // 2 - 1)
            if m in (8, 9):
                k = m - 8
                if k == 0:
                    pe.wait_ge(p_loaded, 32)
                    pe.wait_ge(tail_taken, 3)
                else:
                    pe.wait_ge(pT_ready, 1)
                for c in range(3):
                    r = ROWS[c]
                    last = pe.transpose(ps[:, 5, c * P:c * P + r], prow[0:r, c, k * P:(k + 1) * P], ident[0:r, 0:r])
                last.then_inc(p_turned, 1)
        turn_back(KD - 1, 0)
        logits(KD - 3)
        turn_router(KD - 2)
        logits(KD - 2)
        turn_router(KD - 1)
        logits(KD - 1)
        pe.wait_ge(pT_ready, 2)
        for n in range(CT_PLE, CT_PLE + PLE_FIRST):
            dense(n, 0, pT, CH_PLE)
        pe.wait_ge(assigned, 1)
        pe.wait_ge(iotas_ready, 5)
        for c in range(3):
            r = ROWS[c]
            for cc in range(c + 1):
                rr = ROWS[cc]
                pe.matmul(ps[0:r, 6, c * 64:c * 64 + E], ones[0:rr, 0:r] if cc < c else tri[0:r, 0:r],
                          asg[0:rr, cc, :], start=(cc == 0), stop=(cc == c))
        for c in range(3):
            mm = pe.matmul(ps[:, 6, 192:192 + E], ones[0:ROWS[c], :], asg[0:ROWS[c], c, :],
                           start=(c == 0), stop=(c == 2))
        mm.then_inc(ranks_full, 1)
        for n in range(CT_PLE + PLE_FIRST, CT_PG):
            dense(n, 0, pT, CH_PLE)

        def gather(i, sems):
            pe.wait_ge(sems["slots"], i + 1)
            for b in range(2):
                for c in range(3):
                    r = ROWS[c]
                    for half in range(2):
                        q = 2 * half + b
                        mm = pe.matmul(ps[half * WIN:(half + 1) * WIN, 4 + b, :].rearrange("w (k p) -> w k p", k=4),
                                       wslot[0:r, c, :],
                                       h[0:r, c, :].rearrange("t (p k) -> t k p", k=KD)[:, 4 * q:4 * q + 4, :],
                                       start=(c == 0), stop=(c == 2))
            mm.then_inc(sems["gathered"], 1)

        def turn_rows(i, sems):
            pe.wait_ge(sems["rows"], 2 * i + 2)
            for b in range(2):
                for kk in range(4):
                    last = pe.transpose(ps[:, 6 + b, kk * P:(kk + 1) * P], xrow[:, b, kk * P:(kk + 1) * P], ident[:, :])
            last.then_inc(sems["rows_turned"], 1)

        pe.wait_ge(acc_free, freed(CT_PG - 1))

        def expert(i, sems, weights, loaded, release_chunks, following=False):
            pe.wait_ge(sems["window"], i + 1)
            for j in range(4):
                loaded(2 * j)
                loaded(2 * j + 1)
                for kk in range(4):
                    k = 4 * j + kk
                    for part in range(2):
                        mm = pe.matmul(ps[part * WIN:(part + 1) * WIN, 0, :], xwin[:, k, :],
                                       weights(2 * j + part)[:, kk * F:(kk + 1) * F],
                                       start=(k == 0), stop=(k == KD - 1))
                if j < 3 and release_chunks:
                    mm.then_inc(chunk_used, 1)
            mm.then_inc(sems["products"], 1)
            if following:
                gather(i + 1, sems)
            pe.wait_ge(sems["gated"], i + 1)
            for t in range(4):
                mm = pe.matmul(ps[:, 1, t * WIN:(t + 1) * WIN], sgl[WIN:2 * WIN, t * P:(t + 1) * P],
                               ident[WIN:2 * WIN, WIN:2 * WIN], start=True, stop=True)
            mm.then_inc(sems["turned"], 1)
            pe.wait_ge(sems["hid"], i + 1)
            for t in range(4):
                loaded(8 + t)
                for b in range(2):
                    for half in range(2):
                        q = 2 * half + b
                        mm = pe.matmul(ps[half * WIN:(half + 1) * WIN, 2 + b, :], hid[:, t, :],
                                       weights(8 + t)[:, q * 512:(q + 1) * 512], start=(t == 0), stop=(t == 3))
                if t < 3 and release_chunks:
                    mm.then_inc(chunk_used, 1)
                if t == 1 and following:
                    turn_rows(i + 1, sems)
            mm.then_inc(sems["down"], 1)

        def main_expert(pair, par, following):
            e = pair * 2 + par

            def weights(j):
                return odd_ring[:, j, :] if par == 1 and j < ODD else ring[:, EXP_SLOT[j], :]

            def loaded(j):
                if j >= ODD:
                    pe.wait_ge(slot_loaded[EXP_SLOT[j]], e * 16 + expert_count(j))
                elif par == 0:
                    pe.wait_ge(slot_loaded[EXP_SLOT[j]], pair * 16 + expert_count(j))
                else:
                    pe.wait_ge(odd_loaded[j], pair * 16 + 16)

            expert(e, main, weights, loaded, True, following)

        gather(0, main)
        turn_rows(0, main)
        with pe.Fori(0, E // 2 - 1) as pair:
            for par in range(2):
                main_expert(pair, par, True)
        main_expert(E // 2 - 1, 0, True)
        main_expert(E // 2 - 1, 1, False)
        pe.wait_ge(table_out, 16)
        n_over = pe.value_load(offs[0:1, 40:41], min_val=0, max_val=MAX_OVER)
        with pe.If(n_over > 0):
            with pe.Fori(0, n_over) as i:
                gather(i, extra)
                turn_rows(i, extra)

                def over_wait(j):
                    if j == 0:
                        pe.wait_ge(over_loaded, 16 * CH_EXP * (i + 1))

                expert(i, extra, lambda j: ring[:, j, :], over_wait, False)

        turn_x(8, lambda c, k: xs3[0:ROWS[c], c, k * P:(k + 1) * P], 6)

        def turn_prod(m):
            pe.wait_ge(prod_ready, m + 1)
            if m >= 2:
                pe.wait_ge(h_added, KD + m - 1)
            for c in range(3):
                r = ROWS[c]
                last = turn(ps[0:r, 3 + m % 2, c * P:(c + 1) * P], pleT[:, m, c * P:c * P + r], r)
            last.then_inc(h_turned, 1)

        for m in range(KD):
            split_product(KD + m, CT_PG + m, range(KD), x_lo, (xT_dve, 8))
            if m:
                turn_prod(m - 1)
        turn_prod(KD - 1)

    @block.scalar
    def _(act):
        order = [0]

        def step(ins):
            order[0] += 1
            ins.then_inc(act_order, 1)

        def link(ins):
            step(ins)
            act.wait_ge(act_order, order[0])

        sums = [0]

        def squares(dst, src, out):
            if sums[0]:
                act.wait_ge(ssq_act, sums[0])
            sums[0] += 1
            act.activation(dst, src, ACT.Square, accum_out=out).then_inc(ssq_act, 1)

        act.wait_ge(ssum_set, 1)
        for c in (1, 2):
            r = ROWS[c]
            act.wait_ge(x_loaded[c], 16)
            squares(xdump[0:r, 1, :], h[0:r, c, :], ssum[0:r, c:c + 1])
        def normalise(rows, n):
            act.wait_ge(rstd_ready, n)
            act.wait_ge(ssq_act, sums[0])
            act.activation(rows[:, 1, :], h[:, 1, :], ACT.Copy, scale=rstd[:, 1:2]).then_inc(xs_ready, 1)

        act.wait_ge(ms_ready, 1)
        act.activation(ssum[:, 0:3], ssum[:, 0:3], ACT.Sqrt).then_inc(root_ready, 1)
        normalise(xs, 1)
        act.wait_ge(consts_ready, 5)
        act.wait_ge(vec_ready, 1)
        lam = vT[:, V_LAM:V_LAM + TC]
        link(act.activation(spt[:, 0, :], lam, ACT.Abs))
        link(act.activation(spt[:, 0, :], spt[:, 0, :], ACT.Exp, scale=-1.0))
        step(act.activation(spt[:, 1, :], spt[:, 0, :], ACT.Ln, bias=ones[:, 0:1]))

        def take_xT(base, gain):
            for k in range(1, KD, 2):
                act.wait_ge(x_turned, 2 * base + k + 1)
                act.activation(xT[:, k, :], ps[:, 3 + k % 4, 0:TOK], ACT.Copy, scale=gain(k)).then_inc(xT_act, 1)

        take_xT(0, lambda k: vT[:, V_N1 + k:V_N1 + k + 1])
        act.wait_ge(x_turned, KD)
        act.dma_start(wa[:, :, :], a["lru_wa"][0].rearrange("h i j -> i h j")).then_inc(gates_loaded, 16)
        act.dma_start(wx[:, :, :], a["lru_wx"][0].rearrange("h i j -> i h j")).then_inc(gates_loaded, 16)
        act.dma_start(wr[:, :, 0:NG], a["w_grp"][0].rearrange("(k p) n -> p k n", k=KD)).then_inc(router_loaded, 16)
        act.dma_start(wr[:, :, NG:], a["w_rt"][0].rearrange("(k p) n -> p k n", k=KD)).then_inc(router_loaded, 16)
        act.dma_start(br[:, 0:NG], a["b_grp"][0].partition_broadcast(P)).then_inc(router_loaded, 16)
        act.dma_start(br[:, NG:], a["b_rt"][0].partition_broadcast(P)).then_inc(router_loaded, 16)

        def quarter_squares(q, base, dump):
            act.wait_ge(h_added, base + 4 * q + 4)
            for c in range(3):
                r = ROWS[c]
                squares(dump[0:r, :], h[0:r, c, 512 * q:512 * (q + 1)], sqp[0:r, c, q:q + 1])

        def gates(j):
            act.wait_ge(gates_full, j + 1)
            if j >= 4:
                act.wait_ge(scan_done, 1)
            act.activation(R[:, j % 4, :], ps[:, 3, 0:TOK], ACT.Sigmoid, bias=vT[:, V_BA + j:V_BA + j + 1])
            if j >= 2:
                act.wait_ge(i_used, j - 1)
            act.activation(I[:, j % 2, :], ps[:, 4, 0:TOK], ACT.Sigmoid, bias=vT[:, V_BX + j:V_BX + j + 1])\
                .then_inc(gates_taken, 1)

        def decays(b):
            act.wait_ge(gates_taken, 4 * b + 4)
            act.wait_ge(vec_ready, 2)
            if b:
                act.wait_ge(scan_done, 1)
            else:
                act.wait_ge(y_out, 64)
            for j in range(4):
                act.activation(T[:, j, :], R[:, j, :], ACT.Tanh, scale=negc[:, 4 * b + j:4 * b + j + 1])
            for j in range(4):
                last = act.activation(R[:, j, :], R[:, j, :], ACT.Exp, scale=negc[:, 4 * b + j:4 * b + j + 1])
            last.then_inc(tanh_ready, 1)
            act.wait_ge(z_ready, b + 1)
            act.activation(T[:, :, :], T[:, :, :], ACT.Sqrt, scale=-1.0).then_inc(beta_ready, 1)

        def round_weights(t):
            act.wait_ge(*tile_in(t))
            act.activation(ring_r[:, hi_slot(t), :, :].rearrange("p k c -> p (k c)"), ring[:, lo_slot(t), :],
                           ACT.Copy).then_inc(w_hi_ready, 1)

        for n in range(CT_OUT):
            g, i = n // 4, n % 4
            col = V_BIN + GROUP_COL[g] // P + (i if g >= 4 else i % 2 + i // 2 * TC)
            bias = vT[:, col:col + 1]
            bank = ps[:, n % 3, 0:TOK]
            act.wait_ge(acc_full, n + 1)
            if g < 4 and i < 2:
                act.activation(U[:, 2 * g + i, CK - 1:], bank, ACT.Identity, bias=bias).then_inc(acc_free, 1)
            elif g < 4:
                t = 2 * g + i - 2
                if t >= 2:
                    act.wait_ge(u_ready, t - 1)
                act.activation(gate_buf[t % 2][:, :], bank, ACT.Sigmoid, bias=bias).then_inc(acc_free, 1)
            elif g in (4, 5):
                act.activation(L[:, n - 16, LK - 1:], bank, ACT.Identity, bias=bias).then_inc(acc_free, 1)
            else:
                t = n - 24
                if t >= 2:
                    act.wait_ge(mixr_ready, t - 1)
                act.activation(gate_buf[t % 2][:, :], bank, ACT.Gelu_apprx_tanh, bias=bias).then_inc(acc_free, 1)
            if 20 <= n < 28:
                gates(n - 20)
            if n == 23:
                decays(0)
            if n == 27:
                decays(1)
            if 25 <= n < 29:
                p = n - 25
                for j in range(2 * p, 2 * p + 2):
                    act.wait_ge(centred, j + 1)
                    if p:
                        act.wait_ge(sq_used, p)
                    act.activation(sq[:, j % 2, :], mix[:, j, :], ACT.Square).then_inc(sq_ready, 1)
            if n == 30:
                act.wait_ge(var_ready, 1)
                act.activation(I[:, 1, :], I[:, 0, :], ACT.Sqrt).then_inc(sd_ready, 1)
            if 28 <= n < 31:
                round_weights(n - 28)
        def silu(j):
            act.wait_ge(scaled, j + 1)
            act.activation(mix[:, j, :], mix[:, j, :], ACT.Silu, scale=vT[:, V_LNG + j:V_LNG + j + 1],
                           bias=vT[:, V_LNB + j:V_LNB + j + 1]).then_inc(mixc_ready, 1)

        for j in MIX_ORDER:
            if j < TC:
                if j == 0:
                    silu(0)
                if j + 1 < TC:
                    silu(j + 1)
                act.wait_ge(mixc_ready, j + 1)
            else:
                act.wait_ge(mixr_ready, j - TC + 1)
            act.activation(x_hi[:, j, :], mix[:, j, :], ACT.Copy).then_inc(mix_hi_ready, 1)

        def take_router(m):
            act.wait_ge(r_turned, m + 1)
            act.activation(rxT[:, m % 3, :], ps[:, 6, 0:TOK], ACT.Copy, scale=g2n[:, m:m + 1]).then_inc(rx_ready, 1)

        for m in range(KD):
            n = CT_OUT + m
            act.wait_ge(acc_full, n + 1)
            if m >= 2:
                act.wait_ge(h_turned, m - 1)
            act.activation(hT[:, m % 2, :], ps[:, n % 3, 0:TOK], ACT.Copy).then_inc(hT_ready, 1)
            if m + 3 < KD:
                round_weights(m + 3)
            if m >= 2:
                take_router(m - 2)
            if m % 4 == 1 and m > 4:
                quarter_squares(m // 4 - 1, 0, sdump)
            if m in (9, 10):
                act.wait_ge(p_turned, m - 8)
                act.activation(pT[:, m - 9, :], ps[:, 5, 0:TOK], ACT.Copy).then_inc(pT_ready, 1)
        take_router(KD - 2)
        take_router(KD - 1)
        quarter_squares(3, 0, sdump)
        act.wait_ge(ms_ready, 2)
        act.activation(ssum[:, 0:3], ssum[:, 0:3], ACT.Sqrt).then_inc(root_ready, 1)
        act.wait_ge(state_out, 16 * 8)
        for m in range(KD):
            n = CT_PLE + m
            if m == PLE_FIRST:
                act.wait_ge(softmax_in, 1)
                act.activation(gex[:, :, :], gex[:, :, :], ACT.Exp)
                act.activation(ex[:, :], ex[:, :], ACT.Exp).then_inc(softmax_out, 1)
            act.wait_ge(acc_full, n + 1)
            act.activation(pleT[:, m, :], ps[:, n % 3, 0:TOK], ACT.Copy).then_inc(acc_free, 1)
        for c in range(3):
            r = ROWS[c]
            act.wait_ge(hot_ready, c + 1)
            act.activation(onehot[0:r, c, :], onehot[0:r, c, :], ACT.Copy, scale=rstd[0:r, c:c + 1]).then_inc(onehot_ready, 1)

        def take_rows(i, sems):
            act.wait_ge(sems["gathered"], i + 1)
            act.activation(xrow[:, 0, :], ps[:, 4, :], ACT.Copy).then_inc(sems["rows"], 1)

        def expert(i, par, sems, following=False):
            act.wait_ge(sems["products"], i + 1)
            act.activation(sgl[WIN:2 * WIN, :], ps[0:WIN, 0, :], ACT.Silu).then_inc(sems["silu"], 1)
            if following:
                take_rows(i + 1, sems)
            act.wait_ge(sems["down"], i + 1)
            if sems is main:
                act.wait_ge(y_out, (i + 1) * 32)
            act.activation(ysb[:, par, 0:512], ps[:, 2, :], ACT.Copy).then_inc(sems["evac"], 1)

        act.wait_ge(table_ready, 1)
        take_rows(0, main)
        with act.Fori(0, E - 2, 2) as e2:
            for par in range(2):
                expert(e2 + par, par, main, True)
        expert(E - 2, 0, main, True)
        expert(E - 1, 1, main)
        act.wait_ge(table_out, 16)
        n_over = act.value_load(offs[0:1, 40:41], min_val=0, max_val=MAX_OVER)
        with act.If(n_over > 0):
            with act.Fori(0, n_over) as i:
                act.wait_ge(over_free, i + 1)
                take_rows(i, extra)
                expert(i, 0, extra)
        for n, c in enumerate((2, 0, 1)):
            r = ROWS[c]
            if n == 2:
                round_weights(KD)
            act.wait_ge(h2_ready, n + 1)
            squares(g0[0:r, c, :], h[0:r, c, :], ssum[0:r, c:c + 1])
        act.wait_ge(ms_ready, 3)
        act.activation(ssum[:, 0:3], ssum[:, 0:3], ACT.Sqrt).then_inc(root_ready, 1)
        normalise(xs3, 3)
        act.dma_start(fing[:, :], a["final_g"].partition_broadcast(P)).then_inc(fing_loaded, 16)
        for k in range(KD):
            act.wait_ge(x_turned, KD + k + 1)
            act.activation(x_hi[:, k, :], ps[:, 3 + k % 4, 0:TOK], ACT.Copy, scale=vT[:, V_PN + k:V_PN + k + 1])\
                .then_inc(xT_act, 1)
            if k in (7, 15):
                round_weights(KD + k // 8 + 1)
        for m in range(KD):
            n = CT_PG + m
            act.wait_ge(acc_full, n + 1)
            if m >= 2:
                act.wait_ge(prod_ready, m - 1)
            act.activation(gate_tail(m), ps[:, n % 3, 0:TOK], ACT.Sigmoid,
                           bias=vT[:, V_BPG + m:V_BPG + m + 1]).then_inc(acc_free, 1)
            if m + 3 < KD:
                round_weights(KD + m + 3)
            if m % 4 == 2 and m > 4:
                quarter_squares(m // 4 - 1, KD, sdump2)
        quarter_squares(3, KD, sdump2)
        act.wait_ge(ms_ready, 4)
        act.activation(ssum[:, 0:3], ssum[:, 0:3], ACT.Sqrt).then_inc(root_ready, 1)
        act.wait_ge(rstd_ready, 4)
        act.activation(hg[:, 1, :], hg[:, 1, :], ACT.Copy, scale=rstd[:, 1:2]).then_inc(y_act, 1)
        act.wait_ge(y_act, 1)
        act.dma_start(o["y_prompt"][0, P:2 * P, :], hg[:, 1, :]).then_inc(out_done, 16)

    @block.vector
    def _(dve):
        order = [0]

        def step(ins):
            order[0] += 1
            ins.then_inc(dve_order, 1)
            return order[0]

        def link(ins):
            dve.wait_ge(dve_order, step(ins))

        def stt(out, in0, s, in1, op0, op1):
            return dve.scalar_tensor_tensor(out=out, in0=in0, scalar=s, in1=in1, op0=op0, op1=op1)

        def inverse_rms(n):
            dve.tensor_scalar(ssum[:, 0:3], ssum[:, 0:3], 1.0 / D, EPS, ALU.mult, ALU.add).then_inc(ms_ready, 1)
            dve.wait_ge(root_ready, n)
            dve.reciprocal(rstd[:, 0:3], ssum[:, 0:3]).then_inc(rstd_ready, 1)
            dve.wait_ge(rstd_ready, n)

        def normalise(rows):
            for c in (0, 2):
                r = ROWS[c]
                dve.tensor_scalar(rows[0:r, c, :], h[0:r, c, :], rstd[0:r, c:c + 1], None, ALU.mult).then_inc(xs_ready, 1)

        dve.memset(ssum[:, :], 1.0).then_inc(ssum_set, 1)
        dve.wait_ge(ssum_set, 1)
        dve.wait_ge(x_loaded[0], 16)
        link(dve.tensor_tensor_reduce(xdump[:, 0, :], h[:, 0, :], h[:, 0, :], 1.0, 0.0, ALU.mult, ALU.add, ssum[:, 0:1]))
        dve.wait_ge(ssq_act, 2)
        inverse_rms(1)
        normalise(xs)
        dve.wait_ge(vec_turned, 1)
        dve.tensor_copy(g2n[:, :], ps[:, 7, NV:NV + KD])
        dve.tensor_copy(vT[:, :], ps[:, 7, 0:NV]).then_inc(vec_ready, 1)
        dve.wait_ge(vec_ready, 1)

        def take_xT(base, gain):
            for k in range(0, KD, 2):
                dve.wait_ge(x_turned, 2 * base + k + 1)
                dve.tensor_scalar(xT[:, k, :], ps[:, 3 + k % 4, 0:TOK], gain(k), None, ALU.mult).then_inc(xT_dve, 1)

        take_xT(0, lambda k: vT[:, V_N1 + k:V_N1 + k + 1])

        dve.wait_ge(act_order, 3)
        z, ln1, t = spt[:, 0, :], spt[:, 1, :], spt[:, 2, :]
        link(dve.tensor_scalar(t, z, 1.0, -1.0, ALU.add, ALU.add))
        link(dve.tensor_scalar(negc[:, :], t, 0.0, None, ALU.is_equal))
        link(dve.tensor_tensor(t, t, negc[:, :], ALU.add))
        link(dve.tensor_tensor(ln1, ln1, negc[:, :], ALU.add))
        link(dve.reciprocal(t, t))
        link(dve.tensor_tensor(ln1, ln1, t, ALU.mult))
        link(dve.tensor_tensor(ln1, ln1, z, ALU.mult))
        link(dve.tensor_scalar(t, vT[:, V_LAM:V_LAM + TC], -1.0, 0.0, ALU.mult, ALU.max))
        link(dve.tensor_tensor(t, t, ln1, ALU.add))
        dve.tensor_scalar(negc[:, :], t, -8.0, None, ALU.mult).then_inc(vec_ready, 1)
        link(dve.memset(sqp[:, :, :], 0.0))

        cw = vT[:, 0:TC * (CK - 1)].rearrange("p (t c) -> p c t", c=TC)
        for j in range(TC):
            dve.wait_ge(state_turned, j + 1)
            link(dve.tensor_tensor(ptmp[:, :].rearrange("p (b t) -> p b t", b=NB),
                                   ps[:, 3 + j % 4, 0:240].rearrange("p (b t) -> p b t", b=NB),
                                   cw[:, j:j + 1, :].broadcast_to([P, NB, CK - 1]), ALU.mult))
            dve.tensor_reduce(pconv[:, j, :], ptmp[:, :].rearrange("p (b t) -> p b t", b=NB), AX, ALU.add)\
                .then_inc(state_used, 1)
            dve.wait_ge(state_used, j + 1)
        link(dve.tensor_tensor(pconv[:, :, :], pconv[:, :, :],
                               vT[:, V_DWB:V_DWB + TC].unsqueeze(2).broadcast_to([P, TC, NB]), ALU.add))
        dve.wait_ge(state_turned, TC + 1)
        lw = vT[:, V_LW:V_LW + TC * (LK - 1)].rearrange("p (t c) -> p c t", c=TC)
        for j in range(TC):
            link(dve.tensor_tensor(ptmp[:, 0:24].rearrange("p (b t) -> p b t", b=NB),
                                   ps[:, 7, j * 24:(j + 1) * 24].rearrange("p (b t) -> p b t", b=NB),
                                   lw[:, j:j + 1, :].broadcast_to([P, NB, LK - 1]), ALU.mult))
            link(dve.tensor_reduce(plru[:, j, :], ptmp[:, 0:24].rearrange("p (b t) -> p b t", b=NB), AX, ALU.add))
        link(dve.tensor_tensor(plru[:, :, :], plru[:, :, :],
                               vT[:, V_LB:V_LB + TC].unsqueeze(2).broadcast_to([P, TC, NB]), ALU.add))

        dve.wait_ge(consts_ready, 5)
        for p in range(0, TC, 2):
            for j in (p, p + 1):
                n = 4 * (j // 2) + 2 + j % 2
                dve.wait_ge(acc_free, n + 1)
                dve.tensor_tensor(U[:, j, CK - 1:], U[:, j, CK - 1:], gate_buf[j % 2][:, :], ALU.mult)\
                    .then_inc(u_ready, 1)
            dve.wait_ge(u_ready, p + 2)
            last = {}
            for t in range(CK):
                for j in (p, p + 1):
                    w = vT[:, t * TC + j:t * TC + j + 1]
                    if t == 0:
                        last[j] = step(dve.tensor_scalar(mix[:, j, 0:SEQ], U[:, j, 0:SEQ], w,
                                                         vT[:, V_DWB + j:V_DWB + j + 1], ALU.mult, ALU.add))
                    else:
                        dve.wait_ge(dve_order, last[j])
                        last[j] = step(stt(mix[:, j, 0:SEQ], U[:, j, t:t + SEQ], w, mix[:, j, 0:SEQ],
                                           ALU.mult, ALU.add))
            for j in (p, p + 1):
                w = vT[:, (CK - 1) * TC + j:(CK - 1) * TC + j + 1]
                stt(mix[:, j, SEQ:TOK], U[:, j, UW - NB:UW], w, pconv[:, j, :], ALU.mult, ALU.add)\
                    .then_inc(conv_done, 1)

        def lconv(j):
            dve.wait_ge(acc_free, 16 + j + 1)
            for t in range(LK):
                w = vT[:, V_LW + t * TC + j:V_LW + t * TC + j + 1]
                if t == 0:
                    link(dve.tensor_scalar(lxc[:, j, 0:SEQ], L[:, j, 0:SEQ], w, vT[:, V_LB + j:V_LB + j + 1],
                                           ALU.mult, ALU.add))
                else:
                    link(stt(lxc[:, j, 0:SEQ], L[:, j, t:t + SEQ], w, lxc[:, j, 0:SEQ], ALU.mult, ALU.add))
            stt(lxc[:, j, SEQ:TOK], L[:, j, LW - NB:LW], w, plru[:, j, :], ALU.mult, ALU.add).then_inc(lconv_done, 1)

        def gated(j):
            dve.wait_ge(gates_taken, j + 1)
            dve.tensor_tensor(lxc[:, j, :], lxc[:, j, :], I[:, j % 2, :], ALU.mult).then_inc(i_used, 1)

        def recur(b):
            dve.wait_ge(tanh_ready, b + 1)
            dve.wait_ge(i_used, 4 * b + 4)
            link(dve.tensor_scalar(T[:, :, :], T[:, :, :], -1e-30, None, ALU.min))
            for x in (0, 2):
                link(dve.tensor_tensor(I[:, :, :], R[:, x:x + 2, :], R[:, x:x + 2, :], ALU.mult))
                last = stt(T[:, x:x + 2, :], I[:, :, :], 1.0, T[:, x:x + 2, :], ALU.add, ALU.mult)
                if x == 0:
                    link(last)
            last.then_inc(z_ready, 1)
            dve.wait_ge(beta_ready, b + 1)
            link(dve.tensor_tensor(T[:, :, :], T[:, :, :], lxc[:, 4 * b:4 * b + 4, :], ALU.mult))
            for j in range(4):
                dve.tensor_tensor_scan(mix[:, TC + 4 * b + j, 0:SEQ], R[:, j, 0:SEQ], T[:, j, 0:SEQ], 0.0,
                                       ALU.mult, ALU.add)
            h0 = vT[:, V_H0:V_H0 + 64].rearrange("p (b c) -> p c b", c=TC)[:, 4 * b:4 * b + 4, :]
            link(dve.tensor_tensor(R[:, :, SEQ:TOK], R[:, :, SEQ:TOK], h0, ALU.mult))
            link(dve.tensor_tensor(mix[:, TC + 4 * b:TC + 4 * b + 4, SEQ:TOK], R[:, :, SEQ:TOK], T[:, :, SEQ:TOK],
                                   ALU.add))
            dve.tensor_copy(htail[:, 4 * b:4 * b + 4, :], mix[:, TC + 4 * b:TC + 4 * b + 4, SEQ - 1:TOK])\
                .then_inc(scan_done, 1)
            dve.wait_ge(scan_done, b + 1)

        def rest_weights(t):
            dve.wait_ge(w_hi_ready, t + 1)
            lo = ring_r[:, lo_slot(t), :, :].rearrange("p k c -> p (k c)")
            hi = ring_r[:, hi_slot(t), :, :].rearrange("p k c -> p (k c)")
            dve.tensor_tensor(lo, ring[:, lo_slot(t), :], hi.bitcast(F32), ALU.subtract).then_inc(w_lo_ready, 1)

        def gelu_mul(j):
            dve.wait_ge(acc_free, 24 + j + 1)
            dve.tensor_tensor(mix[:, TC + j, :], mix[:, TC + j, :], gate_buf[j % 2][:, :], ALU.mult)\
                .then_inc(mixr_ready, 1)

        for j in range(4):
            lconv(j)
        for j in range(4):
            lconv(4 + j)
            gated(j)
        recur(0)
        gelu_mul(0)
        gated(4)
        dve.wait_ge(mean_full, 1)
        for j in range(TC):
            stt(mix[:, j, :], ps[:, 6, 0:TOK], -1.0 / DC, mix[:, j, :], ALU.mult, ALU.add).then_inc(centred, 1)
        for j in range(1, 4):
            gelu_mul(j)
            gated(4 + j)
        recur(1)
        for j in range(4, 6):
            gelu_mul(j)
        dve.wait_ge(sq_used, 4)
        dve.wait_ge(i_used, TC)
        dve.tensor_scalar(I[:, 0, :], ps[:, 7, 0:TOK], 1.0 / DC, EPS, ALU.mult, ALU.add).then_inc(var_ready, 1)
        for t in range(2):
            rest_weights(t)
        gelu_mul(6)
        dve.wait_ge(sd_ready, 1)
        link(dve.reciprocal(I[:, 0, :], I[:, 1, :]))
        for j in range(TC):
            dve.tensor_tensor(mix[:, j, :], mix[:, j, :], I[:, 0, :], ALU.mult).then_inc(scaled, 1)
        gelu_mul(7)
        for i, k in enumerate(MIX_ORDER):
            dve.wait_ge(mix_hi_ready, i + 1)
            dve.tensor_tensor(mix_lo[:, k, :], mix[:, k, :], x_hi[:, k, :].bitcast(F32), ALU.subtract)\
                .then_inc(mix_lo_ready, 1)
        rest_weights(2)

        def add_back(m, base):
            dve.wait_ge(h_turned, base + m + 1)
            b = ps[:, 3 + m % 2, :]
            cols = slice(m * P, (m + 1) * P)
            dve.tensor_tensor(h[:, 0:2, cols], h[:, 0:2, cols], b[:, 0:2 * P].rearrange("p (c d) -> p c d", c=2), ALU.add)
            dve.tensor_tensor(h[0:NB, 2, cols], h[0:NB, 2, cols], b[0:NB, 2 * P:3 * P], ALU.add).then_inc(h_added, 1)

        for m in range(KD):
            if m + 3 < KD:
                rest_weights(m + 3)
            add_back(m, 0)
            if m in (2, 4, 6):
                w = m // 2 - 1
                dst, r = [(sc_out, CK - 1 + NB), (sl_out, LK - 1 + NB), (sh_out, 1 + NB)][w]
                dve.wait_ge(tail_turned, w + 1)
                dve.tensor_copy(dst[0:r, :].rearrange("p (a b) -> p a b", a=2), ps[0:r, 5:7, :]).then_inc(tail_taken, 1)

        dve.wait_ge(h_added, KD)
        dve.memset(logit[:, :, :], 0.0)
        dve.memset(gl[:, :, :], -3.0e38)
        link(dve.memset(rank[:, :, :], 0.0))
        dve.wait_ge(ssq_act, 2 + 12)
        link(dve.tensor_reduce(ssum[:, 0:3], sqp[:, :, :], AX, ALU.add))
        inverse_rms(2)
        dve.wait_ge(logits_full, 1)
        for c in range(3):
            r = ROWS[c]
            last = stt(logit[0:r, c, :], ps[0:r, 7, c * 64:c * 64 + NG + E], rstd[0:r, c:c + 1], br[0:r, :],
                       ALU.mult, ALU.add)
        link(last)
        link(dve.tensor_copy(gl[:, :, 0:NG], logit[:, :, 0:NG]))
        for c in range(3):
            last = dve.max(gmx[:, c, :], gl[:, c, :])
        link(last)
        for c in range(3):
            last = dve.max_index(gix[:, c, :], gmx[:, c, :], gl[:, c, :])
        link(last)
        link(dve.tensor_copy(gf[:, :], gix[:, :, 0]))
        link(dve.tensor_tensor(gex[:, :, :], logit[:, :, 0:NG], gmx[:, :, 0:1].broadcast_to([P, 3, NG]), ALU.subtract))
        dve.wait_ge(iotas_ready, 5)
        link(dve.tensor_tensor(oh4[:, :, :], i32r[:, 0:NG].unsqueeze(1).broadcast_to([P, 3, NG]),
                               gf[:, :].unsqueeze(2).broadcast_to([P, 3, NG]), ALU.is_equal))
        for c in range(3):
            last = dve.tensor_tensor(el[:, c, :, :], logit[:, c, NG:].rearrange("p (g j) -> p g j", g=NG),
                                     oh4[:, c, :].unsqueeze(2).broadcast_to([P, NG, EG]), ALU.mult)
        link(last)
        link(dve.tensor_reduce(ein[:, :, :], el[:, :, :, :].rearrange("p c g j -> p c j g"), AX, ALU.add))
        for c in range(3):
            last = dve.max(emx[:, c, :], ein[:, c, :])
        link(last)
        link(dve.tensor_tensor(ex[:, :], emx[:, :, 1], emx[:, :, 0], ALU.subtract))
        for c in range(3):
            last = dve.max_index(eix[:, c, :], emx[:, c, :], ein[:, c, :])
        last.then_inc(softmax_in, 1)
        dve.wait_ge(softmax_in, 1)
        link(dve.tensor_copy(ef[:, :, :], eix[:, :, 0:2]))
        for q in range(2):
            last = stt(ef[:, :, q], gf[:, :], float(EG), ef[:, :, q], ALU.mult, ALU.add)
        link(last)
        for q in range(2):
            last = dve.tensor_tensor(oh[:, q, :, :], i32r[:, :].unsqueeze(1).broadcast_to([P, 3, E]),
                                     ef[:, :, q].unsqueeze(2).broadcast_to([P, 3, E]), ALU.is_equal)
        link(last)
        dve.tensor_tensor(asg[:, :, :], oh[:, 0, :, :], oh[:, 1, :, :], ALU.add).then_inc(assigned, 1)
        dve.wait_ge(ranks_full, 1)
        rk = ps[:, 6, 0:192].rearrange("p (c n) -> p c n", c=3)
        dve.tensor_copy(rank[:, 0:2, :], rk[:, 0:2, 0:E])
        dve.tensor_copy(rank[0:NB, 2, :], rk[0:NB, 2, 0:E])
        link(dve.tensor_copy(cnt[:, :], ps[:, 6, 192:192 + E]))
        link(dve.tensor_tensor_scan(off[:, :], ones[:, 0:E], cnt[:, :], 0.0, ALU.mult, ALU.add))
        link(dve.tensor_tensor(off[:, :], off[:, :], cnt[:, :], ALU.subtract))
        for q in range(2):
            link(dve.tensor_tensor(prod[:, :, :], oh[:, q, :, :], rank[:, :, :], ALU.mult))
            link(dve.tensor_reduce(rnk[:, q, :], prod[:, :, :], AX, ALU.add))
            link(dve.tensor_tensor(prod[:, :, :], oh[:, q, :, :], off[:, :].unsqueeze(1).broadcast_to([P, 3, E]), ALU.mult))
            link(dve.tensor_reduce(pos[:, q, :], prod[:, :, :], AX, ALU.add))
        link(dve.tensor_tensor(pos[:, :, :], pos[:, :, :], rnk[:, :, :], ALU.add))
        dve.wait_ge(iotas_ready, 6)
        for c in range(3):
            r = ROWS[c]
            link(dve.tensor_scalar(onehot[0:r, c, :], iota[0:r, :], pos[0:r, 0, c:c + 1], None, ALU.is_equal))
            stt(onehot[0:r, c, :], iota[0:r, :], pos[0:r, 1, c:c + 1], onehot[0:r, c, :], ALU.is_equal, ALU.add)\
                .then_inc(hot_ready, 1)
        dve.wait_ge(softmax_out, 1)
        link(dve.tensor_reduce(gw[:, :], gex[:, :, :], AX, ALU.add))
        link(dve.tensor_scalar(wts[:, 1, :], ex[:, :], 1.0, None, ALU.add))
        link(dve.tensor_tensor(gw[:, :], gw[:, :], wts[:, 1, :], ALU.mult))
        link(dve.reciprocal(wts[:, 0, :], gw[:, :]))
        link(dve.tensor_tensor(wts[:, 1, :], wts[:, 0, :], ex[:, :], ALU.mult))
        link(dve.tensor_scalar(rnk[:, :, :], rnk[:, :, :], float(WIN), float(XW), ALU.is_ge, ALU.mult))
        link(dve.tensor_tensor(rowix[:, :, :], pos[:, :, :], rnk[:, :, :], ALU.add))
        link(dve.tensor_copy(offs[0:1, 0:E], off[0:1, :]))
        link(dve.memset(offs[0:1, E:E + 1], NSLOT))
        link(dve.tensor_scalar(highf[:, 0, :], cnt[0:1, :], float(LOW), None, ALU.is_gt))
        link(dve.tensor_tensor_scan(highf[:, 1, :], ones[0:1, 0:E], highf[:, 0, :], 0.0, ALU.mult, ALU.add))
        link(dve.tensor_scalar(highf[:, 1, :], highf[:, 1, :], 32.0, None, ALU.mult))
        dve.tensor_copy(high[:, 1, 0:E], highf[:, 1, :])
        link(dve.tensor_copy(high[:, 0, 0:E], cnt[0:1, :]))
        cb = cnt[:, :].unsqueeze(2).broadcast_to([P, E, 4])
        wb = win64[:, :].unsqueeze(1).broadcast_to([P, E, 4])
        link(dve.tensor_tensor(over[:, :, :], cb, wb, ALU.is_gt))
        ov = over[:, :, :].rearrange("p e c -> p (e c)")
        oi = oidx[:, :, :].rearrange("p e c -> p (e c)")
        link(dve.tensor_tensor_scan(oi, ones[:, :], ov, 0.0, ALU.mult, ALU.add))
        link(dve.tensor_copy(offs[0:1, 40:41], oi[0:1, E * 4 - 1:E * 4]))
        link(dve.tensor_tensor(oi, oi, ov, ALU.subtract))
        link(dve.tensor_scalar(osel[:, :, :], oidx[:, :, :], pidx[:, 0:1], None, ALU.is_equal))
        link(dve.tensor_tensor(osel[:, :, :], osel[:, :, :], over[:, :, :], ALU.mult))
        link(dve.tensor_tensor(opr[:, :, :], osel[:, :, :], i32r[:, :].unsqueeze(2).broadcast_to([P, E, 4]), ALU.mult))
        link(dve.tensor_reduce(otab[:, 0:1], opr[:, :, :].rearrange("p e c -> p (e c)"), AX, ALU.add))
        link(dve.tensor_tensor(opr[:, :, :], off[:, :].unsqueeze(2).broadcast_to([P, E, 4]), wb, ALU.add))
        link(dve.tensor_tensor(opr[:, :, :], opr[:, :, :], osel[:, :, :], ALU.mult))
        link(dve.tensor_reduce(otab[:, 1:2], opr[:, :, :].rearrange("p e c -> p (e c)"), AX, ALU.add))
        dve.tensor_copy(otabi[:, :], otab[:, :]).then_inc(table_ready, 1)
        dve.wait_ge(acc_full, CT_PG)

        def take_rows(i, sems):
            dve.wait_ge(sems["gathered"], i + 1)
            dve.tensor_copy(xrow[:, 1, :], ps[:, 5, :]).then_inc(sems["rows"], 1)

        def take_window(i, sems):
            dve.wait_ge(sems["rows_turned"], i + 1)
            dve.tensor_tensor(xwin[:, :, :].rearrange("p (h x) w -> p x h w", h=2),
                              ps[:, 6:8, :].rearrange("p b (k h w) -> p (b k) h w", h=2, w=WIN),
                              g2[:, :].rearrange("p (h x) -> p x h", h=2).unsqueeze(3).broadcast_to([P, 8, 2, WIN]),
                              ALU.mult).then_inc(sems["window"], 1)

        def expert(i, sems):
            dve.wait_ge(sems["silu"], i + 1)
            dve.tensor_tensor(sgl[WIN:2 * WIN, :], sgl[WIN:2 * WIN, :], ps[WIN:2 * WIN, 0, :], ALU.mult)\
                .then_inc(sems["gated"], 1)
            dve.wait_ge(sems["turned"], i + 1)
            dve.tensor_copy(hid[:, :, :].rearrange("p t w -> p (t w)"), ps[:, 1, 0:4 * WIN]).then_inc(sems["hid"], 1)

        def take_results(i, par, sems):
            dve.wait_ge(sems["down"], i + 1)
            if sems is main:
                dve.wait_ge(y_out, (i + 1) * 32)
            dve.tensor_copy(ysb[:, par, 512:1024], ps[:, 3, :]).then_inc(sems["evac"], 1)

        take_rows(0, main)
        take_window(0, main)
        with dve.Fori(0, E - 2, 2) as e2:
            for par in range(2):
                expert(e2 + par, main)
                take_rows(e2 + par + 1, main)
                take_window(e2 + par + 1, main)
                take_results(e2 + par, par, main)
        expert(E - 2, main)
        take_rows(E - 1, main)
        take_window(E - 1, main)
        take_results(E - 2, 0, main)
        expert(E - 1, main)
        take_results(E - 1, 1, main)
        dve.wait_ge(table_out, 16)
        n_over = dve.value_load(offs[0:1, 40:41], min_val=0, max_val=MAX_OVER)
        with dve.If(n_over > 0):
            with dve.Fori(0, n_over) as i:
                take_rows(i, extra)
                take_window(i, extra)
                expert(i, extra)
                take_results(i, 0, extra)

        for c in (2, 0, 1):
            r = ROWS[c]
            dve.wait_ge(rows_back[c], 32)
            link(stt(h[0:r, c, :], g0[0:r, c, :], wts[0:r, 0, c:c + 1], h[0:r, c, :], ALU.mult, ALU.add))
            stt(h[0:r, c, :], g1[0:r, c, :], wts[0:r, 1, c:c + 1], h[0:r, c, :], ALU.mult, ALU.add).then_inc(h2_ready, 1)

        rest_weights(KD)
        dve.wait_ge(ssq_act, 2 + 12 + 3)
        inverse_rms(3)
        normalise(xs3)
        for k in range(KD):
            dve.wait_ge(xT_act, 8 + k + 1)
            stt(x_lo[:, k, :], ps[:, 3 + k % 4, 0:TOK], vT[:, V_PN + k:V_PN + k + 1], x_hi[:, k, :].bitcast(F32),
                ALU.mult, ALU.subtract).then_inc(xT_dve, 1)
            if k in (7, 15):
                rest_weights(KD + k // 8 + 1)
        dve.wait_ge(fing_loaded, 16)

        def final_gain(q):
            cols = slice(512 * q, 512 * (q + 1))
            dve.wait_ge(h_added, KD + 4 * q + 4)
            dve.tensor_tensor(hg[:, 0:2, cols], h[:, 0:2, cols], fing[:, cols].unsqueeze(1).broadcast_to([P, 2, 512]),
                              ALU.mult)
            link(dve.tensor_tensor(hg[0:NB, 2, cols], h[0:NB, 2, cols], fing[0:NB, cols], ALU.mult))

        for m in range(KD):
            dve.wait_ge(acc_free, freed(CT_PG + m))
            dve.tensor_tensor(pleT[:, m, :], pleT[:, m, :], gate_tail(m), ALU.mult).then_inc(prod_ready, 1)
            if m:
                add_back(m - 1, KD)
            if m and m % 4 == 0:
                final_gain(m // 4 - 1)
            if m + 3 < KD:
                rest_weights(KD + m + 3)
        add_back(KD - 1, KD)
        final_gain(3)
        dve.wait_ge(ssq_act, 2 + 12 + 3 + 12)
        link(dve.tensor_reduce(ssum[:, 0:3], sqp[:, :, :], AX, ALU.add))
        inverse_rms(4)
        for c in (2, 0):
            r = ROWS[c]
            dve.tensor_scalar(hg[0:r, c, :], hg[0:r, c, :], rstd[0:r, c:c + 1], None, ALU.mult).then_inc(y_ready, 1)

    block.__exit__(None, None, None)


N_ROWS = 17


def row_loads(a, vrow, stage, lstage, g2):
    def rows(x):
        return x.rearrange("l (r p) -> (l r) p", p=P)

    cw = a["conf_dw_w"].rearrange("l t (c p) -> (l t c) p", p=P)
    yield vrow[:, 0, :], cw[0:P, :]
    yield vrow[0:120, 1, :], cw[P:248, :]
    at = 0
    for name, n in (("norm1_g", 16), ("ple_norm_g", 16), ("b_in", 32), ("b_pg", 16), ("conf_dw_b", 8),
                    ("conf_ln_g", 8), ("conf_ln_b", 8)):
        yield vrow[at:at + n, 2, :], rows(a[name])
        at += n
    yield vrow[0:32, 3, :], a["lru_conv_w"].rearrange("l t (c p) -> (l t c) p", p=P)
    yield vrow[32:40, 3, :], rows(a["lru_conv_b"])
    yield vrow[40:48, 3, :], a["lru_ba"].rearrange("l h j -> (l h) j")
    yield vrow[48:56, 3, :], a["lru_bx"].rearrange("l h j -> (l h) j")
    yield vrow[56:64, 3, :], rows(a["lru_lambda"])
    yield vrow[64:128, 3, :], a["state_lru_h"].rearrange("l b (c p) -> (l b c) p", p=P)
    yield vrow[0:16, 4, :], rows(a["norm2_g"])
    yield g2[:, :], a["norm2_g"].rearrange("l (p k) -> p (l k)", k=KD)
    yield stage[0:120, :, :], a["state_conf_conv"].rearrange("l (q b) t c -> (b t) (l q) c", q=2)
    yield lstage[0:24, :], a["state_lru_conv"].rearrange("l b t c -> (l b t) c")


INPUTS = ["x_prompt", "x_sample", "state_conf_conv", "state_lru_conv", "state_lru_h", "p_prompt", "p_sample",
          "norm1_g", "w_in", "b_in", "conf_dw_w", "conf_dw_b", "conf_ln_g", "conf_ln_b", "lru_conv_w", "lru_conv_b",
          "lru_wa", "lru_ba", "lru_wx", "lru_bx", "lru_lambda", "w_out", "norm2_g", "w_grp", "b_grp", "w_rt", "b_rt",
          "w_gate", "w_up", "w_down", "ple_norm_g", "w_ple", "w_pg", "b_pg", "final_g"]
OUTPUTS = [("y_prompt", (1, SEQ, D)), ("y_sample", (NB, 1, D)), ("conf_prompt", (1, 1, CK - 1, DC)),
           ("conf_sample", (1, NB, CK - 1, DC)), ("lru_prompt", (1, 1, LK - 1, DC)),
           ("lru_sample", (1, NB, LK - 1, DC)), ("h_prompt", (1, 1, DC)), ("h_sample", (1, NB, DC))]


def kernel(**inputs):
    import numpy as _np
    import concourse.bacc as _bacc
    from concourse import mybir as _mybir
    from concourse.bass_utils import run_bass_kernel_spmd as _run

    nc = _bacc.Bacc("TRN2", target_bir_lowering=False, num_devices=1)
    arrays, a, o = {}, {}, {}
    for name in INPUTS:
        x = _np.ascontiguousarray(inputs[name])
        arrays[f"in_{name}_dram"] = x
        a[name] = nc.dram_tensor(f"in_{name}_dram", x.shape, _mybir.dt.from_np(x.dtype), kind="ExternalInput").ap()
    for name, shape in OUTPUTS:
        o[name] = nc.dram_tensor(f"out_{name}_dram", shape, _mybir.dt.float32, kind="ExternalOutput").ap()
    build(nc, a, o)
    r = _run(nc, [arrays], core_ids=[0])
    return tuple(r.results[0][f"out_{name}_dram"] for name, _ in OUTPUTS)
```
